# Optimizing a Trainium2 kernel written in Bass

```python
import math
import jax, jax.numpy as jnp
from jax import lax
import numpy as np

D_MODEL = 1024
BATCH = 1
SEQ = 1024
DEPTH = 1

CHUNK = 64
S5_WIDTH = 512
S5_GROUP = 16
S5_GROUPS = S5_WIDTH // S5_GROUP
S5_STATE = 64
CONV_WIDTH = 512
CONV_K = 3
ATTN_HEADS = 8
HEAD_DIM = 64
ATTN_WIDTH = ATTN_HEADS * HEAD_DIM
Q_BLOCK = 128
N_BRANCH = 3
MIX_WIDTH = S5_WIDTH + CONV_WIDTH + ATTN_WIDTH
D_FF = 4 * D_MODEL
IN_WIDTH = S5_WIDTH + 3 * CONV_WIDTH + 3 * ATTN_WIDTH + ATTN_HEADS + N_BRANCH * D_MODEL
EPS = 1e-6
NEG_INF = -1e30


def rmsnorm(x, g):
    xf = x.astype(jnp.float32)
    y = xf * lax.rsqrt(jnp.mean(xf * xf, axis=-1, keepdims=True) + EPS)
    return (y * g.astype(jnp.float32)).astype(x.dtype)

def s5_mixer(u, a_re, a_im, log_dt, b_re, b_im, c_re, c_im, d_skip, w_glu):
    bsz, L, _ = u.shape
    f32 = jnp.float32
    uf = u.astype(f32).reshape(bsz, L, S5_GROUPS, S5_GROUP)
    lam = lax.complex(jnp.minimum(a_re.astype(f32), -1e-4), a_im.astype(f32))
    dt = jnp.exp(log_dt.astype(f32))[:, None]
    a_bar = jnp.exp(lam * dt)
    b = lax.complex(b_re.astype(f32), b_im.astype(f32))
    b_bar = ((a_bar - 1.0) / lam)[..., None] * b
    bu = lax.complex(jnp.einsum('gph,blgh->blgp', jnp.real(b_bar), uf),
                     jnp.einsum('gph,blgh->blgp', jnp.imag(b_bar), uf))
    a_seq = jnp.broadcast_to(a_bar, bu.shape)

    def combine(left, right):
        a_l, s_l = left
        a_r, s_r = right
        return a_r * a_l, a_r * s_l + s_r

    _, states = lax.associative_scan(combine, (a_seq, bu), axis=1)
    y = (jnp.einsum('ghp,blgp->blgh', c_re.astype(f32), jnp.real(states))
         - jnp.einsum('ghp,blgp->blgh', c_im.astype(f32), jnp.imag(states))
         + d_skip.astype(f32) * uf)
    y = jax.nn.gelu(y)
    y = y * jax.nn.sigmoid(jnp.einsum('blgh,ghk->blgk', y, w_glu.astype(f32)))
    return y.reshape(bsz, L, S5_WIDTH).astype(u.dtype)

def short_conv_mixer(x_in, gate_b, gate_c, conv_w):
    L = x_in.shape[1]
    v = gate_c * x_in
    vp = jnp.pad(v, ((0, 0), (CONV_K - 1, 0), (0, 0)))
    conv = vp[:, 0:L] * conv_w[0]
    for tap in range(1, CONV_K):
        conv = conv + vp[:, tap:tap + L] * conv_w[tap]
    return gate_b * conv

def forgetting_attention(q, k, v, f_logit, b_f):
    bsz, L, _ = q.shape
    q = q.reshape(bsz, L, ATTN_HEADS, HEAD_DIM)
    k = k.reshape(bsz, L, ATTN_HEADS, HEAD_DIM)
    v = v.reshape(bsz, L, ATTN_HEADS, HEAD_DIM)
    log_f = jax.nn.log_sigmoid((f_logit + b_f).astype(jnp.float32))
    cum = jnp.cumsum(log_f, axis=1).transpose(0, 2, 1)
    scale = HEAD_DIM ** -0.5
    outs = []
    for blk in range(L // Q_BLOCK):
        q0 = blk * Q_BLOCK
        kend = q0 + Q_BLOCK
        s = jnp.einsum('bqhd,bkhd->bhqk', q[:, q0:kend], k[:, :kend]).astype(jnp.float32) * scale
        s = s + cum[:, :, q0:kend, None] - cum[:, :, None, :kend]
        q_pos = q0 + jnp.arange(Q_BLOCK)
        k_pos = jnp.arange(kend)
        s = jnp.where(k_pos[None, :] <= q_pos[:, None], s, NEG_INF)
        p = jax.nn.softmax(s, axis=-1)
        outs.append(jnp.einsum('bhqk,bkhd->bqhd', p.astype(v.dtype), v[:, :kend]))
    return jnp.concatenate(outs, axis=1).reshape(bsz, L, ATTN_WIDTH)

def hybrid_layer(x, g_pre_mix, w_in, b_gate, a_re, a_im, log_dt, b_re, b_im, c_re, c_im,
                 d_skip, w_glu, conv_w, b_f, w_branch, w_out, g_post_mix, g_pre_mlp,
                 w_ff1, w_ff2, g_post_mlp):
    bsz, L, _ = x.shape
    h = rmsnorm(x, g_pre_mix)
    proj = jnp.einsum('bld,dn->bln', h, w_in)
    widths = [S5_WIDTH, CONV_WIDTH, CONV_WIDTH, CONV_WIDTH, ATTN_WIDTH, ATTN_WIDTH,
              ATTN_WIDTH, ATTN_HEADS, N_BRANCH * D_MODEL]
    offsets = np.cumsum(widths)[:-1].tolist()
    (u_s5, x_conv, b_conv, c_conv, q, k, v, f_logit, gate_logits) = jnp.split(proj, offsets, axis=-1)

    y_a = s5_mixer(u_s5, a_re, a_im, log_dt, b_re, b_im, c_re, c_im, d_skip, w_glu)
    y_b = short_conv_mixer(x_conv, b_conv, c_conv, conv_w)
    y_c = forgetting_attention(q, k, v, f_logit, b_f)

    gates = jax.nn.sigmoid((gate_logits + b_gate).astype(jnp.float32)).astype(x.dtype)
    gates = gates.reshape(bsz, L, N_BRANCH, D_MODEL)
    wa = w_branch[:S5_WIDTH]
    wb = w_branch[S5_WIDTH:S5_WIDTH + CONV_WIDTH]
    wc = w_branch[S5_WIDTH + CONV_WIDTH:]
    merged = (gates[:, :, 0] * jnp.einsum('blc,cd->bld', y_a, wa)
              + gates[:, :, 1] * jnp.einsum('blc,cd->bld', y_b, wb)
              + gates[:, :, 2] * jnp.einsum('blc,cd->bld', y_c, wc))
    mix = jnp.einsum('bld,de->ble', merged, w_out)
    x = x + rmsnorm(mix, g_post_mix)

    h = rmsnorm(x, g_pre_mlp)
    ff = jnp.einsum('blf,fd->bld', jnp.square(jax.nn.relu(jnp.einsum('bld,df->blf', h, w_ff1))), w_ff2)
    return x + rmsnorm(ff, g_post_mlp)

def first_inputs(seed: int = 0) -> dict:
    key = jax.random.key(seed)
    ks = jax.random.split(key, 24)
    f32 = jnp.float32
    nrm = lambda k, shape, s: (jax.random.normal(k, shape, f32) * s)
    G, P, H = S5_GROUPS, S5_STATE, S5_GROUP
    x = jax.random.normal(ks[0], (BATCH, SEQ, D_MODEL), f32)
    g_pre_mix = 1.0 + nrm(ks[1], (DEPTH, D_MODEL), 0.05)
    w_in = nrm(ks[2], (DEPTH, D_MODEL, IN_WIDTH), D_MODEL ** -0.5)
    b_gate = nrm(ks[3], (DEPTH, N_BRANCH * D_MODEL), 0.01)
    n_idx = jnp.arange(P, dtype=f32)
    s5_a_re = -0.5 + nrm(ks[4], (DEPTH, G, P), 0.01)
    s5_a_im = math.pi * n_idx + nrm(ks[5], (DEPTH, G, P), 0.01)
    s5_log_dt = jax.random.uniform(ks[6], (DEPTH, G), f32, math.log(1e-3), math.log(1e-1))
    s5_b_re = nrm(ks[7], (DEPTH, G, P, H), (2.0 * H) ** -0.5)
    s5_b_im = nrm(ks[8], (DEPTH, G, P, H), (2.0 * H) ** -0.5)
    s5_c_re = nrm(ks[9], (DEPTH, G, H, P), (2.0 * P) ** -0.5)
    s5_c_im = nrm(ks[10], (DEPTH, G, H, P), (2.0 * P) ** -0.5)
    s5_d = nrm(ks[11], (DEPTH, G, H), 1.0)
    s5_w_glu = nrm(ks[12], (DEPTH, G, H, H), H ** -0.5)
    conv_w = nrm(ks[13], (DEPTH, CONV_K, CONV_WIDTH), CONV_K ** -0.5)
    fox_b_f = jnp.linspace(1.0, 6.0, ATTN_HEADS, dtype=f32)[None, :] + nrm(ks[14], (DEPTH, ATTN_HEADS), 0.1)
    w_branch = nrm(ks[15], (DEPTH, MIX_WIDTH, D_MODEL), S5_WIDTH ** -0.5)
    w_out = nrm(ks[16], (DEPTH, D_MODEL, D_MODEL), D_MODEL ** -0.5)
    g_post_mix = 1.0 + nrm(ks[17], (DEPTH, D_MODEL), 0.05)
    g_pre_mlp = 1.0 + nrm(ks[18], (DEPTH, D_MODEL), 0.05)
    w_ff1 = nrm(ks[19], (DEPTH, D_MODEL, D_FF), D_MODEL ** -0.5)
    w_ff2 = nrm(ks[20], (DEPTH, D_FF, D_MODEL), D_FF ** -0.5)
    g_post_mlp = 1.0 + nrm(ks[21], (DEPTH, D_MODEL), 0.05)
    return {"x": x, "g_pre_mix": g_pre_mix, "w_in": w_in, "b_gate": b_gate,
            "s5_a_re": s5_a_re, "s5_a_im": s5_a_im, "s5_log_dt": s5_log_dt,
            "s5_b_re": s5_b_re, "s5_b_im": s5_b_im, "s5_c_re": s5_c_re, "s5_c_im": s5_c_im,
            "s5_d": s5_d, "s5_w_glu": s5_w_glu, "conv_w": conv_w, "fox_b_f": fox_b_f,
            "w_branch": w_branch, "w_out": w_out, "g_post_mix": g_post_mix,
            "g_pre_mlp": g_pre_mlp, "w_ff1": w_ff1, "w_ff2": w_ff2, "g_post_mlp": g_post_mlp}

def first_block(x, g_pre_mix, w_in, b_gate, s5_a_re, s5_a_im, s5_log_dt, s5_b_re, s5_b_im,
              s5_c_re, s5_c_im, s5_d, s5_w_glu, conv_w, fox_b_f, w_branch, w_out,
              g_post_mix, g_pre_mlp, w_ff1, w_ff2, g_post_mlp):
    for layer in range(DEPTH):
        x = hybrid_layer(x, g_pre_mix[layer], w_in[layer], b_gate[layer],
                         s5_a_re[layer], s5_a_im[layer], s5_log_dt[layer],
                         s5_b_re[layer], s5_b_im[layer], s5_c_re[layer], s5_c_im[layer],
                         s5_d[layer], s5_w_glu[layer], conv_w[layer], fox_b_f[layer],
                         w_branch[layer], w_out[layer], g_post_mix[layer], g_pre_mlp[layer],
                         w_ff1[layer], w_ff2[layer], g_post_mlp[layer])
    return x


ATTN_HEADS_PER_GROUP = 8
DILATED_GROUPS = ((128, 1), (512, 4), (2048, 16))
N_DIL = len(DILATED_GROUPS)
ATTN_WIDTH_2 = ATTN_HEADS_PER_GROUP * HEAD_DIM
ROPE_DIM = HEAD_DIM // 4
ROPE_THETA = 500000.0
BLK = 128
SGU_CHUNK = 128
SGU_GROUPS = 8
SGU_WIDTH = D_MODEL // 2
SGU_GROUP_DIM = SGU_WIDTH // SGU_GROUPS
D_FF_2 = -(-8 * D_MODEL // (3 * 256)) * 256
QKV_COLS = 3 * N_DIL * ATTN_WIDTH_2
IN_COLS = QKV_COLS + 2 * SGU_WIDTH + 2 * D_MODEL


def rmsnorm_2(x, g):
    xf = x.astype(jnp.float32)
    y = xf * lax.rsqrt(jnp.mean(xf * xf, axis=-1, keepdims=True) + EPS)
    return (y * g.astype(jnp.float32)).astype(x.dtype)

def layernorm(x, g, b):
    xf = x.astype(jnp.float32)
    mu = jnp.mean(xf, axis=-1, keepdims=True)
    xc = xf - mu
    y = xc * lax.rsqrt(jnp.mean(xc * xc, axis=-1, keepdims=True) + EPS)
    return (y * g.astype(jnp.float32) + b.astype(jnp.float32)).astype(x.dtype)

def partial_rope(t, positions):
    half = ROPE_DIM // 2
    inv_freq = ROPE_THETA ** (-jnp.arange(0, ROPE_DIM, 2, dtype=jnp.float32) / ROPE_DIM)
    ang = positions.astype(jnp.float32)[..., None] * inv_freq
    cos = jnp.cos(ang)[:, :, None, :]
    sin = jnp.sin(ang)[:, :, None, :]
    tf = t.astype(jnp.float32)
    x1, x2 = tf[..., :half], tf[..., half:ROPE_DIM]
    rot = jnp.concatenate([x1 * cos - x2 * sin, x2 * cos + x1 * sin, tf[..., ROPE_DIM:]], axis=-1)
    return rot.astype(t.dtype)

def dilated_attention(q, k, v, window, dilation):
    B, S, H, Dh = q.shape
    span = window // dilation
    L = -(-S // dilation)
    L_pad = -(-L // BLK) * BLK
    S_pad = L_pad * dilation
    nb = L_pad // BLK
    pad = ((0, 0), (0, S_pad - S), (0, 0), (0, 0))

    def strided(t):
        t = jnp.pad(t, pad).reshape(B, L_pad, dilation, H, Dh).transpose(0, 2, 1, 3, 4)
        return t.reshape(B, dilation, nb, BLK, H, Dh)

    def with_prev(t):
        prev = jnp.pad(t, ((0, 0), (0, 0), (1, 0), (0, 0), (0, 0), (0, 0)))[:, :, :-1]
        return jnp.concatenate([prev, t], axis=3)

    qs = strided(q * (Dh ** -0.5))
    kb = with_prev(strided(k))
    vb = with_prev(strided(v))
    s = jnp.einsum('brnqhd,brnkhd->brnhqk', qs, kb, preferred_element_type=jnp.float32)

    i = jnp.arange(BLK)[:, None]
    j = jnp.arange(2 * BLK)[None, :]
    diff = BLK + i - j
    band = (diff >= 0) & (diff <= span)
    key_exists = (jnp.arange(nb)[:, None, None] > 0) | (j >= BLK)[None]
    mask = band[None] & key_exists
    s = jnp.where(mask[None, None, :, None], s, -jnp.inf)

    m = jnp.max(s, axis=-1, keepdims=True)
    p = jnp.exp(s - m)
    den = jnp.sum(p, axis=-1)
    lse = m[..., 0] + jnp.log(den)
    o = jnp.einsum('brnhqk,brnkhd->brnqhd', p, vb.astype(jnp.float32))
    o = o / jnp.swapaxes(den, -1, -2)[..., None]

    o = o.reshape(B, dilation, L_pad, H, Dh).transpose(0, 2, 1, 3, 4).reshape(B, S_pad, H, Dh)[:, :S]
    lse = jnp.swapaxes(lse, -1, -2).reshape(B, dilation, L_pad, H).transpose(0, 2, 1, 3)
    lse = lse.reshape(B, S_pad, H)[:, :S]
    return o.astype(q.dtype), lse

def spatial_gating(uv, ln_g, ln_b, w_s, b_s):
    B, S, _ = uv.shape
    z = jax.nn.gelu(uv, approximate=False)
    u, v = z[..., :SGU_WIDTH], z[..., SGU_WIDTH:]
    v = layernorm(v, ln_g, ln_b)
    vc = v.reshape(B, S // SGU_CHUNK, SGU_CHUNK, SGU_GROUPS, SGU_GROUP_DIM)
    causal = jnp.tril(jnp.ones((SGU_CHUNK, SGU_CHUNK), dtype=bool))
    w_causal = jnp.where(causal[None], w_s, jnp.zeros_like(w_s))
    mixed = jnp.einsum('gts,bnsgc->bntgc', w_causal, vc)
    mixed = mixed + jnp.transpose(b_s)[None, None, :, :, None]
    return u * mixed.reshape(B, S, SGU_WIDTH)

def second_inputs(seed: int = 0) -> dict:
    key = jax.random.key(seed)
    ks = jax.random.split(key, 18)
    f32 = jnp.float32
    x = jax.random.normal(ks[0], (BATCH, SEQ, D_MODEL), f32)
    offset = jax.random.randint(ks[1], (BATCH, 1), 0, 4096, dtype=jnp.int32)
    positions = offset + jnp.arange(SEQ, dtype=jnp.int32)[None, :]
    nrm = lambda k, shape, fan_in: jax.random.normal(k, shape, f32) * (fan_in ** -0.5)
    return {
        "x": x,
        "positions": positions,
        "norm1_g": 1.0 + 0.02 * jax.random.normal(ks[2], (DEPTH, D_MODEL), f32),
        "w_in": nrm(ks[3], (DEPTH, D_MODEL, IN_COLS), D_MODEL),
        "sgu_ln_g": 1.0 + 0.02 * jax.random.normal(ks[4], (DEPTH, SGU_WIDTH), f32),
        "sgu_ln_b": 0.02 * jax.random.normal(ks[5], (DEPTH, SGU_WIDTH), f32),
        "w_spatial": nrm(ks[6], (DEPTH, SGU_GROUPS, SGU_CHUNK, SGU_CHUNK), SGU_CHUNK),
        "b_spatial": 1.0 + 0.1 * jax.random.normal(ks[7], (DEPTH, SGU_GROUPS, SGU_CHUNK), f32),
        "w_proj_attn": nrm(ks[8], (DEPTH, ATTN_WIDTH_2, D_MODEL), ATTN_WIDTH_2),
        "w_proj_sgu": nrm(ks[9], (DEPTH, SGU_WIDTH, D_MODEL), SGU_WIDTH),
        "w_out": nrm(ks[10], (DEPTH, D_MODEL, D_MODEL), D_MODEL),
        "norm2_g": 1.0 + 0.02 * jax.random.normal(ks[11], (DEPTH, D_MODEL), f32),
        "w_ffn_gate": nrm(ks[12], (DEPTH, D_MODEL, D_FF_2), D_MODEL),
        "w_ffn_up": nrm(ks[13], (DEPTH, D_MODEL, D_FF_2), D_MODEL),
        "w_ffn_down": nrm(ks[14], (DEPTH, D_FF_2, D_MODEL), D_FF_2),
        "final_g": 1.0 + 0.02 * jax.random.normal(ks[15], (D_MODEL,), f32),
    }

def second_block(x, positions, norm1_g, w_in, sgu_ln_g, sgu_ln_b, w_spatial, b_spatial,
              w_proj_attn, w_proj_sgu, w_out, norm2_g, w_ffn_gate, w_ffn_up, w_ffn_down,
              final_g):
    B, S, _ = x.shape
    for l in range(DEPTH):
        h = rmsnorm_2(x, norm1_g[l])
        proj = h @ w_in[l]
        qkv = proj[..., :QKV_COLS].reshape(B, S, 3, N_DIL, ATTN_HEADS_PER_GROUP, HEAD_DIM)
        uv = proj[..., QKV_COLS:QKV_COLS + 2 * SGU_WIDTH]
        gate_a = jax.nn.sigmoid(proj[..., QKV_COLS + 2 * SGU_WIDTH:QKV_COLS + 2 * SGU_WIDTH + D_MODEL])
        gate_b = jax.nn.sigmoid(proj[..., QKV_COLS + 2 * SGU_WIDTH + D_MODEL:])

        outs, lses = [], []
        for g, (window, dilation) in enumerate(DILATED_GROUPS):
            q = partial_rope(qkv[:, :, 0, g], positions)
            k = partial_rope(qkv[:, :, 1, g], positions)
            o, lse = dilated_attention(q, k, qkv[:, :, 2, g], window, dilation)
            outs.append(o)
            lses.append(lse)
        alpha = jax.nn.softmax(jnp.stack(lses, axis=0), axis=0)
        attn = jnp.sum(alpha[..., None].astype(x.dtype) * jnp.stack(outs, axis=0), axis=0)
        attn = attn.reshape(B, S, ATTN_WIDTH_2)

        sgu = spatial_gating(uv, sgu_ln_g[l], sgu_ln_b[l], w_spatial[l], b_spatial[l])

        merged = gate_a * (attn @ w_proj_attn[l]) + gate_b * (sgu @ w_proj_sgu[l])
        x = x + merged @ w_out[l]

        h2 = rmsnorm_2(x, norm2_g[l])
        ff = jax.nn.silu(h2 @ w_ffn_gate[l]) * (h2 @ w_ffn_up[l])
        x = x + ff @ w_ffn_down[l]
    return rmsnorm_2(x, final_g)


def setup_inputs(seed=0):
    out = dict(first_inputs(seed))
    for name, value in second_inputs(seed + 1).items():
        if name != "x":
            out[name + "_2"] = value
    return out


def reference(
    x, g_pre_mix, w_in, b_gate, s5_a_re, s5_a_im, s5_log_dt, s5_b_re, s5_b_im, s5_c_re, s5_c_im,
    s5_d, s5_w_glu, conv_w, fox_b_f, w_branch, w_out, g_post_mix, g_pre_mlp, w_ff1, w_ff2,
    g_post_mlp, positions_2, norm1_g_2, w_in_2, sgu_ln_g_2, sgu_ln_b_2, w_spatial_2,
    b_spatial_2, w_proj_attn_2, w_proj_sgu_2, w_out_2, norm2_g_2, w_ffn_gate_2, w_ffn_up_2,
    w_ffn_down_2, final_g_2,
):
    x = first_block(
        x, g_pre_mix, w_in, b_gate, s5_a_re, s5_a_im, s5_log_dt, s5_b_re, s5_b_im, s5_c_re,
        s5_c_im, s5_d, s5_w_glu, conv_w, fox_b_f, w_branch, w_out, g_post_mix, g_pre_mlp, w_ff1,
        w_ff2, g_post_mlp,
    )
    return second_block(
        x, positions_2, norm1_g_2, w_in_2, sgu_ln_g_2, sgu_ln_b_2, w_spatial_2, b_spatial_2,
        w_proj_attn_2, w_proj_sgu_2, w_out_2, norm2_g_2, w_ffn_gate_2, w_ffn_up_2, w_ffn_down_2,
        final_g_2,
    )


_drawn_inputs = setup_inputs


def setup_inputs(seed=0):
    import zlib

    import numpy as np

    out = dict(_drawn_inputs(seed))
    spreads = {}
    factors = {'b_gate': 8.0,
     's5_a_re': 64.0,
     's5_a_im': 112.008,
     's5_log_dt': 111.328,
     's5_b_re': 200.0,
     's5_b_im': 200.0,
     's5_c_re': 200.0,
     's5_c_im': 200.0,
     'norm1_g_2': 8.0,
     'sgu_ln_g_2': 61.824,
     'sgu_ln_b_2': 57.939,
     'b_spatial_2': 2.683,
     'norm2_g_2': 25.042,
     'final_g_2': 23.98}
    for name, (base, spread) in spreads.items():
        noise = np.random.default_rng([zlib.crc32(name.encode()), seed]).standard_normal(out[name].shape)
        drawn = base * np.exp(spread * noise) if base else spread * noise
        out[name] = __import__('jax').numpy.asarray(drawn.astype(out[name].dtype))
    for name, factor in factors.items():
        out[name] = (out[name] * factor).astype(out[name].dtype)
    return out
```

```python
from contextlib import ExitStack

import concourse.bass as bass
from concourse import mybir

F32 = mybir.dt.float32
F32R = mybir.dt.float32r
I32 = mybir.dt.int32
ALU = mybir.AluOpType
ACT = mybir.ActivationFunctionType
AX = mybir.AxisListType.X

P = 128
L = 1024
D = 1024
KT = D // P
HALF = 512
EPS = 1e-6
UNIT = 2048

S5W, GRP, NG, ST = 512, 16, 32, 64
HEADS, HD = 8, 64
AW = HEADS * HD
DFF = 4 * D
O_U, O_X, O_B, O_C = 0, 512, 1024, 1536
O_Q, O_K, O_V, O_F, O_G = 2048, 2560, 3072, 3584, 3592
DFF2 = 2816
NDIL = 3
O2_QKV, O2_U, O2_V, O2_GA, O2_GB = 0, 4608, 5120, 5632, 6656

SC, NC = 8, 128
GB = 8

V_NORM = 0
V_BG = 7 * KT
V_CW = V_BG + 24
V_N = V_CW + 12

TWO_PI = 6.283185307179586
MAGIC = 12582912.0


def split_const(x, parts, bits):
    import math
    out = []
    for _ in range(parts - 1):
        e = math.floor(math.log2(abs(x)))
        q = 2.0 ** (e - bits + 1)
        c = math.floor(x / q) * q
        out.append(c)
        x -= c
    return out + [x]


PI_PARTS = split_const(TWO_PI, 3, 11)
LN2_PARTS = split_const(0.6931471805599453, 2, 12)


class Signal:

    def __init__(self, sem):
        self.sem, self.n = sem, 0

    def take(self, n):
        base = self.n
        self.n += n
        return base


def hybrid_kernel(nc, A, out, upto=99):
    ctx = ExitStack()
    with ctx:
        def sb(name, shape, dt=F32, at=ctx):
            return at.enter_context(nc.sbuf_tensor(name, shape, dt))

        def sig(name):
            return Signal(ctx.enter_context(nc.semaphore(name)))

        ps = ctx.enter_context(nc.psum_tensor("ps", [P, 8, HALF], F32))
        scratch = {n: nc.dram_tensor(n, s, F32).ap() for n, s in (
            ("x_keep", [P, KT, L]), ("y_keep", [3, P, 4, L]), ("dil_keep", [NDIL, L, HEADS, HD + 2]))}

        cst = sb("cst", [P, 6 * P + 8])
        ident = cst[:, 0:P]
        m_band = cst[:, P:3 * P]
        m_causal = cst[:, 2 * P:3 * P]
        m_even = cst[:, 3 * P:4 * P]
        ones = cst[:, 4 * P:5 * P]
        tril = cst[:, 5 * P:6 * P]
        c_freq = cst[:, 6 * P:6 * P + 1]
        c_rsgn = cst[:, 6 * P + 1:6 * P + 2]
        c_sgn = cst[:, 6 * P + 2:6 * P + 3]
        c_nsgn = cst[:, 6 * P + 3:6 * P + 4]
        vecs = sb("vecs", [P, V_N])
        rstd = sb("rstd", [P, L])
        bf = sb("bf", [P, 1])

        raw = [sb(f"raw{j}", [P, UNIT]) for j in range(2)]
        whi = [sb(f"whi{j}", [P, UNIT], F32R) for j in range(2)]
        wlo = [sb(f"wlo{j}", [P, UNIT], F32R) for j in range(2)]
        h_hi = sb("h_hi", [P, KT, L], F32R)
        with ExitStack() as at_low:
            xh = sb("xh", [P, KT, L], F32, at_low)
        h_lo = sb("h_lo", [P, KT, L], F32R)
        H = (h_hi, h_lo)

        def phase(items):
            at = ExitStack()
            made = [sb(n, s, d, at) for n, s, d in items]
            at.close()
            return made

        (U, ug, WT, W1, W2, MM, M2, TZ, CT, SN, tm, zz, PP, YA, WG, BA, BB, C1, C2, PR, PI, MR, MI,
         sm, ki, nat, DD, bst) = phase([
            ("U", [P, NG, SC, GRP], F32), ("ug", [P, GB, P], F32), ("WT", [P, GB, SC * GRP], F32),
            ("W1", [P, GB, P], F32), ("W2", [P, GB, P], F32), ("MM", [P, GB, SC + 1, GRP], F32),
            ("M2", [P, GB, SC, GRP], F32), ("TZ", [P, GB, P], F32), ("CT", [P, GB, NC], F32),
            ("SN", [P, GB, NC], F32), ("tm", [P, GB * (SC + 1) * GRP], F32), ("zz", [P, GB, NC], F32),
            ("PP", [P, 2, GB, NC + 1], F32), ("YA", [P, L], F32), ("WG", [P, P], F32),
            ("BA", [P, GB, GRP], F32), ("BB", [P, GB, GRP], F32), ("C1", [P, GB, GRP], F32),
            ("C2", [P, GB, GRP], F32), ("PR", [P, NG, SC + 1], F32), ("PI", [P, NG, SC + 1], F32),
            ("MR", [P, 8, NG], F32), ("MI", [P, 8, NG], F32), ("sm", [P, 20, NG], F32),
            ("ki", [P, NG], I32), ("nat", [P, 4, P], F32), ("DD", [GRP, NG], F32),
            ("bst", [P, 2, GB, GRP], F32)])
        (QA, KA, VT, PB, PT, OT, cum, Yc, mx, dn, rd) = phase([
            ("QA", [P, 4, L], F32), ("KA", [P, 4, L], F32), ("VT", [P, 8, 256], F32),
            ("PB", [P, 2, L], F32), ("PT", [P, 2, L], F32), ("OT", [P, 8, 256], F32),
            ("cum", [P, L], F32), ("Yc", [P, 4, L], F32),
            ("mx", [P, 64], F32), ("dn", [P, 64], F32), ("rd", [P, 64], F32)])
        (cx, vbuf, cacc) = phase([
            ("cx", [P, 2, L], F32), ("vbuf", [P, L + 2], F32), ("cacc", [P, 4, L], F32)])
        at_big = ExitStack()
        big = sb("big", [P, KT, L], F32, at_big)
        (y_hi, y_lo, yt, gate, bcur) = phase([
            ("y_hi", [P, 4, L], F32R), ("y_lo", [P, 4, L], F32R),
            ("yt", [P, 2, L], F32), ("gate", [P, 4, HALF], F32), ("bcur", [P, 2], F32)])
        (xr, sq, ht) = phase([
            ("xr", [P, KT, L], F32), ("sq", [P, 3, L], F32), ("ht", [P, 2, L], F32)])
        (f_hi, f_lo, fr, fv) = phase([
            ("f_hi", [P, 2, 2, L], F32R), ("f_lo", [P, 2, 2, L], F32R),
            ("fr", [P, 4, HALF], F32), ("fv", [P, 2, HALF], F32)])
        at_big.close()
        (COSR, SINR, Q2, K2, V2, rt, rp, PB2, PT2, OS, mx2) = phase([
            ("COSR", [P, L], F32), ("SINR", [P, L], F32), ("Q2", [64, 4, L], F32), ("K2", [64, 4, L], F32),
            ("V2", [P, 8, 256], F32), ("rt", [P, HALF], F32), ("rp", [P, HALF], F32),
            ("PB2", [P, 2, 4, 256], F32), ("PT2", [P, 2, 4, 2, P], F32), ("OS", [P, 8, 4, HD + 2], F32),
            ("mx2", [P, 32], F32)])
        ang = PB2[:, 0].rearrange("p h n -> p (h n)")
        ang2 = PB2[:, 1].rearrange("p h n -> p (h n)")
        posi = V2[:, 0:4].rearrange("p t n -> p (t n)").bitcast(I32)
        (Yd, dl, cw, ct) = phase([
            ("Yd", [P, 4, L], F32), ("dl", [P, 3, HEADS, HD + 2], F32), ("cw", [P, 8, 3 * HEADS], F32),
            ("ct", [P, 2, AW], F32)])
        (gu, gv, wsp, wspT, lng, lnb, bsp, st6, mv, st_tmp) = phase([
            ("gu", [P, 4, L], F32), ("gv", [P, 8, 512], F32), ("wsp", [P, 8, P], F32),
            ("wspT", [P, 8, P], F32), ("lng", [P, 512], F32), ("lnb", [P, 512], F32),
            ("bsp", [P, 4, P], F32), ("st6", [P, 6], F32), ("mv", [P, 4], F32), ("st_tmp", [P, 2, 4, P], F32)])
        ld = [sig(f"unit_loaded{j}") for j in range(2)]
        s_hi, s_lo, s_begun = sig("unit_hi_ready"), sig("unit_lo_ready"), sig("unit_begun")
        pe_a, pe_b = sig("pe_tile_a"), sig("pe_tile_b")
        dve_a, dve_b, act_a, act_b = sig("dve_took_a"), sig("dve_took_b"), sig("act_took_a"), sig("act_took_b")
        dv, ac, po, pe_s = sig("dve_step"), sig("act_step"), sig("pool_step"), sig("pe_step")
        d_in, d_in2 = sig("loaded"), sig("loaded_more")
        d_out, d_out_pool = sig("stored"), sig("stored_by_gpsimd")
        d_const, d_vec = sig("constants_loaded"), sig("vectors_loaded")


        def unit_no(c, i=None, per=2):
            return c, i, per

        def upto_unit(u, off):
            c, i, per = u
            return c + off if i is None else per * i + (c + off)

        def load_unit(sp, u, src, shape):
            c, i, per = u
            if c >= 2:
                sp.wait_ge(s_lo.sem, upto_unit(u, -1))
            k, n = shape
            sp.dma_start(raw[c % 2][:, 0:k * n].rearrange("p (k n) -> p k n", k=k), src).then_inc(ld[c % 2].sem, 16)

        def split_hi(act, u, early=False):
            c, i, per = u
            if i is None and (c >= N_UNITS or (c in early_units and not early)):
                return
            half = 16 * (c // 2 + 1)
            act.wait_ge(ld[c % 2].sem, half if i is None else 8 * per * i + half)
            if c >= 2:
                act.wait_ge(s_begun.sem, upto_unit(u, 0))
            nc.scalar.activation(whi[c % 2][:, :], raw[c % 2][:, :], ACT.Copy).then_inc(s_hi.sem, 1)

        def split_lo(pool, u):
            c, i, per = u
            if c >= N_UNITS and i is None:
                return
            pool.wait_ge(s_hi.sem, upto_unit(u, 1))
            nc.gpsimd.tensor_tensor(wlo[c % 2][:, :], raw[c % 2][:, :], whi[c % 2][:, :].bitcast(F32),
                                    ALU.subtract).then_inc(s_lo.sem, 1)

        def mm3(out_, lhs, rhs, ks, begins=False):
            for k in range(ks):
                for n, (a, b) in enumerate(((0, 0), (0, 1), (1, 0))):
                    last = nc.tensor.matmul(out_, lhs(a, k), rhs(b, k), start=(k == 0 and n == 0),
                                            stop=(k == ks - 1 and n == 2))
                    if begins and k == 0 and n == 0:
                        last.then_inc(s_begun.sem, 1)
            return last

        def unit_view(c, ks):
            cols = 1024 if ks == 4 else UNIT
            hi_lo = [w[c % 2][:, 0:cols].rearrange("p (k n) -> p k n", k=ks) for w in (whi, wlo)]
            return lambda a, k, lo, n: hi_lo[a][:, k, lo:lo + n]

        def feature_tiles(pe, u, ks, src, bank, waits, ready):
            w = unit_view(u[0], ks)
            pe.wait_ge(s_lo.sem, upto_unit(u, 1))
            for n in range(4):
                m, half = n // 2, n % 2
                for s, v in waits(n):
                    pe.wait_ge(s.sem, v)
                mm3(ps[:, bank + n, :], lambda a, k: w(a, k, m * P, P),
                    lambda b, k: src[b][:, k, half * HALF:(half + 1) * HALF], ks, n == 0).then_inc(ready.sem, 1)

        def first_tiles(pe, u, src, waits, ready, kwait):
            w = unit_view(u[0], KT)
            pe.wait_ge(s_lo.sem, upto_unit(u, 1))
            for n in range(4):
                for s, v in waits(n):
                    pe.wait_ge(s.sem, v)
            for k in range(KT):
                kwait(k)
                for n in range(4):
                    m, half = n // 2, n % 2
                    for q, (a, b) in enumerate(((0, 0), (0, 1), (1, 0))):
                        last = nc.tensor.matmul(ps[:, n, :], w(a, k, m * P, P),
                                                src[b][:, k, half * HALF:(half + 1) * HALF],
                                                start=(k == 0 and q == 0), stop=(k == KT - 1 and q == 2))
                        if k == 0 and n == 0 and q == 0:
                            last.then_inc(s_begun.sem, 1)
                    if k == KT - 1:
                        last.then_inc(ready.sem, 1)

        compute_signals = [pe_a, pe_b, dve_a, dve_b, act_a, act_b, dv, ac, po, pe_s, d_in, d_in2]
        marks = [{}, {}]

        class Stage:

            def __init__(self):
                self.after = [(x, n) for x, n in marks[-1].items() if n and marks[-2].get(x, 0) != n]

            def close(self, stores=True):
                marks.append({x: x.n for x in compute_signals + ([d_out, d_out_pool] if stores else [])})

            def begin(self, e, stores=True):
                for x, n in self.after:
                    if stores or x not in (d_out, d_out_pool):
                        e.wait_ge(x.sem, n)

            def sp(self, e): pass
            def act(self, e): pass
            def pool(self, e): pass
            def dve(self, e): pass
            def pe(self, e): pass

        units, early_units = [0], []

        def take_units(n):
            b = units[0]
            units[0] += n
            return b

        class LoadX(Stage):

            def __init__(self):
                super().__init__()
                self.a, self.da = pe_a.take(16), dve_a.take(16)
                self.i = (d_in.take(64), d_in2.take(64))

            def act(self, e):
                for t in range(8):
                    if t >= 2:
                        e.wait_ge(pe_a.sem, self.a + 2 * (t - 1))
                    e.dma_start(sq[:, t % 2, :], A["x"][0, t * P:(t + 1) * P, :]).then_inc((d_in, d_in2)[t % 2].sem, 16)

            def pe(self, e):
                e.wait_ge(d_const.sem, 16)
                for t in range(8):
                    e.wait_ge((d_in, d_in2)[t % 2].sem, self.i[t % 2] + 16 * (t // 2 + 1))
                    for q in range(2):
                        n = 2 * t + q
                        if n >= 4:
                            e.wait_ge(dve_a.sem, self.da + n - 3)
                        for j in range(4):
                            k = 4 * q + j
                            last = nc.tensor.transpose(ps[:, n % 4, j * P:(j + 1) * P],
                                                       sq[:, t % 2, k * P:(k + 1) * P], ident)
                        last.then_inc(pe_a.sem, 1)

            def dve(self, e):
                for n in range(16):
                    t, q = n // 2, n % 2
                    e.wait_ge(pe_a.sem, self.a + n + 1)
                    nc.vector.tensor_copy(big[:, 4 * q:4 * q + 4, t * P:(t + 1) * P],
                                          ps[:, n % 4, :].rearrange("p (k t) -> p k t", k=4)).then_inc(dve_a.sem, 1)

        class Vectors(Stage):

            def __init__(self):
                super().__init__()
                self.p, self.d = pe_s.take(1), dv.take(1)

            def pe(self, e):
                self.begin(e)
                e.wait_ge(d_vec.sem, 16 * 10)
                nc.tensor.transpose(ps[:, 4, 0:V_N], ht[0:V_N, 0, 0:P], ident[0:V_N, 0:V_N]).then_inc(pe_s.sem, 1)

            def dve(self, e):
                e.wait_ge(pe_s.sem, self.p + 1)
                nc.vector.tensor_copy(vecs[:, :], ps[:, 4, 0:V_N]).then_inc(dv.sem, 1)

        class Rstd:

            def __init__(self, bank):
                self.bank = bank
                self.a, self.d, self.p = ac.take(9), dv.take(2), pe_s.take(8)

            def act(self, e, final):
                for k in range(KT):
                    for x, n in final(k):
                        e.wait_ge(x.sem, n)
                    if k >= 3:
                        e.wait_ge(pe_s.sem, self.p + k - 2)
                    nc.scalar.activation(sq[:, k % 3, :], big[:, k, :], ACT.Square).then_inc(ac.sem, 1)
                e.wait_ge(dv.sem, self.d + 1)
                nc.scalar.activation(rstd[:, :], rstd[:, :], ACT.Sqrt).then_inc(ac.sem, 1)

            def dve(self, e):
                e.wait_ge(pe_s.sem, self.p + 8)
                nc.vector.tensor_scalar(rstd[:, :], ps[:, self.bank:self.bank + 2, :].rearrange("p a n -> p (a n)"),
                                        1.0 / D, EPS, ALU.mult, ALU.add).then_inc(dv.sem, 1)
                e.wait_ge(ac.sem, self.a + 9)
                nc.vector.reciprocal(rstd[:, :], rstd[:, :]).then_inc(dv.sem, 1)
                e.wait_ge(dv.sem, self.d + 2)

            def pe(self, e):
                for k in range(KT):
                    e.wait_ge(ac.sem, self.a + k + 1)
                    for half in range(2):
                        last = nc.tensor.matmul(ps[:, self.bank + half, :], ones,
                                                sq[:, k % 3, half * HALF:(half + 1) * HALF],
                                                start=k == 0, stop=k == KT - 1)
                    last.then_inc(pe_s.sem, 1)

        def vec(row, k):
            return vecs[:, row + k:row + k + 1]

        def after_a(k):
            return max(2 * k, 1)

        def after_b(k):
            return min(2 * k + 3, 2 * KT)

        def in_pairs(a, b):
            for k in range(KT):
                a(k)
                if k:
                    b(k - 1)
            b(KT - 1)

        class Norm(Stage):

            def __init__(self, row, post=None, x=None, x_in=None, final=None, bank=4, keep=False):
                super().__init__()
                self.row, self.post, self.x, self.x_in, self.final, self.keep = row, post, x, x_in, final, keep
                if post is not None:
                    self.r0, self.d0 = Rstd(bank), dv.take(16)
                self.r = Rstd(4)
                self.a, self.d = ac.take(8), dv.take(16)
                early_units.append(units[0] + 1)
                self.next_unit = units[0]
                if keep:
                    d_out.take(16)

            def ready(self, k):
                return [(dv, self.d + after_b(k))]

            def act(self, e):
                if self.final is None:
                    self.begin(e)
                final = self.final or (lambda k: [])
                if self.post is not None:
                    self.r0.act(e, final)
                    final = lambda k: [(dv, self.d0 + after_b(k))]
                self.r.act(e, final)
                if self.keep:
                    e.dma_start(scratch["x_keep"], big[:, :, :]).then_inc(d_out.sem, 16)
                for k in range(KT):
                    e.wait_ge(dv.sem, self.d + after_a(k))
                    nc.scalar.activation(h_hi[:, k, :], ht[:, k % 2, :], ACT.Copy).then_inc(ac.sem, 1)
                    if k == 4:
                        split_hi(e, unit_no(self.next_unit + 1), early=True)

            def dve(self, e):
                if self.final is None:
                    self.begin(e)
                if self.post is not None:
                    self.r0.dve(e)
                    e.wait_ge(d_in.sem, self.x_in + 16)

                    def scale(k):
                        nc.vector.scalar_tensor_tensor(out=big[:, k, :], in0=big[:, k, :], scalar=vec(self.post, k),
                                                       in1=rstd[:, :], op0=ALU.mult, op1=ALU.mult).then_inc(dv.sem, 1)

                    def add_x(k):
                        e.wait_ge(dv.sem, self.d0 + after_a(k))
                        nc.vector.tensor_tensor(big[:, k, :], big[:, k, :], self.x[:, k, :], ALU.add).then_inc(dv.sem, 1)
                    in_pairs(scale, add_x)
                self.r.dve(e)

                def normed(k):
                    if k >= 2:
                        e.wait_ge(dv.sem, self.d + after_b(k - 2))
                    nc.vector.scalar_tensor_tensor(out=ht[:, k % 2, :], in0=big[:, k, :], scalar=vec(self.row, k),
                                                   in1=rstd[:, :], op0=ALU.mult, op1=ALU.mult).then_inc(dv.sem, 1)

                def low(k):
                    e.wait_ge(ac.sem, self.a + k + 1)
                    nc.vector.tensor_tensor(h_lo[:, k, :], ht[:, k % 2, :], h_hi[:, k, :].bitcast(F32),
                                            ALU.subtract).then_inc(dv.sem, 1)
                in_pairs(normed, low)

            def pe(self, e):
                if self.final is None:
                    self.begin(e)
                if self.post is not None:
                    self.r0.pe(e)
                self.r.pe(e)

        class Store0(Stage):

            def __init__(self):
                super().__init__()
                d_out.take(16)

            def act(self, e):
                self.begin(e)
                e.dma_start(scratch["x_keep"], big[:, :, :]).then_inc(d_out.sem, 16)

        class Final(Stage):

            def __init__(self, final):
                super().__init__()
                self.final, self.r = final, Rstd(0)
                self.d, self.a, self.da = dv.take(8), pe_a.take(16), dve_a.take(16)
                d_out.take(16 * 8)

            def act(self, e):
                self.r.act(e, self.final)
                for t in range(8):
                    e.wait_ge(dve_a.sem, self.da + 2 * t + 2)
                    e.dma_start(out[0, t * P:(t + 1) * P, :], xr[:, t, :]).then_inc(d_out.sem, 16)

            def dve(self, e):
                self.r.dve(e)
                for k in range(KT):
                    nc.vector.scalar_tensor_tensor(out=big[:, k, :], in0=big[:, k, :], scalar=vec(V_NORM + 6 * KT, k),
                                                   in1=rstd[:, :], op0=ALU.mult, op1=ALU.mult).then_inc(dv.sem, 1)
                for n in range(16):
                    e.wait_ge(pe_a.sem, self.a + n + 1)
                    nc.vector.tensor_copy(xr[:, n // 2, (n % 2) * HALF:(n % 2 + 1) * HALF],
                                          ps[:, n % 4, :]).then_inc(dve_a.sem, 1)

            def pe(self, e):
                self.r.pe(e)
                e.wait_ge(dv.sem, self.d + 8)
                for n in range(16):
                    t, q = n // 2, n % 2
                    if n >= 4:
                        e.wait_ge(dve_a.sem, self.da + n - 3)
                    for j in range(4):
                        last = nc.tensor.transpose(ps[:, n % 4, j * P:(j + 1) * P],
                                                   big[:, 4 * q + j, t * P:(t + 1) * P], ident)
                    last.then_inc(pe_a.sem, 1)

        class Out(Stage):

            def __init__(self, w, merge, add_x):
                super().__init__()
                self.w, self.merge, self.add_x = w, merge, add_x
                self.u, self.a, self.da = take_units(4), pe_a.take(16), dve_a.take(16)
                self.ac, self.d, self.x_in = ac.take(8), dv.take(8), d_in.take(16)

            def final(self, k):
                return [(dve_a, self.da + 2 * k + 2)]

            def sp(self, e):
                for j in range(4):
                    load_unit(e, unit_no(self.u + j), w_cols(self.w, 0, 256 * j, KT, 256), (KT, 256))

            def act(self, e):
                e.wait_ge(pe_a.sem, self.a)
                for k in range(KT):
                    e.wait_ge(dv.sem, self.merge.final(k))
                    nc.scalar.activation(h_hi[:, k, :], big[:, k, :], ACT.Copy).then_inc(ac.sem, 1)
                e.wait_ge(pe_b.sem, self.merge.b + 16 * self.merge.nb)
                e.dma_start(xr[:, :, :], scratch["x_keep"]).then_inc(d_in.sem, 16)
                with e.Fori(0, 2) as i:
                    for j in range(2):
                        split_hi(e, unit_no(self.u + 1 + j, i))

            def pool(self, e):
                with e.Fori(0, 2) as i:
                    for j in range(2):
                        split_lo(e, unit_no(self.u + 1 + j, i))

            def dve(self, e):
                for k in range(KT):
                    e.wait_ge(ac.sem, self.ac + k + 1)
                    nc.vector.tensor_tensor(h_lo[:, k, :], big[:, k, :], h_hi[:, k, :].bitcast(F32),
                                            ALU.subtract).then_inc(dv.sem, 1)
                e.wait_ge(dv.sem, self.d + 8)
                if self.add_x:
                    e.wait_ge(d_in.sem, self.x_in + 16)
                with e.Fori(0, 2) as i:
                    for n in range(8):
                        e.wait_ge(pe_a.sem, 8 * i + (self.a + n + 1))
                        at = (slice(None), bass.ds(4 * i + n // 2, 1), slice((n % 2) * HALF, (n % 2 + 1) * HALF))
                        if self.add_x:
                            nc.vector.tensor_tensor(big[at], ps[:, n % 4, :].unsqueeze(1), xr[at], ALU.add
                                                    ).then_inc(dve_a.sem, 1)
                        else:
                            nc.vector.tensor_copy(big[at], ps[:, n % 4, :].unsqueeze(1)).then_inc(dve_a.sem, 1)

            def pe(self, e):
                first_tiles(e, unit_no(self.u), H, lambda n: [], pe_a,
                            lambda k: e.wait_ge(dv.sem, self.d + k + 1))
                for j in range(1, 4):
                    feature_tiles(e, unit_no(self.u + j), KT, H, 0,
                                  lambda n: [(dve_a, self.da + 4 * j + n - 3)], pe_a)

        def w_cols(w, row0, col0, ks, n):
            return w[row0:row0 + ks * P, col0:col0 + n].rearrange("(k p) n -> p k n", p=P)

        class Merge(Stage):

            def __init__(self, w_in, gate_col, w_branch, bias):
                super().__init__()
                self.w_in, self.gate_col, self.wb, self.bias = w_in, gate_col, w_branch, bias
                nb = self.nb = len(w_branch)
                self.u = take_units(8 * nb)
                self.a, self.b = pe_a.take(16 * nb), pe_b.take(16 * nb)
                self.aa = act_a.take(16 * nb)
                self.d = [dv.take(16 if b == 0 else 32) for b in range(nb)]
                self.per = 4 if bias is None else 8
                self.ac, self.lo = ac.take(self.per * nb), dve_a.take(4 * nb)
                self.i = (d_in.take(32 * nb), d_in2.take(32 * nb))

            def final(self, k):
                return self.d[-1] + 4 * (k + 1)

            def taken(self, b, i, n):
                if b == 0:
                    return 4 * i + (self.d[0] + n - 3)
                return 8 * i + (self.d[b] + (n - 3 if b == 1 else 2 * n - 6))

            def sp(self, e):
                for b in range(self.nb):
                    for i in range(4):
                        u = self.u + 8 * b + 2 * i
                        load_unit(e, unit_no(u), w_cols(self.w_in, 0, self.gate_col[b] + 256 * i, KT, 256), (KT, 256))
                        load_unit(e, unit_no(u + 1), w_cols(self.wb[b], 0, 256 * i, 4, 256), (4, 256))

            def act(self, e):
                self.begin(e)
                for b in range(self.nb):
                    for k in range(4):
                        n = 4 * b + k
                        if n >= 2:
                            e.wait_ge(dve_a.sem, self.lo + n - 1)
                        e.dma_start(yt[:, k % 2, :], scratch["y_keep"][b, :, k, :]).then_inc((d_in, d_in2)[k % 2].sem, 16)
                        if k == 0:
                            continue
                        if k == 1 and b:
                            e.wait_ge(pe_b.sem, self.b + 16 * b)
                        for kk in (0, 1) if k == 1 else (k,):
                            e.wait_ge((d_in, d_in2)[kk % 2].sem, self.i[kk % 2] + 16 * ((4 * b + kk) // 2 + 1))
                            nc.scalar.activation(y_hi[:, kk, :], yt[:, kk % 2, :], ACT.Copy).then_inc(ac.sem, 1)
                    with e.Fori(0, 4) as i:
                        if self.bias is not None:
                            e.wait_ge(act_a.sem, 4 * i + (self.aa + 16 * b))
                            nc.scalar.activation(bcur[:, :], vecs[:, bass.ds(2 * i + (self.bias + 8 * b), 2)],
                                                 ACT.Copy).then_inc(ac.sem, 1)
                        split_hi(e, unit_no(self.u + 8 * b + 1, i))
                        for n in range(4):
                            if n == 0 and self.bias is not None:
                                e.wait_ge(ac.sem, i + (self.ac + self.per * b + 5))
                            e.wait_ge(dv.sem, self.taken(b, i, n))
                            e.wait_ge(pe_a.sem, 4 * i + (self.a + 16 * b + n + 1))
                            if self.bias is None:
                                nc.scalar.activation(gate[:, n, :], ps[:, n, :], ACT.Sigmoid).then_inc(act_a.sem, 1)
                            else:
                                nc.scalar.activation(
                                    gate[:, n, :], ps[:, n, :], ACT.Sigmoid,
                                    bias=bcur[:, n // 2:n // 2 + 1]).then_inc(act_a.sem, 1)
                        split_hi(e, unit_no(self.u + 8 * b + 2, i))

            def pool(self, e):
                for b in range(self.nb):
                    with e.Fori(0, 4) as i:
                        split_lo(e, unit_no(self.u + 8 * b + 1, i))
                        split_lo(e, unit_no(self.u + 8 * b + 2, i))

            def dve(self, e):
                self.begin(e)
                for b in range(self.nb):
                    for k in range(4):
                        e.wait_ge(ac.sem, self.ac + self.per * b + k + 1)
                        nc.vector.tensor_tensor(y_lo[:, k, :], yt[:, k % 2, :], y_hi[:, k, :].bitcast(F32),
                                                ALU.subtract).then_inc(dve_a.sem, 1)
                    with e.Fori(0, 4) as i:
                        for n in range(4):
                            dst = big[:, bass.ds(2 * i + n // 2, 1), (n % 2) * HALF:(n % 2 + 1) * HALF]
                            e.wait_ge(act_a.sem, 4 * i + (self.aa + 16 * b + n + 1))
                            e.wait_ge(pe_b.sem, 4 * i + (self.b + 16 * b + n + 1))
                            if b == 0:
                                nc.vector.tensor_tensor(dst, gate[:, n, :].unsqueeze(1), ps[:, 4 + n, :].unsqueeze(1),
                                                        ALU.mult).then_inc(dv.sem, 1)
                            else:
                                nc.vector.tensor_tensor(gate[:, n, :], gate[:, n, :], ps[:, 4 + n, :],
                                                        ALU.mult).then_inc(dv.sem, 1)
                                e.wait_ge(dv.sem, 8 * i + (self.d[b] + 2 * n + 1))
                                nc.vector.tensor_tensor(dst, dst, gate[:, n, :].unsqueeze(1), ALU.add).then_inc(dv.sem, 1)

            def pe(self, e):
                self.begin(e, stores=False)
                for b in range(self.nb):
                    with e.Fori(0, 4) as i:
                        feature_tiles(e, unit_no(self.u + 8 * b, i), KT, H, 0,
                                      lambda n: [(act_a, 4 * i + (self.aa + 16 * b + n - 3))], pe_a)
                        e.wait_ge(dve_a.sem, self.lo + 4 * b + 4)
                        feature_tiles(e, unit_no(self.u + 8 * b + 1, i), 4, (y_hi, y_lo), 4,
                                      lambda n: [(dv, self.taken(b, i, n))], pe_b)

        class FeedForward(Stage):

            def __init__(self, ups, down, width, norm, onto_x, load_x=False):
                super().__init__()
                self.norm, self.onto_x, self.stored = norm, onto_x, d_out.n
                self.x_in = d_in.take(16) if load_x else None
                self.ups, self.down, self.n = ups, down, width // 256
                self.g = len(ups)
                n = self.n
                self.u = take_units(n * (self.g + 1))
                self.a, self.b = pe_a.take(4 * self.g * n), pe_b.take(16 * n)
                self.aa, self.db, self.d = act_a.take(4 * n), dve_b.take(16 * n), dv.take(8 * n)
                self.o = po.take(4 * n) - 1 if onto_x else po.take(4 * n + 1)

            def final(self, k):
                return [(po, self.o + 4 * self.n + 1), (dve_b, self.db + 16 * (self.n - 1) + 2 * k + 2)]

            def units_of(self, c, i):
                per = 2 * (self.g + 1)
                first = self.u + self.g + (self.g + 1) * c
                return [unit_no(first + j, i, per) for j in range(self.g + 1)]

            def slots(self, e, ups, down):
                n = self.n
                ups(0, None, [unit_no(self.u + j) for j in range(self.g)])
                pairs = (n - 1) // 2
                with e.Fori(0, pairs) as i:
                    for c in range(2):
                        us = self.units_of(c, i)
                        ups(c + 1, i, us[:-1])
                        down(c, i, us[-1])
                for c in range(2 * pairs, n):
                    us = self.units_of(c, None)
                    if c + 1 < n:
                        ups(c + 1, None, us[:-1])
                        down(c, None, us[-1])
                    else:
                        down(c, None, unit_no(self.u + (self.g + 1) * n - 1))

            @staticmethod
            def at(base, step, c, i):
                return base + step * c if i is None else 2 * step * i + (base + step * c)

            def sp(self, e):
                def col(c, i):
                    return 256 * c if i is None else e.snap(512 * i + 256 * c)

                def ups(c, i, us):
                    for w, u in zip(self.ups, us):
                        load_unit(e, u, w[:, bass.ds(col(c, i), 256)].rearrange("(k p) n -> p k n", p=P), (KT, 256))

                def down(c, i, u):
                    load_unit(e, u, self.down[bass.ds(col(c, i), 256), :].rearrange("(k p) n -> p k n", p=P), (2, D))
                self.slots(e, ups, down)
                if self.x_in is not None:
                    e.wait_ge(d_out.sem, self.stored)
                    e.wait_ge(pe_a.sem, self.a + 4 * self.g * self.n)
                    e.dma_start(xh[:, :, :], scratch["x_keep"]).then_inc(d_in.sem, 16)

            def act(self, e):
                self.begin(e)

                def ups(c, i, us):
                    split_hi(e, (us[0][0] + 1,) + us[0][1:])
                    for n in range(4):
                        if not (i is None and c == 0):
                            e.wait_ge(dv.sem, self.at(self.d, 8, c - 1, i) + (2 * n + 1))
                        e.wait_ge(pe_a.sem, self.at(self.a, 4 * self.g, c, i) + (n + 1))
                        nc.scalar.activation(fr[:, n, :], ps[:, n, :], ACT.Relu if self.g == 1 else ACT.Silu
                                             ).then_inc(act_a.sem, 1)
                    if self.g == 2:
                        split_hi(e, (us[1][0] + 1,) + us[1][1:])

                def down(c, i, u):
                    split_hi(e, (u[0] + 1,) + u[1:])
                self.slots(e, ups, down)

            def pool(self, e):
                split_lo(e, unit_no(self.u + 1))
                self.begin(e)
                if not self.onto_x:
                    e.wait_ge(d_out.sem, self.stored)
                    nc.gpsimd.memset(big[:, :, :], 0.0).then_inc(po.sem, 1)

                def ups(c, i, us):
                    if not (c == 0 and i is None):
                        split_lo(e, (us[0][0] + 1,) + us[0][1:])
                    if self.g == 2:
                        split_lo(e, (us[1][0] + 1,) + us[1][1:])
                    for n in range(4):
                        e.wait_ge(dv.sem, self.at(self.d, 8, c, i) + (2 * n + 2))
                        nc.gpsimd.tensor_tensor(f_lo[:, c % 2, n // 2, (n % 2) * HALF:(n % 2 + 1) * HALF],
                                                fv[:, n % 2, :],
                                                f_hi[:, c % 2, n // 2, (n % 2) * HALF:(n % 2 + 1) * HALF].bitcast(F32),
                                                ALU.subtract).then_inc(po.sem, 1)

                def down(c, i, u):
                    split_lo(e, (u[0] + 1,) + u[1:])
                self.slots(e, ups, down)

            def dve(self, e):
                self.begin(e)

                def ups(c, i, us):
                    for n in range(4):
                        e.wait_ge(act_a.sem, self.at(self.aa, 4, c, i) + (n + 1))
                        e.wait_ge(po.sem, self.at(self.o, 4, c, i) + n)
                        if self.g == 1:
                            nc.vector.tensor_tensor(fv[:, n % 2, :], fr[:, n, :], fr[:, n, :], ALU.mult).then_inc(dv.sem, 1)
                        else:
                            e.wait_ge(pe_a.sem, self.at(self.a, 8, c, i) + (4 + n + 1))
                            nc.vector.tensor_tensor(fv[:, n % 2, :], fr[:, n, :], ps[:, n, :], ALU.mult).then_inc(dv.sem, 1)
                        if n == 0 and (i is not None or c >= 2):
                            e.wait_ge(pe_b.sem, self.at(self.b, 16, c - 1, i))
                        e.wait_ge(dv.sem, self.at(self.d, 8, c, i) + (2 * n + 1))
                        nc.vector.tensor_copy(f_hi[:, c % 2, n // 2, (n % 2) * HALF:(n % 2 + 1) * HALF],
                                              fv[:, n % 2, :]).then_inc(dv.sem, 1)

                def down(c, i, u):
                    for t in range(16):
                        m, half = t // 2, t % 2
                        e.wait_ge(pe_b.sem, self.at(self.b, 16, c, i) + (t + 1))
                        e.wait_ge(dve_b.sem, self.at(self.db, 16, c, i) + (t - 15))
                        dst = big[:, m, half * HALF:(half + 1) * HALF]
                        nc.vector.tensor_tensor(dst, dst, ps[:, 4 + t % 4, :], ALU.add).then_inc(dve_b.sem, 1)
                self.slots(e, ups, down)

            def pe(self, e):
                def ups(c, i, us):
                    first = i is None and c == 0
                    if first:
                        first_tiles(e, us[0], H, lambda n: [], pe_a,
                                    lambda k: [e.wait_ge(x.sem, n) for x, n in self.norm.ready(k)])
                    elif self.g == 1:
                        feature_tiles(e, us[0], KT, H, 0, lambda n: [(act_a, self.at(self.aa, 4, c, i) + (n - 3))], pe_a)
                    else:
                        feature_tiles(e, us[0], KT, H, 0,
                                      lambda n: [(dv, self.at(self.d, 8, c, i) + (2 * n - 7))], pe_a)
                    if self.g == 2:
                        feature_tiles(e, us[1], KT, H, 0,
                                      lambda n: [(act_a, self.at(self.aa, 4, c, i) + (n + 1))], pe_a)

                def down(c, i, u):
                    w = unit_view(u[0], 2)
                    e.wait_ge(s_lo.sem, upto_unit(u, 1))
                    e.wait_ge(po.sem, self.at(self.o, 4, c, i) + 5)
                    for t in range(16):
                        m, half = t // 2, t % 2
                        e.wait_ge(dve_b.sem, self.at(self.db, 16, c, i) + (t - 3))
                        mm3(ps[:, 4 + t % 4, :], lambda a, k: w(a, k, m * P, P),
                            lambda b, k: (f_hi, f_lo)[b][:, c % 2, k, half * HALF:(half + 1) * HALF],
                            2, t == 0).then_inc(pe_b.sem, 1)
                self.slots(e, ups, down)

        m = {n: sig(n) for n in (
            "s5_in", "s5_natT", "s5_arg", "s5_fun", "s5_cT", "s5_wt", "s5_mm", "s5_m2", "s5_wT", "s5_k", "s5_w",
            "s5_kp", "s5_tz", "s5_uT", "s5_ug", "s5_v", "s5_p", "s5_y", "s5_g", "s5_yT", "s5_ya", "s5_glu",
            "s5_sg", "s5_out", "s5_step", "s5_wg", "s5_ld")}
        s5_done = m["s5_out"]
        s5_done.take(4)
        m = {n: x.sem for n, x in m.items()}

        class S5(Stage):

            def __init__(self):
                super().__init__()
                self.u = take_units(2)
                self.a, self.aa = pe_a.take(16), act_a.take(16)
                self.out = d_out.take(64)

            def close(self):
                super().close()
                marks[-1][s5_done] = 4

            def sp(self, e):
                for j in range(2):
                    load_unit(e, unit_no(self.u + j), w_cols(A["w_in"][0], 0, O_U + 256 * j, KT, 256), (KT, 256))

            def act(self, e):
                self.begin(e)
                for k, name in enumerate(("s5_a_re", "s5_a_im")):
                    for half in range(2):
                        e.dma_start(nat[0:NG, 2 + k, half * ST:(half + 1) * ST], A[name][0]).then_inc(m["s5_ld"], 16)
                e.dma_start(sm[:, 19, :], A["s5_log_dt"][0:1, :].partition_broadcast(P)).then_inc(m["s5_ld"], 16)
                e.dma_start(DD[:, :], A["s5_d"][0].rearrange("g h -> h g"),
                            allow_slow_non_contiguous=True).then_inc(m["s5_ld"], 16)
                for n, (o, i, fn, sc) in enumerate(((1, 0, ACT.Tanh, 0.5), (5, 4, ACT.Tanh, 0.5),
                                                    (7, 6, ACT.Sin, 1.0), (8, 6, ACT.Sin, 0.5))):
                    if n != 3:
                        e.wait_ge(m["s5_arg"], n + 1)
                    nc.scalar.activation(sm[:, o, :], sm[:, i, :], fn, scale=sc).then_inc(m["s5_fun"], 1)
                split_hi(e, unit_no(self.u + 1))
                for n in range(16):
                    j, s = n // 8, n % 8
                    e.wait_ge(pe_a.sem, self.a + n + 1)
                    nc.scalar.activation(U[:, 16 * j:16 * j + 16, SC - 1 - s, :],
                                         ps[:, n % 4, 0:256].rearrange("p (g h) -> p g h", h=GRP),
                                         ACT.Copy).then_inc(act_a.sem, 1)
                    if n == 7:
                        split_hi(e, unit_no(self.u + 2))
                for f in range(4):
                    if f:
                        e.wait_ge(m["s5_out"], f)
                    rows = slice(f * P, f * P + P)
                    cre = A["s5_c_re"][0].rearrange("g h p -> (g h) p")
                    cim = A["s5_c_im"][0].rearrange("g h p -> (g h) p")
                    for k, (lo, hi_) in enumerate(((cre, cim), (cim, cre))):
                        e.dma_start(nat[:, k, 0:ST], lo[rows, :]).then_inc(m["s5_in"], 16)
                        e.dma_start(nat[:, k, ST:P], hi_[rows, :]).then_inc(m["s5_in"], 16)
                    gr = slice(f * GB, f * GB + GB)
                    bre = A["s5_b_re"][0][gr].rearrange("g p h -> p g h")
                    bim = A["s5_b_im"][0][gr].rearrange("g p h -> p g h")
                    for k, (lo, hi_) in enumerate(((bre, bim), (bim, bre))):
                        e.dma_start(bst[0:ST, k], lo).then_inc(m["s5_in"], 16)
                        e.dma_start(bst[ST:P, k], hi_).then_inc(m["s5_in"], 16)
                    if f == 0:
                        e.wait_ge(m["s5_wg"], 1)
                    for g in range(GB):
                        e.dma_start(WG[g * GRP:(g + 1) * GRP, g * GRP:(g + 1) * GRP],
                                    A["s5_w_glu"][0, f * GB + g]).then_inc(m["s5_in"], 16)
                    e.wait_ge(m["s5_wT"], f + 1)
                    v = ps[:, 0:2, :].rearrange("p b (g n) -> p (b g) n", n=P)
                    nc.scalar.activation(W1[:, :, :], v, ACT.Copy)
                    nc.scalar.activation(W2[:, :, 0:ST], v[:, :, ST:P], ACT.Copy)
                    nc.scalar.activation(W2[:, :, ST:P], v[:, :, 0:ST], ACT.Copy, scale=-1.0).then_inc(m["s5_w"], 1)
                    e.wait_ge(m["s5_uT"], f + 1)
                    nc.scalar.activation(ug[:, :, :], ps[:, 4:6, :].rearrange("p b (g n) -> p (b g) n", n=P),
                                         ACT.Copy).then_inc(m["s5_ug"], 1)
                    e.wait_ge(m["s5_y"], f + 1)
                    yv = WT[:, :, :].rearrange("p a b -> p (a b)").rearrange("p (t g h) -> p g t h", t=SC, g=GB)
                    for b in range(2):
                        last = nc.scalar.activation(
                            yv[:, 4 * b:4 * b + 4], ps[:, 4 + b, :].rearrange("p (g t h) -> p g t h", g=4, t=SC),
                            ACT.Gelu_apprx_tanh)
                    last.then_inc(m["s5_g"], 1)
                    e.wait_ge(m["s5_yT"], f + 1)
                    if f:
                        e.wait_ge(d_out.sem, self.out + 16 * f)
                    for b in range(2):
                        last = nc.scalar.activation(
                            YA[:, :].rearrange("p (c t) -> p t c", t=SC)[:, 4 * b:4 * b + 4, :],
                            ps[:, 6 + b, :].rearrange("p (t c) -> p t c", t=4), ACT.Copy)
                    last.then_inc(m["s5_ya"], 1)
                    e.wait_ge(m["s5_glu"], f + 1)
                    nc.scalar.activation(tm[:, 0:L], ps[:, 0:2, :].rearrange("p b n -> p (b n)"),
                                         ACT.Sigmoid).then_inc(m["s5_sg"], 1)
                    e.wait_ge(m["s5_out"], f + 1)
                    e.dma_start(scratch["y_keep"][0, :, f, :], YA[:, :]).then_inc(d_out.sem, 16)

            def pool(self, e):
                self.begin(e)
                nc.gpsimd.memset(WG[:, :], 0.0).then_inc(m["s5_wg"], 1)
                split_lo(e, unit_no(self.u + 1))
                split_lo(e, unit_no(self.u + 2))
                kp = PP[0:GRP].rearrange("p a g n -> p (a g n)")[:, 0:GB * 240].rearrange("p (g n) -> p g n", g=GB)
                for f in range(4):
                    e.wait_ge(m["s5_kp"], f + 1)
                    for s in range(SC):
                        e.dma_start(TZ[s * GRP:(s + 1) * GRP, :, :], kp[:, :, s * GRP:s * GRP + P]).then_inc(m["s5_tz"], 16)

            def dve(self, e):
                self.begin(e)
                n = [0]

                def link(ins):
                    ins.then_inc(m["s5_step"], 1)
                    n[0] += 1
                    e.wait_ge(m["s5_step"], n[0])

                def tt(o, a, b, op):
                    link(nc.vector.tensor_tensor(o, a, b, op))

                def ts(o, a, s1, op0, s2=None, op1=ALU.bypass):
                    link(nc.vector.tensor_scalar(o, a, s1, s2, op0, op1))

                S = [sm[:, j, :] for j in range(20)]
                e.wait_ge(m["s5_ld"], 16 * 6)
                ts(S[9], S[19], 1.4426950408889634, ALU.mult)
                ts(S[9], S[9], MAGIC, ALU.add, -MAGIC, ALU.add)
                ts(S[9], S[9], -127.0, ALU.max, 127.0, ALU.min)
                ts(S[0], S[9], -LN2_PARTS[0], ALU.mult)
                tt(S[0], S[0], S[19], ALU.add)
                ts(S[10], S[9], -LN2_PARTS[1], ALU.mult)
                nc.vector.tensor_tensor(S[0], S[0], S[10], ALU.add).then_inc(m["s5_arg"], 1)
                ts(S[9], S[9], 127.0, ALU.add, 8388608.0, ALU.mult)
                link(nc.vector.tensor_copy(ki[:, :], S[9]))

                def expm1(o, th):
                    ts(S[10], th, -1.0, ALU.mult, 1.0, ALU.add)
                    link(nc.vector.reciprocal(S[10], S[10]))
                    tt(o, th, S[10], ALU.mult)
                    ts(o, o, 2.0, ALU.mult)

                e.wait_ge(m["s5_fun"], 1)
                expm1(S[2], S[1])
                ts(S[2], S[2], 1.0, ALU.add)
                tt(S[2], S[2], ki[:, :].bitcast(F32), ALU.mult)
                e.wait_ge(m["s5_natT"], 1)
                ts(S[3], ps[:, 6, 0:NG], -1e-4, ALU.min)
                link(nc.vector.tensor_copy(S[11], ps[:, 6, NG:2 * NG]))
                nc.vector.tensor_tensor(S[4], S[3], S[2], ALU.mult).then_inc(m["s5_arg"], 1)
                tt(S[6], S[11], S[2], ALU.mult)
                ts(S[9], S[6], 1.0 / TWO_PI, ALU.mult)
                ts(S[9], S[9], MAGIC, ALU.add, -MAGIC, ALU.add)
                for c in PI_PARTS:
                    ts(S[10], S[9], -c, ALU.mult)
                    tt(S[6], S[6], S[10], ALU.add)
                ts(S[6], S[6], 3.1415925, ALU.min, -3.1415925, ALU.max)
                nc.vector.tensor_copy(S[12], S[6]).then_inc(m["s5_arg"], 1)
                e.wait_ge(m["s5_fun"], 2)
                expm1(S[5], S[5])
                ts(S[13], S[5], 1.0, ALU.add)
                e.wait_ge(m["s5_fun"], 4)
                tt(S[9], S[8], S[8], ALU.mult)
                ts(S[9], S[9], -2.0, ALU.mult)
                ts(S[8], S[9], 1.0, ALU.add)
                tt(S[10], S[5], S[8], ALU.mult)
                tt(S[9], S[9], S[10], ALU.add)
                tt(S[10], S[13], S[7], ALU.mult)
                tt(S[14], S[3], S[3], ALU.mult)
                tt(S[15], S[11], S[11], ALU.mult)
                tt(S[14], S[14], S[15], ALU.add)
                link(nc.vector.reciprocal(S[14], S[14]))
                tt(S[15], S[9], S[3], ALU.mult)
                tt(S[16], S[10], S[11], ALU.mult)
                tt(S[15], S[15], S[16], ALU.add)
                tt(S[15], S[15], S[14], ALU.mult)
                tt(S[16], S[10], S[3], ALU.mult)
                tt(S[17], S[9], S[11], ALU.mult)
                tt(S[16], S[16], S[17], ALU.subtract)
                tt(S[16], S[16], S[14], ALU.mult)
                link(nc.vector.memset(PR[:, :, 0:1], 1.0))
                link(nc.vector.memset(PI[:, :, 0:1], 0.0))
                link(nc.vector.tensor_scalar(PR[:, :, 1:2], S[9].unsqueeze(2), 1.0, None, ALU.add))
                link(nc.vector.tensor_copy(PI[:, :, 1:2], S[10].unsqueeze(2)))
                scr = tm[:, 0:NG * 4].rearrange("p (g k) -> p g k", g=NG)

                def cmul(o_r, o_i, x_r, x_i, y_r, y_i, s):
                    tt(o_r, x_r, y_r, ALU.mult)
                    tt(s, x_i, y_i, ALU.mult)
                    tt(o_r, o_r, s, ALU.subtract)
                    tt(o_i, x_r, y_i, ALU.mult)
                    tt(s, x_i, y_r, ALU.mult)
                    tt(o_i, o_i, s, ALU.add)

                for k in (1, 2, 4):
                    bc = lambda x: x[:, :, k:k + 1].to_broadcast([P, NG, k])
                    cmul(PR[:, :, k + 1:2 * k + 1], PI[:, :, k + 1:2 * k + 1], PR[:, :, 1:k + 1], PI[:, :, 1:k + 1],
                         bc(PR), bc(PI), scr[:, :, 0:k])
                for k in range(3):
                    tt(S[13], S[13], S[13], ALU.mult)
                link(nc.vector.tensor_copy(MR[:, 0, :], S[8]))
                link(nc.vector.tensor_copy(MI[:, 0, :], S[7]))
                for k in range(3):
                    tt(S[17], MR[:, 0, :], MI[:, 0, :], ALU.mult)
                    tt(MR[:, 0, :], MR[:, 0, :], MR[:, 0, :], ALU.mult)
                    tt(MI[:, 0, :], MI[:, 0, :], MI[:, 0, :], ALU.mult)
                    tt(MR[:, 0, :], MR[:, 0, :], MI[:, 0, :], ALU.subtract)
                    ts(MI[:, 0, :], S[17], 2.0, ALU.mult)
                for j in range(6):
                    cmul(MR[:, j + 1, :], MI[:, j + 1, :], MR[:, j, :], MI[:, j, :], MR[:, j, :], MI[:, j, :], S[17])

                for f in range(4):
                    gr = slice(f * GB, f * GB + GB)
                    e.wait_ge(m["s5_in"], 256 * (f + 1))
                    q_r = sm[:, 15, gr].unsqueeze(2).to_broadcast([P, GB, GRP])
                    q_i = sm[:, 16, gr].unsqueeze(2).to_broadcast([P, GB, GRP])
                    b1, b2 = bst[:, 0], bst[:, 1]
                    ts(b2, b2, c_sgn, ALU.mult)
                    s1 = tm[:, 0:GB * GRP].rearrange("p (g h) -> p g h", g=GB)
                    tt(BA[:, :, :], b1, q_r, ALU.mult)
                    tt(s1, b2, q_i, ALU.mult)
                    tt(BA[:, :, :], BA[:, :, :], s1, ALU.add)
                    tt(BB[:, :, :], b2, q_r, ALU.mult)
                    tt(s1, b1, q_i, ALU.mult)
                    tt(BB[:, :, :], BB[:, :, :], s1, ALU.subtract)

                    def power_sum(o, lo, cnt, x, y, op, done):
                        pr = PR[:, gr, lo:lo + cnt].unsqueeze(3).to_broadcast([P, GB, cnt, GRP])
                        pi = PI[:, gr, lo:lo + cnt].unsqueeze(3).to_broadcast([P, GB, cnt, GRP])
                        s = tm[:, 0:GB * cnt * GRP].rearrange("p (g k h) -> p g k h", g=GB, k=cnt)
                        tt(o, pr, x.unsqueeze(2).to_broadcast([P, GB, cnt, GRP]), ALU.mult)
                        tt(s, pi, y.unsqueeze(2).to_broadcast([P, GB, cnt, GRP]), ALU.mult)
                        tt(o, o, s, op)
                        e.engine_nop().then_inc(done, 1)

                    power_sum(WT[:, :, :].rearrange("p g (k h) -> p g k h", h=GRP), 0, SC, BA[:, :, :], BB[:, :, :],
                              ALU.add, m["s5_wt"])
                    e.wait_ge(m["s5_cT"], f + 1)
                    cT = lambda k: ps[:, 6, k * P:(k + 1) * P].rearrange("p (g h) -> p g h", h=GRP)
                    ts(C1[:, :, :], cT(0), c_nsgn, ALU.mult)
                    ts(C2[:, :, :], cT(1), -1.0, ALU.mult)
                    power_sum(MM[:, :, :, :], 0, SC + 1, C1[:, :, :], C2[:, :, :], ALU.add, m["s5_mm"])
                    power_sum(M2[:, :, :, :], 1, SC, C2[:, :, :], C1[:, :, :], ALU.subtract, m["s5_m2"])
                    kp = PP[0:GRP].rearrange("p a g n -> p (a g n)")[:, 0:GB * 240].rearrange("p (g n) -> p g n", g=GB)
                    if f:
                        e.wait_ge(m["s5_y"], f)
                    nc.vector.memset(kp[:, :, 0:7 * GRP], 0.0)
                    e.wait_ge(m["s5_k"], f + 1)
                    link(nc.vector.tensor_copy(kp[:, :, 7 * GRP:240],
                                               ps[0:GRP, 2:4, :].rearrange("p b (g n) -> p (b g) n", n=P)))
                    dg = tm[0:GRP, 0:GB * GRP].rearrange("p (g h) -> p g h", g=GB)
                    tt(dg, ident[0:GRP, 0:GRP].unsqueeze(1).to_broadcast([GRP, GB, GRP]),
                       DD[:, gr].unsqueeze(2).to_broadcast([GRP, GB, GRP]), ALU.mult)
                    nc.vector.tensor_tensor(kp[:, :, 7 * GRP:8 * GRP], kp[:, :, 7 * GRP:8 * GRP], dg,
                                            ALU.add).then_inc(m["s5_kp"], 1)
                    link(nc.vector.memset(CT[:, :, 0:1], 1.0))
                    link(nc.vector.memset(SN[:, :, 0:1], 0.0))
                    for j in range(7):
                        w = 1 << j
                        s = tm[:, 0:GB * w].rearrange("p (g k) -> p g k", g=GB)
                        bc = lambda x: x[:, j, gr].unsqueeze(2).to_broadcast([P, GB, w])
                        cmul(CT[:, :, w:2 * w], SN[:, :, w:2 * w], CT[:, :, 0:w], SN[:, :, 0:w], bc(MR), bc(MI), s)
                    e.wait_ge(m["s5_v"], f + 1)
                    v = lambda b: ps[:, b:b + 2, :].rearrange("p b (g n) -> p (b g) n", n=P)
                    s = tm[:, 0:L].rearrange("p (g k) -> p g k", g=GB)
                    tt(zz[:, :, :], CT[:, :, :], v(0), ALU.mult)
                    tt(s, SN[:, :, :], v(2), ALU.mult)
                    tt(zz[:, :, :], zz[:, :, :], s, ALU.add)
                    for g in range(GB):
                        link(nc.vector.tensor_tensor_scan(
                            zz[:, g, :], sm[:, 13, f * GB + g:f * GB + g + 1].to_broadcast([P, NC]), zz[:, g, :],
                            0.0, ALU.mult, ALU.add))
                    e.wait_ge(m["s5_tz"], 128 * (f + 1))
                    link(nc.vector.memset(PP[:, :, :, 0:1], 0.0))
                    tt(PP[:, 0, :, 1:], CT[:, :, :], zz[:, :, :], ALU.mult)
                    nc.vector.tensor_tensor(PP[:, 1, :, 1:], SN[:, :, :], zz[:, :, :], ALU.mult).then_inc(m["s5_p"], 1)
                    e.wait_ge(m["s5_sg"], f + 1)
                    nc.vector.tensor_tensor(YA[:, :], YA[:, :], tm[:, 0:L], ALU.mult).then_inc(m["s5_out"], 1)
                    e.wait_ge(m["s5_out"], f + 1)

            def pe(self, e):
                self.begin(e)
                e.wait_ge(m["s5_ld"], 16 * 6)
                nc.tensor.transpose(ps[:, 6, 0:NG], nat[0:NG, 2, :], ident[0:NG, 0:NG])
                nc.tensor.transpose(ps[:, 6, NG:2 * NG], nat[0:NG, 3, :], ident[0:NG, 0:NG]).then_inc(m["s5_natT"], 1)
                for j in range(2):
                    u = unit_no(self.u + j)
                    w = unit_view(u[0], KT)
                    e.wait_ge(s_lo.sem, upto_unit(u, 1))
                    for s in range(SC):
                        n = 8 * j + s
                        if n >= 4:
                            e.wait_ge(act_a.sem, self.aa + n - 3)
                        mm3(ps[:, n % 4, 0:256], lambda a, k: H[a][:, k, s::SC], lambda b, k: w(b, k, 0, 256), KT,
                            s == 0).then_inc(pe_a.sem, 1)
                e.wait_ge(act_a.sem, self.aa + 16)
                e.wait_ge(m["s5_arg"], 3)
                for f in range(4):
                    e.wait_ge(m["s5_in"], 256 * (f + 1))
                    if f:
                        e.wait_ge(m["s5_ya"], f)
                    for k in range(2):
                        last = nc.tensor.transpose(ps[:, 6, k * P:(k + 1) * P], nat[:, k, :], ident)
                    last.then_inc(m["s5_cT"], 1)
                    e.wait_ge(m["s5_wt"], f + 1)
                    if f:
                        e.wait_ge(m["s5_sg"], f)
                    for g in range(GB):
                        last = nc.tensor.transpose(ps[:, g // 4, (g % 4) * P:(g % 4 + 1) * P], WT[:, g, :], ident)
                    last.then_inc(m["s5_wT"], 1)
                    if f:
                        e.wait_ge(m["s5_g"], f)
                    for g in range(GB):
                        last = nc.tensor.transpose(
                            ps[:, 4 + g // 4, (g % 4) * P:(g % 4 + 1) * P],
                            U[:, f * GB + g, :, :].rearrange("p s h -> p (s h)"), ident)
                    last.then_inc(m["s5_uT"], 1)
                    e.wait_ge(m["s5_mm"], f + 1)
                    for g in range(GB):
                        last = nc.tensor.matmul(
                            ps[0:GRP, 2 + g // 4, (g % 4) * P:(g % 4 + 1) * P], BA[:, g, :],
                            MM[:, g, 0:SC, :].rearrange("p k h -> p (k h)"), start=True, stop=True)
                    last.then_inc(m["s5_k"], 1)
                    e.wait_ge(m["s5_w"], f + 1)
                    e.wait_ge(m["s5_ug"], f + 1)
                    e.wait_ge(m["s5_kp"], f + 1)
                    for k, W in enumerate((W1, W2)):
                        for g in range(GB):
                            last = nc.tensor.matmul(ps[:, 2 * k + g // 4, (g % 4) * P:(g % 4 + 1) * P], W[:, g, :],
                                                    ug[:, g, :], start=True, stop=True)
                    last.then_inc(m["s5_v"], 1)
                    e.wait_ge(m["s5_p"], f + 1)
                    e.wait_ge(m["s5_m2"], f + 1)
                    e.wait_ge(m["s5_tz"], 128 * (f + 1))
                    for g in range(GB):
                        o = ps[:, 4 + g // 4, (g % 4) * P:(g % 4 + 1) * P]
                        nc.tensor.matmul(o, ug[:, g, :], TZ[:, g, :], start=True, stop=False)
                        nc.tensor.matmul(o, PP[:, 0, g, 0:NC], MM[:, g, 1:, :].rearrange("p k h -> p (k h)"),
                                         start=False, stop=False)
                        last = nc.tensor.matmul(o, PP[:, 1, g, 0:NC], M2[:, g, :, :].rearrange("p k h -> p (k h)"),
                                                start=False, stop=True)
                    last.then_inc(m["s5_y"], 1)
                    e.wait_ge(m["s5_g"], f + 1)
                    for t in range(SC):
                        last = nc.tensor.transpose(
                            ps[:, 6 + t // 4, (t % 4) * P:(t % 4 + 1) * P],
                            WT[:, :, :].rearrange("p a b -> p (a b)")[:, t * P:(t + 1) * P], ident)
                    last.then_inc(m["s5_yT"], 1)
                    e.wait_ge(m["s5_ya"], f + 1)
                    for half in range(2):
                        last = nc.tensor.matmul(ps[:, half, :], WG[:, :], YA[:, half * HALF:(half + 1) * HALF],
                                                start=True, stop=True)
                    last.then_inc(m["s5_glu"], 1)

        class Conv(Stage):

            def __init__(self):
                super().__init__()
                self.u = take_units(6)
                self.a, self.aa = pe_a.take(24), act_a.take(8)
                self.d = dv.take(1 + 2 * 14)
                self.out = d_out.take(16)

            def sp(self, e):
                for j in range(2):
                    for k, o in enumerate((O_X, O_C, O_B)):
                        load_unit(e, unit_no(self.u + 3 * j + k), w_cols(A["w_in"][0], 0, o + 256 * j, KT, 256), (KT, 256))

            def act(self, e):
                self.begin(e)
                for j in range(2):
                    split_hi(e, unit_no(self.u + 3 * j + 1))
                    for n in range(4):
                        if j:
                            e.wait_ge(dv.sem, self.d + 1 + 14 * (j - 1) + 7 * (n // 2) + 2)
                        e.wait_ge(pe_a.sem, self.a + 12 * j + n + 1)
                        nc.scalar.activation(cx[:, n // 2, (n % 2) * HALF:(n % 2 + 1) * HALF], ps[:, n, :],
                                             ACT.Copy).then_inc(act_a.sem, 1)
                    split_hi(e, unit_no(self.u + 3 * j + 2))
                    split_hi(e, unit_no(self.u + 3 * j + 3))
                e.wait_ge(dv.sem, self.d + 29)
                e.dma_start(scratch["y_keep"][1], cacc[:, :, :]).then_inc(d_out.sem, 16)

            def pool(self, e):
                for k in range(6):
                    split_lo(e, unit_no(self.u + k + 1))

            def dve(self, e):
                self.begin(e)
                nc.vector.memset(vbuf[:, 0:2], 0.0).then_inc(dv.sem, 1)
                for j in range(2):
                    for q in range(2):
                        f = 2 * j + q
                        d = self.d + 1 + 7 * f
                        for half in range(2):
                            e.wait_ge(act_a.sem, self.aa + 4 * j + 2 * q + half + 1)
                            e.wait_ge(pe_a.sem, self.a + 12 * j + 4 + 2 * q + half + 1)
                            nc.vector.tensor_tensor(vbuf[:, 2 + half * HALF:2 + (half + 1) * HALF],
                                                    cx[:, q, half * HALF:(half + 1) * HALF],
                                                    ps[:, 4 + 2 * q + half, :], ALU.mult).then_inc(dv.sem, 1)
                        e.wait_ge(dv.sem, d + 2)
                        tap = lambda t: vecs[:, V_CW + 4 * t + f:V_CW + 4 * t + f + 1]
                        nc.vector.tensor_scalar(cacc[:, f, :], vbuf[:, 0:L], tap(0), None, ALU.mult).then_inc(dv.sem, 1)
                        for t in (1, 2):
                            e.wait_ge(dv.sem, d + 2 + t)
                            nc.vector.scalar_tensor_tensor(out=cacc[:, f, :], in0=vbuf[:, t:t + L], scalar=tap(t),
                                                           in1=cacc[:, f, :], op0=ALU.mult, op1=ALU.add).then_inc(dv.sem, 1)
                        e.wait_ge(dv.sem, d + 5)
                        for half in range(2):
                            sl = slice(half * HALF, (half + 1) * HALF)
                            e.wait_ge(pe_a.sem, self.a + 12 * j + 8 + 2 * q + half + 1)
                            nc.vector.tensor_tensor(cacc[:, f, sl], cacc[:, f, sl], ps[:, 2 * q + half, :],
                                                    ALU.mult).then_inc(dv.sem, 1)

            def pe(self, e):
                self.begin(e)
                for j in range(2):
                    feature_tiles(e, unit_no(self.u + 3 * j), KT, H, 0,
                                  lambda n: [(dv, self.d + 1 + 14 * (j - 1) + 7 * (n // 2 + 1))] if j else [], pe_a)
                    feature_tiles(e, unit_no(self.u + 3 * j + 1), KT, H, 4, lambda n: [], pe_a)
                    feature_tiles(e, unit_no(self.u + 3 * j + 2), KT, H, 0,
                                  lambda n: [(act_a, self.aa + 4 * j + n + 1)], pe_a)

        class Decay(Stage):

            def __init__(self):
                super().__init__()
                self.u = take_units(1)
                self.a, self.d, self.c = pe_a.take(2), dv.take(6), ac.take(3)

            def sp(self, e):
                load_unit(e, unit_no(self.u), w_cols(A["w_in"][0], 0, O_F, KT, 256), (KT, 256))

            def act(self, e):
                self.begin(e)
                split_hi(e, unit_no(self.u + 1))
                a = PB[0:HEADS, 1, :]
                e.wait_ge(dv.sem, self.d + 1)
                nc.scalar.activation(a, PB[0:HEADS, 0, :], ACT.Abs).then_inc(ac.sem, 1)
                e.wait_ge(ac.sem, self.c + 1)
                nc.scalar.activation(a, a, ACT.Exp, scale=-1.0).then_inc(ac.sem, 1)
                e.wait_ge(ac.sem, self.c + 2)
                nc.scalar.activation(a, a, ACT.Ln, bias=1.0).then_inc(ac.sem, 1)

            def pool(self, e):
                split_lo(e, unit_no(self.u + 1))

            def dve(self, e):
                self.begin(e)
                e.wait_ge(pe_a.sem, self.a + 2)
                z = PB[0:HEADS, 0, :]
                nc.vector.tensor_scalar(z, ps[0:HEADS, 0:2, :].rearrange("p b n -> p (b n)"), bf[0:HEADS, 0:1], None,
                                        ALU.add).then_inc(dv.sem, 1)
                e.wait_ge(ac.sem, self.c + 3)
                nc.vector.tensor_scalar(z, z, 0.0, None, ALU.min).then_inc(dv.sem, 1)
                e.wait_ge(dv.sem, self.d + 2)
                nc.vector.tensor_tensor(z, z, PB[0:HEADS, 1, :], ALU.subtract).then_inc(dv.sem, 1)
                e.wait_ge(dv.sem, self.d + 3)
                nc.vector.tensor_tensor_scan(cum[0:HEADS, :], ones[0:HEADS, 0:1].to_broadcast([HEADS, L]), z, 0.0,
                                             ALU.mult, ALU.add).then_inc(dv.sem, 1)
                e.wait_ge(dv.sem, self.d + 4)
                nc.vector.tensor_scalar(cum[32:32 + HEADS, :], cum[0:HEADS, :], -1.0, None, ALU.mult).then_inc(dv.sem, 1)
                nc.vector.memset(QA[64:66, :, :], 1.0)
                nc.vector.memset(KA[64:66, :, :], 1.0).then_inc(dv.sem, 1)

            def pe(self, e):
                self.begin(e)
                u = unit_no(self.u)
                w = unit_view(u[0], KT)
                e.wait_ge(s_lo.sem, upto_unit(u, 1))
                for half in range(2):
                    mm3(ps[:, half, :], lambda a, k: w(a, k, 0, P),
                        lambda b, k: H[b][:, k, half * HALF:(half + 1) * HALF], KT, half == 0).then_inc(pe_a.sem, 1)

        class Attention(Stage):

            def __init__(self, hg):
                super().__init__()
                self.hg = hg
                self.u = take_units(3)
                self.i = d_in.take(32)
                self.a, self.da = pe_a.take(16 + 32 + 4), dve_a.take(16 + 32 + 4)
                self.b, self.db = pe_b.take(32), dve_b.take(32)
                self.p, self.d, self.c = pe_s.take(32), dv.take(64), ac.take(32)
                if hg:
                    self.out = d_out.take(16)

            def sp(self, e):
                for k, o in enumerate((O_Q, O_K, O_V)):
                    load_unit(e, unit_no(self.u + k), w_cols(A["w_in"][0], 0, o + 256 * self.hg, KT, 256), (KT, 256))

            def act(self, e):
                self.begin(e)
                hs = slice(4 * self.hg, 4 * self.hg + 4)
                e.dma_start(QA[64:65, :, :], cum[hs, :]).then_inc(d_in.sem, 16)
                e.dma_start(KA[65:66, :, :], cum[32 + hs.start:32 + hs.stop, :]).then_inc(d_in.sem, 16)
                for k in range(3):
                    split_hi(e, unit_no(self.u + k + 1))
                for n in range(32):
                    kend = P * (n % 8 + 1)
                    e.wait_ge(dve_a.sem, self.da + 16 + n + 1)
                    if n >= 2:
                        e.wait_ge(pe_b.sem, self.b + n - 1)
                    nc.scalar.activation(PB[:, n % 2, 0:kend],
                                         ps[:, 2 * (n % 2):2 * (n % 2) + 2, :].rearrange("p b n -> p (b n)")[:, 0:kend],
                                         ACT.Exp, bias=mx[:, n:n + 1], accum_out=dn[:, n:n + 1]).then_inc(ac.sem, 1)
                if self.hg:
                    e.wait_ge(dve_a.sem, self.da + 52)
                    e.dma_start(scratch["y_keep"][2], Yc[:, :, :]).then_inc(d_out.sem, 16)

            def pool(self, e):
                for k in range(3):
                    split_lo(e, unit_no(self.u + k + 1))

            def dve(self, e):
                self.begin(e)
                for k, X in enumerate((QA, KA)):
                    for n in range(4):
                        j, half = n // 2, n % 2
                        sl = slice(half * HALF, (half + 1) * HALF)
                        e.wait_ge(pe_a.sem, self.a + 4 * k + n + 1)
                        for hh in range(2):
                            last = nc.vector.tensor_scalar(X[0:HD, 2 * j + hh, sl], ps[HD * hh:HD * hh + HD, n, :],
                                                           0.125 if k == 0 else 1.0, None, ALU.mult)
                        last.then_inc(dve_a.sem, 1)
                for t in range(8):
                    e.wait_ge(pe_a.sem, self.a + 8 + t + 1)
                    nc.vector.tensor_copy(VT[:, t, :], ps[:, t % 4, 0:256]).then_inc(dve_a.sem, 1)

                def top(n):
                    kend = P * (n % 8 + 1)
                    e.wait_ge(pe_a.sem, self.a + 16 + n + 1)
                    nc.vector.tensor_reduce(mx[:, n:n + 1],
                                            ps[:, 2 * (n % 2):2 * (n % 2) + 2, :].rearrange("p b n -> p (b n)")[:, 0:kend],
                                            AX, ALU.max, negate=True).then_inc(dve_a.sem, 1)
                top(0)
                top(1)
                for n in range(32):
                    h, i = n // 8, n % 8
                    kend = P * (i + 1)
                    e.wait_ge(pe_b.sem, self.b + n + 1)
                    if n >= 2:
                        e.wait_ge(pe_s.sem, self.p + n - 1)
                    nc.vector.tensor_copy(PT[:, n % 2, 0:kend], ps[:, 4:6, :].rearrange("p b n -> p (b n)")[:, 0:kend]
                                          ).then_inc(dve_b.sem, 1)
                    if n + 2 < 32:
                        top(n + 2)
                    e.wait_ge(ac.sem, self.c + n + 1)
                    nc.vector.reciprocal(rd[:, n:n + 1], dn[:, n:n + 1]).then_inc(dv.sem, 1)
                    e.wait_ge(dv.sem, self.d + 2 * n + 1)
                    e.wait_ge(pe_s.sem, self.p + n + 1)
                    nc.vector.tensor_scalar(OT[:, i, h * HD:(h + 1) * HD], ps[:, 6 + n % 2, 0:HD], rd[:, n:n + 1], None,
                                            ALU.mult).then_inc(dv.sem, 1)
                for n in range(4):
                    j, ig = n // 2, n % 2
                    e.wait_ge(pe_a.sem, self.a + 48 + n + 1)
                    nc.vector.tensor_copy(Yc[:, 2 * self.hg + j, ig * HALF:(ig + 1) * HALF], ps[:, n, :]
                                          ).then_inc(dve_a.sem, 1)

            def pe(self, e):
                self.begin(e)
                for k in range(2):
                    feature_tiles(e, unit_no(self.u + k), KT, H, 0,
                                  lambda n: [(dve_a, self.da + 4 * (k - 1) + n + 1)] if k else [], pe_a)
                u = unit_no(self.u + 2)
                w = unit_view(u[0], KT)
                e.wait_ge(s_lo.sem, upto_unit(u, 1))
                for t in range(8):
                    e.wait_ge(dve_a.sem, self.da + 4 + t + 1)
                    mm3(ps[:, t % 4, 0:256], lambda a, k: H[a][:, k, t * P:(t + 1) * P], lambda b, k: w(b, k, 0, 256), KT,
                        t == 0).then_inc(pe_a.sem, 1)
                e.wait_ge(dve_a.sem, self.da + 16)
                e.wait_ge(d_in.sem, self.i + 32)

                def logits(n):
                    h, i = n // 8, n % 8
                    kend = P * (i + 1)
                    if n >= 2:
                        e.wait_ge(ac.sem, self.c + n - 1)
                    for lo in range(0, kend, HALF):
                        w_ = min(HALF, kend - lo)
                        diag = lo + w_ == kend
                        last = nc.tensor.matmul(ps[:, 2 * (n % 2) + lo // HALF, 0:w_], QA[0:66, h, i * P:(i + 1) * P],
                                                KA[0:66, h, lo:lo + w_], start=True, stop=not diag)
                        if diag:
                            last = nc.tensor.matmul(ps[:, 2 * (n % 2) + lo // HALF, w_ - P:w_], ident, m_causal,
                                                    start=False, stop=True)
                    last.then_inc(pe_a.sem, 1)
                logits(0)
                logits(1)
                for n in range(32):
                    h, i = n // 8, n % 8
                    e.wait_ge(ac.sem, self.c + n + 1)
                    if n:
                        e.wait_ge(dve_b.sem, self.db + n)
                    for k in range(i + 1):
                        last = nc.tensor.transpose(ps[:, 4 + k // 4, (k % 4) * P:(k % 4 + 1) * P],
                                                   PB[:, n % 2, k * P:(k + 1) * P], ident)
                    last.then_inc(pe_b.sem, 1)
                    if n + 2 < 32:
                        logits(n + 2)
                    e.wait_ge(dve_b.sem, self.db + n + 1)
                    if n >= 2:
                        e.wait_ge(dv.sem, self.d + 2 * (n - 1))
                    for k in range(i + 1):
                        last = nc.tensor.matmul(ps[:, 6 + n % 2, 0:HD], PT[:, n % 2, k * P:(k + 1) * P],
                                                VT[:, k, h * HD:(h + 1) * HD], start=k == 0, stop=k == i)
                    last.then_inc(pe_s.sem, 1)
                e.wait_ge(dv.sem, self.d + 64)
                for n in range(4):
                    j, ig = n // 2, n % 2
                    for k in range(4):
                        last = nc.tensor.transpose(ps[:, n, k * P:(k + 1) * P], OT[:, 4 * ig + k, j * P:(j + 1) * P], ident)
                    last.then_inc(pe_a.sem, 1)

        class Rope(Stage):

            def __init__(self):
                super().__init__()
                self.i, self.d, self.c = d_in.take(16), dv.take(10), ac.take(3)

            def act(self, e):
                self.begin(e)
                e.dma_start(posi, A["positions_2"].partition_broadcast(P)).then_inc(d_in.sem, 16)
                e.wait_ge(dv.sem, self.d + 8)
                nc.scalar.activation(SINR[:, :], ang, ACT.Sin).then_inc(ac.sem, 1)
                nc.scalar.activation(ang2, ang, ACT.Abs).then_inc(ac.sem, 1)
                e.wait_ge(dv.sem, self.d + 9)
                nc.scalar.activation(COSR[:, :], ang2, ACT.Sin).then_inc(ac.sem, 1)

            def dve(self, e):
                self.begin(e)
                n = [0]

                def step(ins):
                    ins.then_inc(dv.sem, 1)
                    n[0] += 1
                    e.wait_ge(dv.sem, self.d + n[0])
                e.wait_ge(d_in.sem, self.i + 16)
                step(nc.vector.tensor_copy(ang, posi))
                step(nc.vector.tensor_scalar(ang, ang, c_freq, None, ALU.mult))
                step(nc.vector.tensor_scalar(ang2, ang, 1.0 / TWO_PI, None, ALU.mult))
                step(nc.vector.tensor_scalar(ang2, ang2, MAGIC, -MAGIC, ALU.add, ALU.add))
                for c in PI_PARTS[:-1]:
                    step(nc.vector.scalar_tensor_tensor(out=ang, in0=ang2, scalar=-c, in1=ang, op0=ALU.mult, op1=ALU.add))
                step(nc.vector.scalar_tensor_tensor(out=ang, in0=ang2, scalar=-PI_PARTS[-1], in1=ang, op0=ALU.mult,
                                                    op1=ALU.add))
                step(nc.vector.tensor_scalar(ang, ang, 3.1415925, -3.1415925, ALU.min, ALU.max))
                e.wait_ge(ac.sem, self.c + 2)
                step(nc.vector.tensor_scalar(ang2, ang2, -1.0, 1.5707963267948966, ALU.mult, ALU.add))
                step(nc.vector.tensor_scalar(SINR[:, :], SINR[:, :], c_rsgn, None, ALU.mult))

        class Dilated(Stage):

            def __init__(self, g, hg, norm=None):
                super().__init__()
                self.norm, self.stored = norm, d_out_pool.n
                self.g, self.hg, self.dil = g, hg, (1, 4, 8)[g]
                self.prev = [(b > 0, b % 2 == 1, False)[g] for b in range(8)]
                self.u = take_units(3)
                self.a, self.da = pe_a.take(16 + 8), dve_a.take(16 + 8)
                self.b, self.db = pe_b.take(8), dve_b.take(8)
                self.p, self.d, self.c = pe_s.take(8), dv.take(32 + 8), ac.take(8)
                d_out_pool.take(16 * 8)

            def sp(self, e):
                for k in range(3):
                    c = O2_QKV + 1536 * k + 512 * self.g + 256 * self.hg
                    load_unit(e, unit_no(self.u + k), w_cols(A["w_in_2"][0], 0, c, KT, 256), (KT, 256))

            def act(self, e):
                self.begin(e, stores=False)
                for k in range(3):
                    split_hi(e, unit_no(self.u + k + 1))
                for b in range(8):
                    lo = 0 if self.prev[b] else P
                    e.wait_ge(dve_a.sem, self.da + 16 + b + 1)
                    if b == 0 and self.stored:
                        e.wait_ge(d_out_pool.sem, self.stored)
                    if b >= 2:
                        e.wait_ge(pe_b.sem, self.b + b - 1)
                    for h in range(4):
                        last = nc.scalar.activation(
                            PB2[:, b % 2, h, lo:256],
                            ps[:, 2 * (b % 2) + h // 2, (h % 2) * 256 + lo:(h % 2 + 1) * 256],
                            ACT.Exp, bias=mx2[:, 4 * b + h:4 * b + h + 1], accum_out=OS[:, b, h, HD:HD + 1])
                    last.then_inc(ac.sem, 1)

            def pool(self, e):
                for k in range(3):
                    split_lo(e, unit_no(self.u + k + 1))
                dst = scratch["dil_keep"][self.g][:, 4 * self.hg:4 * self.hg + 4, :]
                for b in range(8):
                    e.wait_ge(dv.sem, self.d + 32 + b + 1)
                    s, st = ((b * P, 1), (b // 2 + 4 * P * (b % 2), 4), (b, 8))[self.g]
                    e.dma_start(dst[s:s + st * (P - 1) + 1:st], OS[:, b, :, :]).then_inc(d_out_pool.sem, 16)

            def dve(self, e):
                self.begin(e, stores=False)
                dil = self.dil
                for k, X in enumerate((Q2, K2)):
                    for n in range(4):
                        j, half = n // 2, n % 2
                        sl = slice(half * HALF, (half + 1) * HALF)
                        sc = 0.125 if k == 0 else 1.0
                        d = self.d + 4 * (4 * k + n)
                        e.wait_ge(pe_a.sem, self.a + 4 * k + n + 1)
                        nc.vector.stream_shuffle(rp[:, :], ps[:, n, :], list(range(8, 16)) + list(range(8)) + list(range(16, 32))
                                                 ).then_inc(dv.sem, 1)
                        nc.vector.scalar_tensor_tensor(out=rt[:, :], in0=ps[:, n, :], scalar=sc, in1=COSR[:, sl],
                                                       op0=ALU.mult, op1=ALU.mult).then_inc(dv.sem, 1)
                        e.wait_ge(dv.sem, d + 1)
                        nc.vector.scalar_tensor_tensor(out=rp[:, :], in0=rp[:, :], scalar=sc, in1=SINR[:, sl],
                                                       op0=ALU.mult, op1=ALU.mult).then_inc(dv.sem, 1)
                        e.wait_ge(dv.sem, d + 3)
                        for hh in range(2):
                            o = X[:, 2 * j + hh, :].rearrange("p (r l) -> p l r", r=dil)[:, half * HALF // dil:(half + 1) * HALF // dil, :]
                            pr = slice(HD * hh, HD * hh + HD)
                            last = nc.vector.tensor_tensor(o, rt[pr, :].rearrange("p (l r) -> p l r", r=dil),
                                                           rp[pr, :].rearrange("p (l r) -> p l r", r=dil), ALU.add)
                            if hh == 0:
                                last.then_inc(dv.sem, 1)
                        last.then_inc(dve_a.sem, 1)
                        e.wait_ge(dve_a.sem, self.da + 4 * k + n + 1)
                for t in range(8):
                    e.wait_ge(pe_a.sem, self.a + 8 + t + 1)
                    nc.vector.tensor_copy(V2[:, t, :], ps[:, t % 4, 0:256]).then_inc(dve_a.sem, 1)

                def top(b):
                    lo = 0 if self.prev[b] else P
                    e.wait_ge(pe_a.sem, self.a + 16 + b + 1)
                    nc.vector.tensor_reduce(
                        mx2[:, 4 * b:4 * b + 4],
                        ps[:, 2 * (b % 2):2 * (b % 2) + 2, :].rearrange("p b (h n) -> p (b h) n", h=2)[:, :, lo:256],
                        AX, ALU.max, negate=True).then_inc(dve_a.sem, 1)
                top(0)
                top(1)
                for b in range(8):
                    lo = 0 if self.prev[b] else 1
                    e.wait_ge(pe_b.sem, self.b + b + 1)
                    if b >= 2:
                        e.wait_ge(pe_s.sem, self.p + b - 1)
                    nc.vector.tensor_copy(
                        PT2[:, b % 2, :, lo:2, :],
                        ps[:, 4:6, :].rearrange("p b (h c n) -> p (b h) c n", h=2, c=2)[:, :, lo:2, :]).then_inc(dve_b.sem, 1)
                    if b + 2 < 8:
                        top(b + 2)
                    e.wait_ge(ac.sem, self.c + b + 1)
                    nc.vector.tensor_scalar(OS[:, b, :, HD + 1:HD + 2], mx2[:, 4 * b:4 * b + 4].unsqueeze(2), -1.0, None,
                                            ALU.mult)
                    e.wait_ge(pe_s.sem, self.p + b + 1)
                    nc.vector.tensor_copy(OS[:, b, :, 0:HD], ps[:, 6 + b % 2, 0:256].rearrange("p (h n) -> p h n", h=4)
                                          ).then_inc(dv.sem, 1)

            def pe(self, e):
                if self.norm is None:
                    self.begin(e, stores=False)
                else:
                    first_tiles(e, unit_no(self.u), H, lambda n: [], pe_a,
                                lambda k: [e.wait_ge(x.sem, n) for x, n in self.norm.ready(k)])
                for k in range(0 if self.norm is None else 1, 2):
                    feature_tiles(e, unit_no(self.u + k), KT, H, 0,
                                  lambda n: [(dve_a, self.da + 4 * (k - 1) + n + 1)] if k else [], pe_a)
                u = unit_no(self.u + 2)
                w = unit_view(u[0], KT)
                e.wait_ge(s_lo.sem, upto_unit(u, 1))

                def tokens(a, k, b):
                    x = H[a][:, k, :]
                    if self.g == 0:
                        return x[:, b * P:(b + 1) * P]
                    if self.g == 1:
                        s = b // 2 + 4 * P * (b % 2)
                        return x[:, s:s + 4 * (P - 1) + 1:4]
                    return x[:, b:b + 8 * (P - 1) + 1:8]
                for t in range(8):
                    e.wait_ge(dve_a.sem, self.da + 4 + t + 1)
                    mm3(ps[:, t % 4, 0:256], lambda a, k: tokens(a, k, t), lambda b, k: w(b, k, 0, 256), KT,
                        t == 0).then_inc(pe_a.sem, 1)
                e.wait_ge(dve_a.sem, self.da + 16)

                def logits(b):
                    if b >= 2:
                        e.wait_ge(ac.sem, self.c + b - 1)
                    for h in range(4):
                        lo = 0 if self.prev[b] else P
                        o = ps[:, 2 * (b % 2) + h // 2, (h % 2) * 256 + lo:(h % 2 + 1) * 256]
                        mask = m_even if self.g == 2 else m_band[:, lo:256]
                        nc.tensor.matmul(o, ident, mask, start=True, stop=False)
                        last = nc.tensor.matmul(o, Q2[:, h, b * P:(b + 1) * P], K2[:, h, b * P - (P - lo):(b + 1) * P],
                                                start=False, stop=True)
                    last.then_inc(pe_a.sem, 1)
                logits(0)
                logits(1)
                for b in range(8):
                    cs = (0, 1) if self.prev[b] else (1,)
                    e.wait_ge(ac.sem, self.c + b + 1)
                    if b:
                        e.wait_ge(dve_b.sem, self.db + b)
                    for h in range(4):
                        for c in cs:
                            o = (h % 2) * 256 + c * P
                            last = nc.tensor.transpose(ps[:, 4 + h // 2, o:o + P], PB2[:, b % 2, h, c * P:(c + 1) * P], ident)
                    last.then_inc(pe_b.sem, 1)
                    if b + 2 < 8:
                        logits(b + 2)
                    e.wait_ge(dve_b.sem, self.db + b + 1)
                    if b >= 2:
                        e.wait_ge(dv.sem, self.d + 32 + b - 1)
                    for h in range(4):
                        for c in cs:
                            last = nc.tensor.matmul(ps[:, 6 + b % 2, h * HD:(h + 1) * HD], PT2[:, b % 2, h, c, :],
                                                    V2[:, b - 1 + c, h * HD:(h + 1) * HD], start=c == cs[0], stop=c == 1)
                    last.then_inc(pe_s.sem, 1)

        class Combine(Stage):

            def __init__(self):
                super().__init__()
                self.i = (d_in.take(64), d_in2.take(64))
                self.d, self.c = dv.take(8 * 16), ac.take(8)
                self.a, self.da = pe_a.take(8), dve_a.take(8)
                d_out.take(16)

            def act(self, e):
                self.begin(e)
                for t in range(8):
                    if t:
                        e.wait_ge(dv.sem, self.d + 16 * t)
                    e.dma_start(dl[:, :, :, :], scratch["dil_keep"][:, t * P:(t + 1) * P, :, :].rearrange(
                        "g p h n -> p g h n")).then_inc((d_in, d_in2)[t % 2].sem, 16)
                    e.wait_ge(dv.sem, self.d + 16 * t + 5)
                    nc.scalar.activation(cw[:, 1, :], cw[:, 1, :], ACT.Exp).then_inc(ac.sem, 1)
                e.wait_ge(dve_a.sem, self.da + 8)
                e.dma_start(scratch["y_keep"][0], Yd[:, :, :]).then_inc(d_out.sem, 16)

            def dve(self, e):
                self.begin(e)
                n = [0]

                def step(ins):
                    ins.then_inc(dv.sem, 1)
                    n[0] += 1
                    e.wait_ge(dv.sem, self.d + n[0])
                for t in range(8):
                    e.wait_ge((d_in, d_in2)[t % 2].sem, self.i[t % 2] + 16 * (t // 2 + 1))
                    mg = lambda g: dl[:, g, :, HD + 1]
                    M, W_, S_ = cw[:, 0, 0:8], cw[:, 1, :], cw[:, 2, :]
                    step(nc.vector.tensor_tensor(M, mg(0), mg(1), ALU.max))
                    step(nc.vector.tensor_tensor(M, M, mg(2), ALU.max))
                    for g in range(3):
                        step(nc.vector.tensor_tensor(cw[:, 1, 8 * g:8 * g + 8], mg(g), M, ALU.subtract))
                    e.wait_ge(ac.sem, self.c + t + 1)
                    step(nc.vector.tensor_tensor(S_.rearrange("p (g h) -> p g h", g=3), W_.rearrange("p (g h) -> p g h", g=3),
                                                 dl[:, :, :, HD], ALU.mult))
                    step(nc.vector.tensor_tensor(cw[:, 3, 0:8], cw[:, 2, 0:8], cw[:, 2, 8:16], ALU.add))
                    step(nc.vector.tensor_tensor(cw[:, 3, 0:8], cw[:, 3, 0:8], cw[:, 2, 16:24], ALU.add))
                    step(nc.vector.reciprocal(cw[:, 3, 0:8], cw[:, 3, 0:8]))
                    step(nc.vector.tensor_tensor(W_.rearrange("p (g h) -> p g h", g=3), W_.rearrange("p (g h) -> p g h", g=3),
                                                 cw[:, 3, 0:8].unsqueeze(1).to_broadcast([P, 3, 8]), ALU.mult))
                    if t:
                        e.wait_ge(pe_a.sem, self.a + t)
                    o, s = [ct[:, j, :].rearrange("p (h n) -> p h n", h=8) for j in range(2)]
                    wg = lambda g: cw[:, 1, 8 * g:8 * g + 8].unsqueeze(2).to_broadcast([P, 8, HD])
                    step(nc.vector.tensor_tensor(o, dl[:, 0, :, 0:HD], wg(0), ALU.mult))
                    for g in (1, 2):
                        step(nc.vector.tensor_tensor(s, dl[:, g, :, 0:HD], wg(g), ALU.mult))
                        step(nc.vector.tensor_tensor(o, o, s, ALU.add))
                    step(e.engine_nop())
                    assert n[0] == 16 * (t + 1)
                    e.wait_ge(pe_a.sem, self.a + t + 1)
                    nc.vector.tensor_copy(Yd[:, :, t * P:(t + 1) * P], ps[:, t % 4, :].rearrange("p (j n) -> p j n", j=4)
                                          ).then_inc(dve_a.sem, 1)

            def pe(self, e):
                self.begin(e)
                for t in range(8):
                    e.wait_ge(dv.sem, self.d + 16 * (t + 1))
                    if t >= 4:
                        e.wait_ge(dve_a.sem, self.da + t - 3)
                    for j in range(4):
                        last = nc.tensor.transpose(ps[:, t % 4, j * P:(j + 1) * P], ct[:, 0, j * P:(j + 1) * P], ident)
                    last.then_inc(pe_a.sem, 1)

        class Spatial(Stage):

            def __init__(self):
                super().__init__()
                self.u = take_units(4)
                self.i = d_in.take(16 * 11)
                self.a = pe_a.take(8 + 16 + 2 + 8)
                self.aa = act_a.take(8 + 16)
                self.d, self.c = dv.take(1 + 8 * 7 + 1 + 16), ac.take(8)
                d_out.take(16)

            def sp(self, e):
                for j in range(2):
                    load_unit(e, unit_no(self.u + j), w_cols(A["w_in_2"][0], 0, O2_U + 256 * j, KT, 256), (KT, 256))
                for j in range(2):
                    load_unit(e, unit_no(self.u + 2 + j), w_cols(A["w_in_2"][0], 0, O2_V + 256 * j, KT, 256), (KT, 256))

            def act(self, e):
                self.begin(e)
                e.dma_start(wsp[:, :, :], A["w_spatial_2"][0].rearrange("g t s -> t g s")).then_inc(d_in.sem, 16)
                e.dma_start(lng[:, :], A["sgu_ln_g_2"].partition_broadcast(P)).then_inc(d_in.sem, 16)
                e.dma_start(lnb[:, :], A["sgu_ln_b_2"].partition_broadcast(P)).then_inc(d_in.sem, 16)
                for g in range(8):
                    e.dma_start(bsp[64 * (g % 2):64 * (g % 2) + 64, g // 2, :],
                                A["b_spatial_2"][0, g:g + 1, :].partition_broadcast(64)).then_inc(d_in.sem, 16)
                for j in range(2):
                    split_hi(e, unit_no(self.u + j + 1))
                    for n in range(4):
                        e.wait_ge(pe_a.sem, self.a + 4 * j + n + 1)
                        nc.scalar.activation(gu[:, 2 * j + n // 2, (n % 2) * HALF:(n % 2 + 1) * HALF], ps[:, n, :],
                                             ACT.Gelu).then_inc(act_a.sem, 1)
                for j in range(2):
                    split_hi(e, unit_no(self.u + 2 + j + 1))
                    for t in range(8):
                        n = 8 * j + t
                        e.wait_ge(pe_a.sem, self.a + 8 + n + 1)
                        nc.scalar.activation(gv[:, t, 256 * j:256 * j + 256], ps[:, t % 4, 0:256], ACT.Gelu
                                             ).then_inc(act_a.sem, 1)
                for t in range(8):
                    e.wait_ge(dv.sem, self.d + 1 + 7 * t + 3)
                    nc.scalar.activation(mv[:, 2:3], mv[:, 2:3], ACT.Sqrt).then_inc(ac.sem, 1)
                e.wait_ge(dv.sem, self.d + 74)
                e.dma_start(scratch["y_keep"][1], gu[:, :, :]).then_inc(d_out.sem, 16)

            def pool(self, e):
                for k in range(4):
                    split_lo(e, unit_no(self.u + k + 1))

            def dve(self, e):
                self.begin(e)
                e.wait_ge(d_in.sem, self.i + 16 * 11)
                nc.vector.tensor_tensor(wsp[:, :, :], wsp[:, :, :], tril.unsqueeze(1).to_broadcast([P, 8, P]),
                                        ALU.mult).then_inc(dv.sem, 1)
                n = [1]

                def step(ins):
                    ins.then_inc(dv.sem, 1)
                    n[0] += 1
                    e.wait_ge(dv.sem, self.d + n[0])
                for t in range(8):
                    e.wait_ge(act_a.sem, self.aa + 8 + 8 + t + 1)
                    x = gv[:, t, :]
                    step(nc.vector.bn_stats(st6[:, :], x))
                    step(nc.vector.bn_aggr(mv[:, 0:2], st6[:, :]))
                    step(nc.vector.tensor_scalar(mv[:, 2:3], mv[:, 1:2], EPS, None, ALU.add))
                    e.wait_ge(ac.sem, self.c + t + 1)
                    step(nc.vector.reciprocal(mv[:, 3:4], mv[:, 2:3]))
                    step(nc.vector.tensor_scalar(x, x, mv[:, 0:1], mv[:, 3:4], ALU.subtract, ALU.mult))
                    step(nc.vector.tensor_tensor(x, x, lng[:, :], ALU.mult))
                    step(nc.vector.tensor_tensor(x, x, lnb[:, :], ALU.add))
                e.wait_ge(pe_a.sem, self.a + 24 + 2)
                nc.vector.tensor_copy(wspT[:, :, :], ps[:, 4:6, :].rearrange("p b (g n) -> p (b g) n", n=P)
                                      ).then_inc(dv.sem, 1)
                for c in range(8):
                    e.wait_ge(pe_a.sem, self.a + 26 + c + 1)
                    o = gu[:, :, c * P:(c + 1) * P]
                    v = ps[:, c % 4, :].rearrange("p (j n) -> p j n", j=4)
                    tmp = st_tmp[:, c % 2, :, :]
                    nc.vector.tensor_tensor(tmp, v, bsp[:, :, :], ALU.add).then_inc(dv.sem, 1)
                    e.wait_ge(dv.sem, self.d + 58 + 2 * c + 1)
                    nc.vector.tensor_tensor(o, o, tmp, ALU.mult).then_inc(dv.sem, 1)

            def pe(self, e):
                self.begin(e)
                for j in range(2):
                    feature_tiles(e, unit_no(self.u + j), KT, H, 0,
                                  lambda n: [(act_a, self.aa + n + 1)] if j else [], pe_a)
                for j in range(2):
                    u = unit_no(self.u + 2 + j)
                    w = unit_view(u[0], KT)
                    e.wait_ge(s_lo.sem, upto_unit(u, 1))
                    for t in range(8):
                        n = 8 * j + t
                        e.wait_ge(act_a.sem, self.aa + 8 + n - 3)
                        mm3(ps[:, t % 4, 0:256], lambda a, k: H[a][:, k, t * P:(t + 1) * P],
                            lambda b, k: w(b, k, 0, 256), KT, t == 0).then_inc(pe_a.sem, 1)
                e.wait_ge(dv.sem, self.d + 1)
                for g in range(8):
                    last = nc.tensor.transpose(ps[:, 4 + g // 4, (g % 4) * P:(g % 4 + 1) * P], wsp[:, g, :], ident)
                    if g % 4 == 3:
                        last.then_inc(pe_a.sem, 1)
                e.wait_ge(dv.sem, self.d + 58)
                e.wait_ge(act_a.sem, self.aa + 24)
                for c in range(8):
                    if c >= 4:
                        e.wait_ge(dv.sem, self.d + 58 + 2 * (c - 4) + 1)
                    for g in range(8):
                        last = nc.tensor.matmul(ps[64 * (g % 2):64 * (g % 2) + 64, c % 4, (g // 2) * P:(g // 2 + 1) * P],
                                                gv[:, c, g * 64:(g + 1) * 64], wspT[:, g, :], start=True, stop=True)
                    last.then_inc(pe_a.sem, 1)

        w_branch = A["w_branch"][0]
        stages = []

        def add(stage, stores=True):
            if isinstance(stage, S5):
                stage.close()
            else:
                stage.close(stores)
            stages.append(stage)
            return stage

        add(LoadX())
        add(Vectors())
        add(Store0(), False)
        add(Norm(V_NORM))
        add(S5())
        add(Conv())
        add(Decay())
        for hg in range(2):
            add(Attention(hg))
        merge = add(Merge(A["w_in"][0], [O_G + D * b for b in range(3)],
                          [w_branch[512 * b:512 * b + 512] for b in range(3)], V_BG))
        mixed = add(Out(A["w_out"][0], merge, add_x=False))
        norm = add(Norm(V_NORM + 2 * KT, post=V_NORM + KT, x=xr, x_in=mixed.x_in, final=mixed.final, keep=True), False)
        ff = add(FeedForward([A["w_ff1"][0]], A["w_ff2"][0], DFF, norm, onto_x=False, load_x=True))
        norm = add(Norm(V_NORM + 4 * KT, post=V_NORM + 3 * KT, x=xh, x_in=ff.x_in, final=ff.final, bank=0, keep=True))
        add(Rope())
        for g in range(NDIL):
            for hg in range(2):
                add(Dilated(g, hg, norm if g + hg == 0 else None))
        add(Combine())
        add(Spatial())
        merge = add(Merge(A["w_in_2"][0], [O2_GA, O2_GB], [A["w_proj_attn_2"][0], A["w_proj_sgu_2"][0]], None))
        mixed = add(Out(A["w_out_2"][0], merge, add_x=True))
        norm = add(Norm(V_NORM + 5 * KT, final=mixed.final))
        ff = add(FeedForward([A["w_ffn_gate_2"][0], A["w_ffn_up_2"][0]], A["w_ffn_down_2"][0], DFF2, norm, onto_x=True))
        add(Final(ff.final))
        N_UNITS = units[0]

        block = ctx.enter_context(nc.Block())

        @block.sync
        def _(sp):
            sp.dma_start(cst[:, :], A["constants"]).then_inc(d_const.sem, 16)
            for n, name in enumerate(("g_pre_mix", "g_post_mix", "g_pre_mlp", "g_post_mlp", "norm1_g_2", "norm2_g_2",
                                      "final_g_2")):
                v = A[name].rearrange("(k p) -> k p", p=P) if len(A[name].shape) == 1 else A[name][0].rearrange("(k p) -> k p", p=P)
                sp.dma_start(ht[8 * n:8 * n + 8, 0, 0:P], v).then_inc(d_vec.sem, 16)
            sp.dma_start(ht[V_BG:V_BG + 24, 0, 0:P], A["b_gate"][0].rearrange("(k p) -> k p", p=P)).then_inc(d_vec.sem, 16)
            sp.dma_start(ht[V_CW:V_CW + 12, 0, 0:P], A["conv_w"][0].rearrange("t (k p) -> (t k) p", p=P)).then_inc(d_vec.sem, 16)
            sp.dma_start(bf[0:HEADS, :], A["fox_b_f"][0].rearrange("(h a) -> h a", a=1)).then_inc(d_vec.sem, 16)
            for s in stages:
                s.sp(sp)
            sp.wait_ge(d_out.sem, d_out.n)
            sp.wait_ge(d_out_pool.sem, d_out_pool.n)

        @block.scalar
        def _(act):
            split_hi(act, unit_no(0))
            for s in stages:
                s.act(act)

        @block.gpsimd
        def _(pool):
            split_lo(pool, unit_no(0))
            for s in stages:
                s.pool(pool)

        @block.vector
        def _(dve):
            for s in stages:
                s.dve(dve)

        @block.tensor
        def _(pe):
            for s in stages:
                s.pe(pe)


_INS = ["x", "g_pre_mix", "w_in", "b_gate", "s5_a_re", "s5_a_im", "s5_log_dt", "s5_b_re", "s5_b_im", "s5_c_re",
        "s5_c_im", "s5_d", "s5_w_glu", "conv_w", "fox_b_f", "w_branch", "w_out", "g_post_mix", "g_pre_mlp", "w_ff1",
        "w_ff2", "g_post_mlp", "positions_2", "norm1_g_2", "w_in_2", "sgu_ln_g_2", "sgu_ln_b_2", "w_spatial_2",
        "b_spatial_2", "w_proj_attn_2", "w_proj_sgu_2", "w_out_2", "norm2_g_2", "w_ffn_gate_2", "w_ffn_up_2",
        "w_ffn_down_2", "final_g_2"]


def constants():
    import numpy as np
    c = np.zeros((P, 6 * P + 8), np.float32)
    i, j = np.arange(P)[:, None], np.arange(P)[None, :]
    c[:, 0:P] = i == j
    c[:, P:2 * P] = np.where(j < i, -1e30, 0)
    c[:, 2 * P:3 * P] = np.where(j > i, -1e30, 0)
    c[:, 3 * P:4 * P] = np.where((j > i) | ((i - j) % 2 == 1), -1e30, 0)
    c[:, 4 * P:5 * P] = 1
    c[:, 5 * P:6 * P] = j <= i
    dim = np.arange(P) % HD
    inv = np.float32(500000.0) ** (-np.arange(0, 16, 2, dtype=np.float32) / np.float32(16))
    c[:, 6 * P] = np.where(dim < 16, inv[dim % 8], 0)
    c[:, 6 * P + 1] = np.where(dim < 8, -1, 1)
    c[:, 6 * P + 2] = np.where(np.arange(P) < 64, -1, 1)
    c[:, 6 * P + 3] = -c[:, 6 * P + 2]
    return c


def kernel(**inputs):
    import numpy as _np
    import concourse.bacc as _bacc
    from concourse import mybir as _mybir
    from concourse.bass_utils import run_bass_kernel_spmd as _run

    nc = _bacc.Bacc("TRN2", target_bir_lowering=False, num_devices=1)
    arrays, args = {}, {}
    for name in _INS + ["constants"]:
        a = constants() if name == "constants" else _np.ascontiguousarray(inputs[name])
        arrays[f"in_{name}_dram"] = a
        args[name] = nc.dram_tensor(f"in_{name}_dram", a.shape, _mybir.dt.from_np(a.dtype), kind="ExternalInput").ap()
    out = nc.dram_tensor("out_0_dram", (1, L, D), _mybir.dt.float32, kind="ExternalOutput").ap()
    hybrid_kernel(nc, args, out)
    r = _run(nc, [arrays], core_ids=[0])
    return r.results[0]["out_0_dram"]
```

```python
from contextlib import ExitStack

import concourse.bass as bass
from concourse import mybir

F32 = mybir.dt.float32
F32R = mybir.dt.float32r
I32 = mybir.dt.int32
ALU = mybir.AluOpType
ACT = mybir.ActivationFunctionType
AX = mybir.AxisListType.X

P = 128
L = 1024
D = 1024
KT = D // P
HALF = 512
EPS = 1e-6
UNIT = 2048

S5W, GRP, NG, ST = 512, 16, 32, 64
HEADS, HD = 8, 64
AW = HEADS * HD
DFF = 4 * D
O_U, O_X, O_B, O_C = 0, 512, 1024, 1536
O_Q, O_K, O_V, O_F, O_G = 2048, 2560, 3072, 3584, 3592
DFF2 = 2816
NDIL = 3
O2_QKV, O2_U, O2_V, O2_GA, O2_GB = 0, 4608, 5120, 5632, 6656

SC, NC = 8, 128
GB = 8

V_NORM = 0
V_BG = 7 * KT
V_CW = V_BG + 24
V_N = V_CW + 12

TWO_PI = 6.283185307179586
MAGIC = 12582912.0


def split_const(x, parts, bits):
    import math
    out = []
    for _ in range(parts - 1):
        e = math.floor(math.log2(abs(x)))
        q = 2.0 ** (e - bits + 1)
        c = math.floor(x / q) * q
        out.append(c)
        x -= c
    return out + [x]


PI_PARTS = split_const(TWO_PI, 3, 11)
LN2_PARTS = split_const(0.6931471805599453, 2, 12)


class Signal:

    def __init__(self, sem):
        self.sem, self.n = sem, 0

    def take(self, n):
        base = self.n
        self.n += n
        return base


def hybrid_kernel(nc, A, out):
    ctx = ExitStack()
    with ctx:
        def sb(name, shape, dt=F32, at=ctx):
            return at.enter_context(nc.sbuf_tensor(name, shape, dt))

        def sig(name):
            return Signal(ctx.enter_context(nc.semaphore(name)))

        ps = ctx.enter_context(nc.psum_tensor("ps", [P, 8, HALF], F32))
        scratch = {n: nc.dram_tensor(n, s, F32).ap() for n, s in (
            ("x_keep", [P, KT, L]), ("y_keep", [3, P, 4, L]), ("dil_keep", [NDIL, L, HEADS, HD + 2]))}

        cst = sb("cst", [P, 6 * P + 8])
        ident = cst[:, 0:P]
        m_causal = cst[:, 2 * P:3 * P]
        ones = cst[:, 4 * P:5 * P]
        tril = cst[:, 5 * P:6 * P]
        c_freq = cst[:, 6 * P:6 * P + 1]
        c_rsgn = cst[:, 6 * P + 1:6 * P + 2]
        c_sgn = cst[:, 6 * P + 2:6 * P + 3]
        c_nsgn = cst[:, 6 * P + 3:6 * P + 4]
        vecs = sb("vecs", [P, V_N])
        rstd = sb("rstd", [P, 8])
        diag = sb("diag", [P, L])
        bf = sb("bf", [P, 1])

        raw = [sb(f"raw{j}", [P, UNIT]) for j in range(2)]
        whi = [sb(f"whi{j}", [P, UNIT], F32R) for j in range(2)]
        wlo = [sb(f"wlo{j}", [P, UNIT], F32R) for j in range(2)]
        h_hi = sb("h_hi", [P, KT, L], F32R)
        with ExitStack() as at_low:
            xh = sb("xh", [P, KT, L], F32, at_low)
        h_lo = sb("h_lo", [P, KT, L], F32R)
        H = (h_hi, h_lo)

        def phase(items):
            at = ExitStack()
            made = [sb(n, s, d, at) for n, s, d in items]
            at.close()
            return made

        (U, ug, WT, W1, W2, MM, M2, TZ, CT, SN, tm, zz, PP, YA, WG, BA, BB, C1, C2, PR, PI, MR, MI,
         sm, ki, nat, DD, bst) = phase([
            ("U", [P, NG, SC, GRP], F32), ("ug", [P, GB, P], F32), ("WT", [P, GB, SC * GRP], F32),
            ("W1", [P, GB, P], F32), ("W2", [P, GB, P], F32), ("MM", [P, GB, SC + 1, GRP], F32),
            ("M2", [P, GB, SC, GRP], F32), ("TZ", [P, GB, P], F32), ("CT", [P, GB, NC], F32),
            ("SN", [P, GB, NC], F32), ("tm", [P, GB * (SC + 1) * GRP], F32), ("zz", [P, GB, NC], F32),
            ("PP", [P, 2, GB, NC + 1], F32), ("YA", [P, L], F32), ("WG", [P, P], F32),
            ("BA", [P, GB, GRP], F32), ("BB", [P, GB, GRP], F32), ("C1", [P, GB, GRP], F32),
            ("C2", [P, GB, GRP], F32), ("PR", [P, NG, SC + 1], F32), ("PI", [P, NG, SC + 1], F32),
            ("MR", [P, 8, NG], F32), ("MI", [P, 8, NG], F32), ("sm", [P, 20, NG], F32),
            ("ki", [P, NG], I32), ("nat", [P, 4, P], F32), ("DD", [GRP, NG], F32),
            ("bst", [P, 2, GB, GRP], F32)])
        (QA, KA, VT, PB, PT, OT, cum, Yc, mx, dn, rd) = phase([
            ("QA", [P, 4, L], F32), ("KA", [P, 4, L], F32), ("VT", [P, 8, 256], F32),
            ("PB", [P, 2, L], F32), ("PT", [P, 2, L], F32), ("OT", [P, 8, 256], F32),
            ("cum", [P, L], F32), ("Yc", [P, 4, L], F32),
            ("mx", [P, 64], F32), ("dn", [P, 64], F32), ("rd", [P, 64], F32)])
        (cx, vbuf, cacc) = phase([
            ("cx", [P, 2, L], F32), ("vbuf", [P, L + 2], F32), ("cacc", [P, 4, L], F32)])
        at_big = ExitStack()
        big = sb("big", [P, KT, L], F32, at_big)
        (y_hi, y_lo, yt, gate, bcur) = phase([
            ("y_hi", [P, 4, L], F32R), ("y_lo", [P, 4, L], F32R),
            ("yt", [P, 2, L], F32), ("gate", [P, 4, HALF], F32), ("bcur", [P, 2], F32)])
        (xr, sq, ht) = phase([
            ("xr", [P, KT, L], F32), ("sq", [P, 3, L], F32), ("ht", [P, 2, L], F32)])
        (f_hi, f_lo, fr, fv) = phase([
            ("f_hi", [P, 2, 2, L], F32R), ("f_lo", [P, 2, 2, L], F32R),
            ("fr", [P, 4, HALF], F32), ("fv", [P, 2, HALF], F32)])
        at_big.close()
        (COSR, SINR, Q2, K2, V2, rt, rp, PB2, PT2, OS, mx2, mask_r) = phase([
            ("COSR", [P, L], F32), ("SINR", [P, L], F32), ("Q2", [64, 4, L], F32), ("K2", [64, 4, L], F32),
            ("V2", [P, 8, 256], F32), ("rt", [P, HALF], F32), ("rp", [P, HALF], F32),
            ("PB2", [P, 2, 4, 256], F32), ("PT2", [P, 2, 4, 2, P], F32), ("OS", [P, 8, 4, HD + 2], F32),
            ("mx2", [P, 32], F32), ("mask_r", [P, 4 * P], F32R)])
        ident_r, band_r, even_r = mask_r[:, 0:P], mask_r[:, P:3 * P], mask_r[:, 3 * P:4 * P]
        ang = PB2[:, 0].rearrange("p h n -> p (h n)")
        ang2 = PB2[:, 1].rearrange("p h n -> p (h n)")
        posi = V2[:, 0:4].rearrange("p t n -> p (t n)").bitcast(I32)
        (Yd, dl, cw, ct, gu, gv, wsp, wspT, lng, lnb, bsp, st6, mv, st_tmp) = phase([
            ("Yd", [P, 4, L], F32), ("dl", [P, 2, 3, HEADS, HD + 2], F32), ("cw", [P, 4, 3 * HEADS], F32),
            ("ct", [P, 3, AW], F32), ("gu", [P, 4, L], F32), ("gv", [P, 8, 512], F32), ("wsp", [P, 8, P], F32),
            ("wspT", [P, 8, P], F32), ("lng", [P, 512], F32), ("lnb", [P, 512], F32), ("bsp", [P, 4, P], F32),
            ("st6", [P, 6], F32), ("mv", [P, 8, 4], F32), ("st_tmp", [P, 2, 4, P], F32)])
        ld = [sig(f"unit_loaded{j}") for j in range(2)]
        s_hi, s_lo, s_begun = sig("unit_hi_ready"), sig("unit_lo_ready"), sig("unit_begun")
        pe_a, pe_b = sig("pe_tile_a"), sig("pe_tile_b")
        dve_a, dve_b, act_a = sig("dve_took_a"), sig("dve_took_b"), sig("act_took_a")
        dv, ac, po, pe_s = sig("dve_step"), sig("act_step"), sig("pool_step"), sig("pe_step")
        d_in, d_in2, d_tab = sig("loaded"), sig("loaded_more"), sig("tables_loaded")
        d_out, d_out_pool = sig("stored"), sig("stored_by_gpsimd")
        d_const, d_vec = sig("constants_loaded"), sig("vectors_loaded")


        def unit_no(c, i=None, per=2):
            return c, i, per

        def upto_unit(u, off):
            c, i, per = u
            return c + off if i is None else per * i + (c + off)

        def load_unit(sp, u, src, shape):
            c, i, per = u
            if c >= 2:
                sp.wait_ge(s_lo.sem, upto_unit(u, -1))
            k, n = shape
            sp.dma_start(raw[c % 2][:, 0:k * n].rearrange("p (k n) -> p k n", k=k), src).then_inc(ld[c % 2].sem, 16)

        def split_hi(act, u, early=False):
            c, i, per = u
            if i is None and (c >= N_UNITS or (c in early_units and not early)):
                return
            half = 16 * (c // 2 + 1)
            act.wait_ge(ld[c % 2].sem, half if i is None else 8 * per * i + half)
            if c >= 2:
                act.wait_ge(s_begun.sem, upto_unit(u, 0))
            nc.scalar.activation(whi[c % 2][:, :], raw[c % 2][:, :], ACT.Copy).then_inc(s_hi.sem, 1)

        def split_lo(pool, u):
            c, i, per = u
            if c >= N_UNITS and i is None:
                return
            pool.wait_ge(s_hi.sem, upto_unit(u, 1))
            nc.gpsimd.tensor_tensor(wlo[c % 2][:, :], raw[c % 2][:, :], whi[c % 2][:, :].bitcast(F32),
                                    ALU.subtract).then_inc(s_lo.sem, 1)

        def mm3(out_, lhs, rhs, ks, begins=False):
            for k in range(ks):
                for n, (a, b) in enumerate(((0, 0), (0, 1), (1, 0))):
                    last = nc.tensor.matmul(out_, lhs(a, k), rhs(b, k), start=(k == 0 and n == 0),
                                            stop=(k == ks - 1 and n == 2))
                    if begins and k == 0 and n == 0:
                        last.then_inc(s_begun.sem, 1)
            return last

        def unit_view(c, ks):
            cols = 1024 if ks == 4 else UNIT
            hi_lo = [w[c % 2][:, 0:cols].rearrange("p (k n) -> p k n", k=ks) for w in (whi, wlo)]
            return lambda a, k, lo, n: hi_lo[a][:, k, lo:lo + n]

        def feature_tiles(pe, u, ks, src, bank, waits, ready, after=lambda n: None):
            w = unit_view(u[0], ks)
            pe.wait_ge(s_lo.sem, upto_unit(u, 1))
            for n in range(4):
                m, half = n // 2, n % 2
                for s, v in waits(n):
                    pe.wait_ge(s.sem, v)
                mm3(ps[:, bank + n, :], lambda a, k: w(a, k, m * P, P),
                    lambda b, k: src[b][:, k, half * HALF:(half + 1) * HALF], ks, n == 0).then_inc(ready.sem, 1)
                after(n)

        def first_tiles(pe, u, src, waits, ready, kwait):
            w = unit_view(u[0], KT)
            pe.wait_ge(s_lo.sem, upto_unit(u, 1))
            for n in range(4):
                for s, v in waits(n):
                    pe.wait_ge(s.sem, v)
            for k in range(KT):
                kwait(k)
                for n in range(4):
                    m, half = n // 2, n % 2
                    for q, (a, b) in enumerate(((0, 0), (0, 1), (1, 0))):
                        last = nc.tensor.matmul(ps[:, n, :], w(a, k, m * P, P),
                                                src[b][:, k, half * HALF:(half + 1) * HALF],
                                                start=(k == 0 and q == 0), stop=(k == KT - 1 and q == 2))
                        if k == 0 and n == 0 and q == 0:
                            last.then_inc(s_begun.sem, 1)
                    if k == KT - 1:
                        last.then_inc(ready.sem, 1)

        compute_signals = [pe_a, pe_b, dve_a, dve_b, act_a, dv, ac, po, pe_s, d_in, d_in2, d_tab]
        marks = [{}, {}]

        class Stage:

            def __init__(self):
                self.after = [(x, n) for x, n in marks[-1].items() if n and marks[-2].get(x, 0) != n]

            def close(self, stores=True):
                marks.append({x: x.n for x in compute_signals + ([d_out, d_out_pool] if stores else [])})

            def begin(self, e, stores=True):
                for x, n in self.after:
                    if stores or x not in (d_out, d_out_pool):
                        e.wait_ge(x.sem, n)

            def sp(self, e): pass
            def act(self, e): pass
            def pool(self, e): pass
            def dve(self, e): pass
            def pe(self, e): pass

        units, early_units = [0], []

        def take_units(n):
            b = units[0]
            units[0] += n
            return b

        class LoadX(Stage):

            def __init__(self):
                super().__init__()
                self.a, self.da = pe_a.take(16), dve_a.take(16)
                self.i = (d_in.take(64), d_in2.take(64))

            def act(self, e):
                for t in range(8):
                    if t >= 2:
                        e.wait_ge(pe_a.sem, self.a + 2 * (t - 1))
                    e.dma_start(sq[:, t % 2, :], A["x"][0, t * P:(t + 1) * P, :]).then_inc((d_in, d_in2)[t % 2].sem, 16)

            def pe(self, e):
                e.wait_ge(d_const.sem, 16)
                for t in range(8):
                    e.wait_ge((d_in, d_in2)[t % 2].sem, self.i[t % 2] + 16 * (t // 2 + 1))
                    for q in range(2):
                        n = 2 * t + q
                        if n >= 4:
                            e.wait_ge(dve_a.sem, self.da + n - 3)
                        for j in range(4):
                            k = 4 * q + j
                            last = nc.tensor.transpose(ps[:, n % 4, j * P:(j + 1) * P],
                                                       sq[:, t % 2, k * P:(k + 1) * P], ident)
                        last.then_inc(pe_a.sem, 1)

            def dve(self, e):
                for n in range(16):
                    t, q = n // 2, n % 2
                    e.wait_ge(pe_a.sem, self.a + n + 1)
                    nc.vector.tensor_copy(big[:, 4 * q:4 * q + 4, t * P:(t + 1) * P],
                                          ps[:, n % 4, :].rearrange("p (k t) -> p k t", k=4)).then_inc(dve_a.sem, 1)

        class Vectors(Stage):

            def __init__(self):
                super().__init__()
                self.p, self.d = pe_s.take(1), dv.take(1)

            def pe(self, e):
                self.begin(e)
                e.wait_ge(d_vec.sem, 16 * 10)
                nc.tensor.transpose(ps[:, 4, 0:V_N], ht[0:V_N, 0, 0:P], ident[0:V_N, 0:V_N]).then_inc(pe_s.sem, 1)

            def dve(self, e):
                e.wait_ge(pe_s.sem, self.p + 1)
                nc.vector.tensor_copy(vecs[:, :], ps[:, 4, 0:V_N]).then_inc(dv.sem, 1)

        class Rstd:

            spread = ps[:, 6:8, :].rearrange("p b n -> p (b n)")

            def __init__(self, bank, maker=None):
                self.bank, self.maker = bank, maker
                if maker is not None:
                    maker.sums = self
                    self.s = dv.take(KT)
                self.ks = KT + 1 if maker is None else 1
                self.a, self.d, self.p = ac.take(9), dv.take(4), pe_s.take(self.ks + 2)

            def add_square(self, e, k):
                e.wait_ge(ac.sem, self.a + k + 1)
                if k == 0:
                    nc.vector.tensor_copy(ht[:, 0, :], sq[:, 0, :]).then_inc(dv.sem, 1)
                else:
                    e.wait_ge(dv.sem, self.s + k)
                    nc.vector.tensor_tensor(ht[:, 0, :], ht[:, 0, :], sq[:, k % 3, :], ALU.add).then_inc(dv.sem, 1)

            def act(self, e, final):
                for k in range(KT):
                    for x, n in final(k):
                        e.wait_ge(x.sem, n)
                    if k >= 3:
                        if self.maker is None:
                            e.wait_ge(pe_s.sem, self.p + k - 2)
                        else:
                            e.wait_ge(dv.sem, self.s + k - 2)
                    nc.scalar.activation(sq[:, k % 3, :], big[:, k, :], ACT.Square).then_inc(ac.sem, 1)
                if self.maker is None:
                    e.wait_ge(pe_s.sem, self.p + self.ks)
                    nc.scalar.activation(rstd[:, :], ps[:, self.bank, 0:8], ACT.Sqrt).then_inc(ac.sem, 1)
                else:
                    e.wait_ge(dv.sem, self.d + 1)
                    nc.scalar.activation(rstd[:, :], rstd[:, :], ACT.Sqrt).then_inc(ac.sem, 1)

            def dve(self, e):
                if self.maker is None:
                    e.wait_ge(pe_s.sem, self.p + KT)
                    nc.vector.tensor_scalar(diag[0:1, :], ps[0:1, self.bank:self.bank + 2, :].rearrange("p b n -> p (b n)"),
                                            1.0 / D, EPS, ALU.mult, ALU.add).then_inc(dv.sem, 1)
                else:
                    e.wait_ge(pe_s.sem, self.p + self.ks)
                    nc.vector.tensor_scalar(rstd[:, :], ps[:, self.bank, 0:8], 1.0 / D, EPS, ALU.mult, ALU.add
                                            ).then_inc(dv.sem, 1)
                e.wait_ge(ac.sem, self.a + 9)
                nc.vector.reciprocal(rstd[:, :], rstd[:, :]).then_inc(dv.sem, 1)
                e.wait_ge(dv.sem, self.d + 2)
                for half in range(2):
                    nc.vector.tensor_tensor(
                        diag[:, half * HALF:(half + 1) * HALF].rearrange("p (t n) -> p t n", t=4),
                        ident.unsqueeze(1).to_broadcast([P, 4, P]),
                        rstd[:, 4 * half:4 * half + 4].unsqueeze(2).to_broadcast([P, 4, P]), ALU.mult).then_inc(dv.sem, 1)
                e.wait_ge(pe_s.sem, self.p + self.ks + 2)

            def pe(self, e):
                if self.maker is None:
                    for k in range(KT):
                        e.wait_ge(ac.sem, self.a + k + 1)
                        for half in range(2):
                            last = nc.tensor.matmul(ps[:, self.bank + half, :], ones,
                                                    sq[:, k % 3, half * HALF:(half + 1) * HALF],
                                                    start=k == 0, stop=k == KT - 1)
                        last.then_inc(pe_s.sem, 1)
                    e.wait_ge(dv.sem, self.d + 1)
                else:
                    e.wait_ge(dv.sem, self.s + KT)
                for t in range(8):
                    x, one = (diag[0:1, :], ones[0:1, 0:1]) if self.maker is None else (ht[:, 0, :], ones[:, 0:1])
                    last = nc.tensor.matmul(ps[:, self.bank, t:t + 1], x[:, t * P:(t + 1) * P], one, start=True, stop=True)
                last.then_inc(pe_s.sem, 1)
                for half in range(2):
                    e.wait_ge(dv.sem, self.d + 3 + half)
                    nc.tensor.matmul(ps[:, 6 + half, :], ones, diag[:, half * HALF:(half + 1) * HALF],
                                     start=True, stop=True).then_inc(pe_s.sem, 1)

        def vec(row, k):
            return vecs[:, row + k:row + k + 1]

        def after_a(k):
            return max(2 * k, 1)

        def after_b(k):
            return min(2 * k + 3, 2 * KT)

        def in_pairs(a, b):
            for k in range(KT):
                a(k)
                if k:
                    b(k - 1)
            b(KT - 1)

        class Norm(Stage):

            def __init__(self, row, post=None, x=None, x_in=None, maker=None, bank=4, keep=False):
                super().__init__()
                self.row, self.post, self.x, self.x_in, self.keep = row, post, x, x_in, keep
                self.final = maker.final if maker is not None else None
                if post is not None:
                    self.r0, self.d0 = Rstd(bank, maker), dv.take(16)
                self.r = Rstd(4, maker if post is None else None)
                self.a, self.d = ac.take(8), dv.take(16)
                early_units.append(units[0] + 1)
                self.next_unit = units[0]
                if keep:
                    d_out.take(16)

            def ready(self, k):
                return [(dv, self.d + after_b(k))]

            def act(self, e):
                if self.final is None:
                    self.begin(e)
                final = self.final or (lambda k: [])
                if self.post is not None:
                    self.r0.act(e, final)
                    final = lambda k: [(dv, self.d0 + after_b(k))]
                self.r.act(e, final)
                if self.keep:
                    e.dma_start(scratch["x_keep"], big[:, :, :]).then_inc(d_out.sem, 16)
                for k in range(KT):
                    e.wait_ge(dv.sem, self.d + after_a(k))
                    nc.scalar.activation(h_hi[:, k, :], ht[:, k % 2, :], ACT.Copy).then_inc(ac.sem, 1)
                    if k == 4:
                        split_hi(e, unit_no(self.next_unit + 1), early=True)

            def dve(self, e):
                if self.final is None:
                    self.begin(e)
                if self.post is not None:
                    self.r0.dve(e)
                    e.wait_ge(d_in.sem, self.x_in + 16)

                    def scale(k):
                        nc.vector.scalar_tensor_tensor(out=big[:, k, :], in0=big[:, k, :], scalar=vec(self.post, k),
                                                       in1=Rstd.spread, op0=ALU.mult, op1=ALU.mult).then_inc(dv.sem, 1)

                    def add_x(k):
                        e.wait_ge(dv.sem, self.d0 + after_a(k))
                        nc.vector.tensor_tensor(big[:, k, :], big[:, k, :], self.x[:, k, :], ALU.add).then_inc(dv.sem, 1)
                    in_pairs(scale, add_x)
                self.r.dve(e)

                def normed(k):
                    if k >= 2:
                        e.wait_ge(dv.sem, self.d + after_b(k - 2))
                    nc.vector.scalar_tensor_tensor(out=ht[:, k % 2, :], in0=big[:, k, :], scalar=vec(self.row, k),
                                                   in1=Rstd.spread, op0=ALU.mult, op1=ALU.mult).then_inc(dv.sem, 1)

                def low(k):
                    e.wait_ge(ac.sem, self.a + k + 1)
                    nc.vector.tensor_tensor(h_lo[:, k, :], ht[:, k % 2, :], h_hi[:, k, :].bitcast(F32),
                                            ALU.subtract).then_inc(dv.sem, 1)
                in_pairs(normed, low)

            def pe(self, e):
                if self.final is None:
                    self.begin(e)
                if self.post is not None:
                    self.r0.pe(e)
                self.r.pe(e)

        class Store0(Stage):

            def __init__(self):
                super().__init__()
                d_out.take(16)

            def act(self, e):
                self.begin(e)
                e.dma_start(scratch["x_keep"], big[:, :, :]).then_inc(d_out.sem, 16)

        class Final(Stage):

            def __init__(self, maker):
                super().__init__()
                self.final, self.r = maker.final, Rstd(0, maker)
                self.d, self.a, self.aa, self.da = dv.take(8), pe_a.take(16), act_a.take(8), dve_a.take(8)
                d_out.take(16 * 8)

            def act(self, e):
                self.r.act(e, self.final)
                for t in range(8):
                    e.wait_ge(pe_a.sem, self.a + t + 1)
                    nc.scalar.activation(xr[:, t, 0:HALF], ps[:, 4 + t % 2, :], ACT.Copy).then_inc(act_a.sem, 1)
                for t in range(8):
                    e.wait_ge(act_a.sem, self.aa + t + 1)
                    e.wait_ge(dve_a.sem, self.da + t + 1)
                    e.dma_start(out[0, t * P:(t + 1) * P, :], xr[:, t, :]).then_inc(d_out.sem, 16)

            def dve(self, e):
                self.r.dve(e)
                for k in range(KT):
                    nc.vector.scalar_tensor_tensor(out=big[:, k, :], in0=big[:, k, :], scalar=vec(V_NORM + 6 * KT, k),
                                                   in1=Rstd.spread, op0=ALU.mult, op1=ALU.mult).then_inc(dv.sem, 1)
                for t in range(8):
                    e.wait_ge(pe_a.sem, self.a + 8 + t + 1)
                    nc.vector.tensor_copy(xr[:, t, HALF:D], ps[:, t % 4, :]).then_inc(dve_a.sem, 1)

            def pe(self, e):
                self.r.pe(e)
                for q in range(2):
                    e.wait_ge(dv.sem, self.d + 4 * q + 4)
                    for t in range(8):
                        bank = 4 + t % 2 if q == 0 else t % 4
                        if q == 0 and t >= 2:
                            e.wait_ge(act_a.sem, self.aa + t - 1)
                        if q == 1 and t >= 4:
                            e.wait_ge(dve_a.sem, self.da + t - 3)
                        for j in range(4):
                            last = nc.tensor.transpose(ps[:, bank, j * P:(j + 1) * P],
                                                       big[:, 4 * q + j, t * P:(t + 1) * P], ident)
                        last.then_inc(pe_a.sem, 1)

        class Out(Stage):

            def __init__(self, w, merge, add_x):
                super().__init__()
                self.w, self.merge, self.add_x = w, merge, add_x
                self.u, self.a, self.da = take_units(4), pe_a.take(16), dve_a.take(16)
                self.ac, self.d, self.x_in = ac.take(8), dv.take(8), d_in.take(16)

            def final(self, k):
                return [(dve_a, self.da + 2 * k + 2)]

            def sp(self, e):
                for j in range(4):
                    load_unit(e, unit_no(self.u + j), w_cols(self.w, 0, 256 * j, KT, 256), (KT, 256))

            def act(self, e):
                e.wait_ge(pe_a.sem, self.a)
                for k in range(KT):
                    e.wait_ge(dv.sem, self.merge.final(k))
                    nc.scalar.activation(h_hi[:, k, :], big[:, k, :], ACT.Copy).then_inc(ac.sem, 1)
                e.wait_ge(pe_b.sem, self.merge.b + 16 * self.merge.nb)
                e.dma_start(xr[:, :, :], scratch["x_keep"]).then_inc(d_in.sem, 16)
                with e.Fori(0, 2) as i:
                    for j in range(2):
                        split_hi(e, unit_no(self.u + 1 + j, i))

            def pool(self, e):
                with e.Fori(0, 2) as i:
                    for j in range(2):
                        split_lo(e, unit_no(self.u + 1 + j, i))

            def dve(self, e):
                for k in range(KT):
                    e.wait_ge(ac.sem, self.ac + k + 1)
                    nc.vector.tensor_tensor(h_lo[:, k, :], big[:, k, :], h_hi[:, k, :].bitcast(F32),
                                            ALU.subtract).then_inc(dv.sem, 1)
                e.wait_ge(dv.sem, self.d + 8)
                if self.add_x:
                    e.wait_ge(d_in.sem, self.x_in + 16)
                for n in range(16):
                    e.wait_ge(pe_a.sem, self.a + n + 1)
                    half = slice((n % 2) * HALF, (n % 2 + 1) * HALF)
                    if self.add_x:
                        nc.vector.tensor_tensor(big[:, n // 2, half], ps[:, n % 4, :], xr[:, n // 2, half], ALU.add
                                                ).then_inc(dve_a.sem, 1)
                    else:
                        nc.vector.tensor_copy(big[:, n // 2, half], ps[:, n % 4, :]).then_inc(dve_a.sem, 1)
                    for k in {13: (0, 1, 2), 14: (3, 4, 5), 15: (6, 7)}.get(n, ()):
                        self.sums.add_square(e, k)

            def pe(self, e):
                first_tiles(e, unit_no(self.u), H, lambda n: [], pe_a,
                            lambda k: e.wait_ge(dv.sem, self.d + k + 1))
                for j in range(1, 4):
                    feature_tiles(e, unit_no(self.u + j), KT, H, 0,
                                  lambda n: [(dve_a, self.da + 4 * j + n - 3)], pe_a)

        def w_cols(w, row0, col0, ks, n):
            return w[row0:row0 + ks * P, col0:col0 + n].rearrange("(k p) n -> p k n", p=P)

        class Merge(Stage):

            def __init__(self, w_in, gate_col, w_branch, bias):
                super().__init__()
                self.w_in, self.gate_col, self.wb, self.bias = w_in, gate_col, w_branch, bias
                nb = self.nb = len(w_branch)
                self.u = take_units(8 * nb)
                self.a, self.b = pe_a.take(16 * nb), pe_b.take(16 * nb)
                self.aa = act_a.take(16 * nb)
                self.d = [dv.take(16 if b == 0 else 32) for b in range(nb)]
                self.per = 4 if bias is None else 8
                self.ac, self.lo = ac.take(self.per * nb), dve_a.take(4 * nb)
                self.i = (d_in.take(32 * nb), d_in2.take(32 * nb))

            def final(self, k):
                return self.d[-1] + 4 * (k + 1)

            def taken(self, b, i, n):
                if b == 0:
                    return 4 * i + (self.d[0] + n - 3)
                return 8 * i + (self.d[b] + (n - 3 if b == 1 else 2 * n - 6))

            def sp(self, e):
                for b in range(self.nb):
                    for i in range(4):
                        u = self.u + 8 * b + 2 * i
                        load_unit(e, unit_no(u), w_cols(self.w_in, 0, self.gate_col[b] + 256 * i, KT, 256), (KT, 256))
                        load_unit(e, unit_no(u + 1), w_cols(self.wb[b], 0, 256 * i, 4, 256), (4, 256))

            def act(self, e):
                self.begin(e)
                for b in range(self.nb):
                    for k in range(4):
                        n = 4 * b + k
                        if n >= 2:
                            e.wait_ge(dve_a.sem, self.lo + n - 1)
                        e.dma_start(yt[:, k % 2, :], scratch["y_keep"][b, :, k, :]).then_inc((d_in, d_in2)[k % 2].sem, 16)
                        if k == 0:
                            continue
                        if k == 1 and b:
                            e.wait_ge(pe_b.sem, self.b + 16 * b)
                        for kk in (0, 1) if k == 1 else (k,):
                            e.wait_ge((d_in, d_in2)[kk % 2].sem, self.i[kk % 2] + 16 * ((4 * b + kk) // 2 + 1))
                            nc.scalar.activation(y_hi[:, kk, :], yt[:, kk % 2, :], ACT.Copy).then_inc(ac.sem, 1)
                    with e.Fori(0, 4) as i:
                        if self.bias is not None:
                            e.wait_ge(act_a.sem, 4 * i + (self.aa + 16 * b))
                            nc.scalar.activation(bcur[:, :], vecs[:, bass.ds(2 * i + (self.bias + 8 * b), 2)],
                                                 ACT.Copy).then_inc(ac.sem, 1)
                        split_hi(e, unit_no(self.u + 8 * b + 1, i))
                        for n in range(4):
                            if n == 0 and self.bias is not None:
                                e.wait_ge(ac.sem, i + (self.ac + self.per * b + 5))
                            e.wait_ge(dv.sem, self.taken(b, i, n))
                            e.wait_ge(pe_a.sem, 4 * i + (self.a + 16 * b + n + 1))
                            if self.bias is None:
                                nc.scalar.activation(gate[:, n, :], ps[:, n, :], ACT.Sigmoid).then_inc(act_a.sem, 1)
                            else:
                                nc.scalar.activation(
                                    gate[:, n, :], ps[:, n, :], ACT.Sigmoid,
                                    bias=bcur[:, n // 2:n // 2 + 1]).then_inc(act_a.sem, 1)
                        split_hi(e, unit_no(self.u + 8 * b + 2, i))

            def pool(self, e):
                for b in range(self.nb):
                    with e.Fori(0, 4) as i:
                        split_lo(e, unit_no(self.u + 8 * b + 1, i))
                        split_lo(e, unit_no(self.u + 8 * b + 2, i))

            def dve(self, e):
                self.begin(e)
                for b in range(self.nb):
                    for k in range(4):
                        e.wait_ge(ac.sem, self.ac + self.per * b + k + 1)
                        nc.vector.tensor_tensor(y_lo[:, k, :], yt[:, k % 2, :], y_hi[:, k, :].bitcast(F32),
                                                ALU.subtract).then_inc(dve_a.sem, 1)
                    with e.Fori(0, 4) as i:
                        for n in range(4):
                            dst = big[:, bass.ds(2 * i + n // 2, 1), (n % 2) * HALF:(n % 2 + 1) * HALF]
                            e.wait_ge(act_a.sem, 4 * i + (self.aa + 16 * b + n + 1))
                            e.wait_ge(pe_b.sem, 4 * i + (self.b + 16 * b + n + 1))
                            if b == 0:
                                nc.vector.tensor_tensor(dst, gate[:, n, :].unsqueeze(1), ps[:, 4 + n, :].unsqueeze(1),
                                                        ALU.mult).then_inc(dv.sem, 1)
                            else:
                                nc.vector.tensor_tensor(gate[:, n, :], gate[:, n, :], ps[:, 4 + n, :],
                                                        ALU.mult).then_inc(dv.sem, 1)
                                e.wait_ge(dv.sem, 8 * i + (self.d[b] + 2 * n + 1))
                                nc.vector.tensor_tensor(dst, dst, gate[:, n, :].unsqueeze(1), ALU.add).then_inc(dv.sem, 1)

            def pe(self, e):
                self.begin(e, stores=False)
                for b in range(self.nb):
                    with e.Fori(0, 4) as i:
                        feature_tiles(e, unit_no(self.u + 8 * b, i), KT, H, 0,
                                      lambda n: [(act_a, 4 * i + (self.aa + 16 * b + n - 3))], pe_a)
                        e.wait_ge(dve_a.sem, self.lo + 4 * b + 4)
                        feature_tiles(e, unit_no(self.u + 8 * b + 1, i), 4, (y_hi, y_lo), 4,
                                      lambda n: [(dv, self.taken(b, i, n))], pe_b)

        class FeedForward(Stage):

            def __init__(self, ups, down, width, norm, onto_x, load_x=False):
                super().__init__()
                self.norm, self.onto_x, self.stored = norm, onto_x, d_out.n
                self.x_in = d_in.take(16) if load_x else None
                self.ups, self.down, self.n = ups, down, width // 256
                self.g = len(ups)
                n = self.n
                self.u = take_units(n * (self.g + 1))
                self.a, self.b = pe_a.take(4 * self.g * n), pe_b.take(16 * n)
                self.aa, self.db, self.d = act_a.take(4 * n), dve_b.take(16 * n), dv.take(8 * n)
                self.o = po.take(4 * n) - 1 if onto_x else po.take(4 * n + 1)

            def final(self, k):
                return [(po, self.o + 4 * self.n + 1), (dve_b, self.db + 16 * (self.n - 1) + 2 * k + 2)]

            def units_of(self, c, i):
                per = 2 * (self.g + 1)
                first = self.u + self.g + (self.g + 1) * c
                return [unit_no(first + j, i, per) for j in range(self.g + 1)]

            def slots(self, e, ups, down):
                n = self.n
                ups(0, None, [unit_no(self.u + j) for j in range(self.g)])
                pairs = (n - 1) // 2
                with e.Fori(0, pairs) as i:
                    for c in range(2):
                        us = self.units_of(c, i)
                        ups(c + 1, i, us[:-1])
                        down(c, i, us[-1])
                for c in range(2 * pairs, n):
                    us = self.units_of(c, None)
                    if c + 1 < n:
                        ups(c + 1, None, us[:-1])
                        down(c, None, us[-1])
                    else:
                        down(c, None, unit_no(self.u + (self.g + 1) * n - 1))

            @staticmethod
            def at(base, step, c, i):
                return base + step * c if i is None else 2 * step * i + (base + step * c)

            def sp(self, e):
                def col(c, i):
                    return 256 * c if i is None else e.snap(512 * i + 256 * c)

                def ups(c, i, us):
                    for w, u in zip(self.ups, us):
                        load_unit(e, u, w[:, bass.ds(col(c, i), 256)].rearrange("(k p) n -> p k n", p=P), (KT, 256))

                def down(c, i, u):
                    load_unit(e, u, self.down[bass.ds(col(c, i), 256), :].rearrange("(k p) n -> p k n", p=P), (2, D))
                self.slots(e, ups, down)
                if self.x_in is not None:
                    e.wait_ge(d_out.sem, self.stored)
                    e.wait_ge(pe_a.sem, self.a + 4 * self.g * self.n)
                    e.dma_start(xh[:, :, :], scratch["x_keep"]).then_inc(d_in.sem, 16)

            def act(self, e):
                self.begin(e)

                def ups(c, i, us):
                    split_hi(e, (us[0][0] + 1,) + us[0][1:])
                    for n in range(4):
                        if not (i is None and c == 0):
                            e.wait_ge(dv.sem, self.at(self.d, 8, c - 1, i) + (2 * n + 1))
                        e.wait_ge(pe_a.sem, self.at(self.a, 4 * self.g, c, i) + (n + 1))
                        nc.scalar.activation(fr[:, n, :], ps[:, n, :], ACT.Relu if self.g == 1 else ACT.Silu
                                             ).then_inc(act_a.sem, 1)
                    if self.g == 2:
                        split_hi(e, (us[1][0] + 1,) + us[1][1:])

                def down(c, i, u):
                    split_hi(e, (u[0] + 1,) + u[1:])
                self.slots(e, ups, down)

            def pool(self, e):
                split_lo(e, unit_no(self.u + 1))
                self.begin(e)
                if not self.onto_x:
                    e.wait_ge(d_out.sem, self.stored)
                    nc.gpsimd.memset(big[:, :, :], 0.0).then_inc(po.sem, 1)

                def ups(c, i, us):
                    if not (c == 0 and i is None):
                        split_lo(e, (us[0][0] + 1,) + us[0][1:])
                    if self.g == 2:
                        split_lo(e, (us[1][0] + 1,) + us[1][1:])
                    for n in range(4):
                        e.wait_ge(dv.sem, self.at(self.d, 8, c, i) + (2 * n + 2))
                        nc.gpsimd.tensor_tensor(f_lo[:, c % 2, n // 2, (n % 2) * HALF:(n % 2 + 1) * HALF],
                                                fv[:, n % 2, :],
                                                f_hi[:, c % 2, n // 2, (n % 2) * HALF:(n % 2 + 1) * HALF].bitcast(F32),
                                                ALU.subtract).then_inc(po.sem, 1)

                def down(c, i, u):
                    split_lo(e, (u[0] + 1,) + u[1:])
                self.slots(e, ups, down)

            def dve(self, e):
                self.begin(e)

                def ups(c, i, us):
                    for n in range(4):
                        e.wait_ge(act_a.sem, self.at(self.aa, 4, c, i) + (n + 1))
                        e.wait_ge(po.sem, self.at(self.o, 4, c, i) + n)
                        if self.g == 1:
                            nc.vector.tensor_tensor(fv[:, n % 2, :], fr[:, n, :], fr[:, n, :], ALU.mult).then_inc(dv.sem, 1)
                        else:
                            e.wait_ge(pe_a.sem, self.at(self.a, 8, c, i) + (4 + n + 1))
                            nc.vector.tensor_tensor(fv[:, n % 2, :], fr[:, n, :], ps[:, n, :], ALU.mult).then_inc(dv.sem, 1)
                        if n == 0 and (i is not None or c >= 2):
                            e.wait_ge(pe_b.sem, self.at(self.b, 16, c - 1, i))
                        e.wait_ge(dv.sem, self.at(self.d, 8, c, i) + (2 * n + 1))
                        nc.vector.tensor_copy(f_hi[:, c % 2, n // 2, (n % 2) * HALF:(n % 2 + 1) * HALF],
                                              fv[:, n % 2, :]).then_inc(dv.sem, 1)

                def down(c, i, u):
                    for t in range(16):
                        m, half = t // 2, t % 2
                        e.wait_ge(pe_b.sem, self.at(self.b, 16, c, i) + (t + 1))
                        e.wait_ge(dve_b.sem, self.at(self.db, 16, c, i) + (t - 15))
                        dst = big[:, m, half * HALF:(half + 1) * HALF]
                        nc.vector.tensor_tensor(dst, dst, ps[:, 4 + t % 4, :], ALU.add).then_inc(dve_b.sem, 1)
                        if i is None and c == self.n - 1 and half and m:
                            self.sums.add_square(e, m - 1)
                self.slots(e, ups, down)
                self.sums.add_square(e, KT - 1)

            def pe(self, e):
                def ups(c, i, us):
                    first = i is None and c == 0
                    if first:
                        first_tiles(e, us[0], H, lambda n: [], pe_a,
                                    lambda k: [e.wait_ge(x.sem, n) for x, n in self.norm.ready(k)])
                    elif self.g == 1:
                        feature_tiles(e, us[0], KT, H, 0, lambda n: [(act_a, self.at(self.aa, 4, c, i) + (n - 3))], pe_a)
                    else:
                        feature_tiles(e, us[0], KT, H, 0,
                                      lambda n: [(dv, self.at(self.d, 8, c, i) + (2 * n - 7))], pe_a)
                    if self.g == 2:
                        feature_tiles(e, us[1], KT, H, 0,
                                      lambda n: [(act_a, self.at(self.aa, 4, c, i) + (n + 1))], pe_a)

                def down(c, i, u):
                    w = unit_view(u[0], 2)
                    e.wait_ge(s_lo.sem, upto_unit(u, 1))
                    e.wait_ge(po.sem, self.at(self.o, 4, c, i) + 5)
                    for t in range(16):
                        m, half = t // 2, t % 2
                        e.wait_ge(dve_b.sem, self.at(self.db, 16, c, i) + (t - 3))
                        mm3(ps[:, 4 + t % 4, :], lambda a, k: w(a, k, m * P, P),
                            lambda b, k: (f_hi, f_lo)[b][:, c % 2, k, half * HALF:(half + 1) * HALF],
                            2, t == 0).then_inc(pe_b.sem, 1)
                self.slots(e, ups, down)

        m = {n: sig(n) for n in (
            "s5_in", "s5_natT", "s5_arg", "s5_fun", "s5_cT", "s5_wt", "s5_mm", "s5_m2", "s5_wT", "s5_k", "s5_w",
            "s5_kp", "s5_tz", "s5_uT", "s5_ug", "s5_v", "s5_p", "s5_y", "s5_g", "s5_yT", "s5_ya", "s5_glu",
            "s5_sg", "s5_out", "s5_step", "s5_wg", "s5_ld", "s5_win", "s5_half", "s5_tables",
            "s5_pool")}
        s5_done = m["s5_out"]
        s5_done.take(4)
        m = {n: x.sem for n, x in m.items()}

        class S5(Stage):

            def __init__(self, norm):
                super().__init__()
                self.norm = norm
                self.u = take_units(2)
                self.a, self.aa = pe_a.take(16), act_a.take(16)
                self.out = d_out.take(64)

            def close(self):
                super().close()
                marks[-1][s5_done] = 4

            def sp(self, e):
                for j in range(2):
                    load_unit(e, unit_no(self.u + j), w_cols(A["w_in"][0], 0, O_U + 256 * j, KT, 256), (KT, 256))
                for j, o in enumerate((O_X, O_C)):
                    load_unit(e, unit_no(self.u + 2 + j), w_cols(A["w_in"][0], 0, o, KT, 256), (KT, 256))
                kp = PP[0:GRP].rearrange("p a g n -> p (a g n)")[:, 0:GB * 240].rearrange("p (g n) -> p g n", g=GB)
                for f in range(4):
                    e.wait_ge(m["s5_kp"], f + 1)
                    for s in range(SC):
                        e.dma_start(TZ[s * GRP:(s + 1) * GRP, :, :], kp[:, :, s * GRP:s * GRP + P]).then_inc(m["s5_tz"], 16)

            def act(self, e):
                self.begin(e)
                for k, name in enumerate(("s5_a_re", "s5_a_im")):
                    for half in range(2):
                        e.dma_start(nat[0:NG, 2 + k, half * ST:(half + 1) * ST], A[name][0]).then_inc(m["s5_ld"], 16)
                e.dma_start(sm[:, 19, :], A["s5_log_dt"][0:1, :].partition_broadcast(P)).then_inc(m["s5_ld"], 16)
                e.dma_start(DD[:, :], A["s5_d"][0].rearrange("g h -> h g"),
                            allow_slow_non_contiguous=True).then_inc(m["s5_ld"], 16)
                for n, (o, i, fn, sc) in enumerate(((1, 0, ACT.Tanh, 0.5), (5, 4, ACT.Tanh, 0.5),
                                                    (7, 6, ACT.Sin, 1.0), (8, 6, ACT.Sin, 0.5))):
                    if n != 3:
                        e.wait_ge(m["s5_arg"], n + 1)
                    nc.scalar.activation(sm[:, o, :], sm[:, i, :], fn, scale=sc).then_inc(m["s5_fun"], 1)
                split_hi(e, unit_no(self.u + 1))
                def load_groups(f):
                    rows = slice(f * P, f * P + P)
                    cre = A["s5_c_re"][0].rearrange("g h p -> (g h) p")
                    cim = A["s5_c_im"][0].rearrange("g h p -> (g h) p")
                    for k, (lo, hi_) in enumerate(((cre, cim), (cim, cre))):
                        e.dma_start(nat[:, k, 0:ST], lo[rows, :]).then_inc(m["s5_in"], 16)
                        e.dma_start(nat[:, k, ST:P], hi_[rows, :]).then_inc(m["s5_in"], 16)
                    gr = slice(f * GB, f * GB + GB)
                    bre = A["s5_b_re"][0][gr].rearrange("g p h -> p g h")
                    bim = A["s5_b_im"][0][gr].rearrange("g p h -> p g h")
                    for k, (lo, hi_) in enumerate(((bre, bim), (bim, bre))):
                        e.dma_start(bst[0:ST, k], lo).then_inc(m["s5_in"], 16)
                        e.dma_start(bst[ST:P, k], hi_).then_inc(m["s5_in"], 16)

                load_groups(0)
                for n in range(16):
                    j, s = n // 8, n % 8
                    e.wait_ge(pe_a.sem, self.a + n + 1)
                    nc.scalar.activation(U[:, 16 * j:16 * j + 16, SC - 1 - s, :],
                                         ps[:, n % 4, 0:256].rearrange("p (g h) -> p g h", h=GRP),
                                         ACT.Copy).then_inc(act_a.sem, 1)
                    if n == 7:
                        split_hi(e, unit_no(self.u + 2))

                def load_glu(f):
                    for g in range(GB):
                        e.dma_start(WG[g * GRP:(g + 1) * GRP, g * GRP:(g + 1) * GRP],
                                    A["s5_w_glu"][0, f * GB + g]).then_inc(m["s5_win"], 16)

                def store(f):
                    e.wait_ge(m["s5_out"], f + 1)
                    e.dma_start(scratch["y_keep"][0, :, f, :], YA[:, :]).then_inc(d_out.sem, 16)
                e.wait_ge(m["s5_wg"], 1)
                load_glu(0)
                for f in range(4):
                    e.wait_ge(m["s5_wT"], f + 1)
                    v = ps[:, 0:2, :].rearrange("p b (g n) -> p (b g) n", n=P)
                    nc.scalar.activation(W1[:, :, :], v, ACT.Copy)
                    nc.scalar.activation(W2[:, :, 0:ST], v[:, :, ST:P], ACT.Copy)
                    nc.scalar.activation(W2[:, :, ST:P], v[:, :, 0:ST], ACT.Copy, scale=-1.0).then_inc(m["s5_w"], 1)
                    e.wait_ge(m["s5_uT"], f + 1)
                    nc.scalar.activation(ug[:, :, :], ps[:, 4:6, :].rearrange("p b (g n) -> p (b g) n", n=P),
                                         ACT.Copy).then_inc(m["s5_ug"], 1)
                    if f < 3:
                        load_groups(f + 1)
                    if f:
                        store(f - 1)
                    e.wait_ge(m["s5_y"], f + 1)
                    yv = WT[:, :, :].rearrange("p a b -> p (a b)").rearrange("p (t g h) -> p g t h", t=SC, g=GB)
                    for b in range(2):
                        last = nc.scalar.activation(
                            yv[:, 4 * b:4 * b + 4], ps[:, 4 + b, :].rearrange("p (g t h) -> p g t h", g=4, t=SC),
                            ACT.Gelu_apprx_tanh)
                    last.then_inc(m["s5_g"], 1)
                    e.wait_ge(m["s5_yT"], f + 1)
                    if f:
                        e.wait_ge(d_out.sem, self.out + 16 * f)
                    for b in range(2):
                        last = nc.scalar.activation(
                            YA[:, :].rearrange("p (c t) -> p t c", t=SC)[:, 4 * b:4 * b + 4, :],
                            ps[:, 6 + b, :].rearrange("p (t c) -> p t c", t=4), ACT.Copy)
                    last.then_inc(m["s5_ya"], 1)
                    e.wait_ge(m["s5_glu"], f + 1)
                    nc.scalar.activation(zz[:, :, :].rearrange("p g n -> p (g n)"), ps[:, 0:2, :].rearrange("p b n -> p (b n)"),
                                         ACT.Sigmoid).then_inc(m["s5_sg"], 1)
                    if f < 3:
                        load_glu(f + 1)
                store(3)

            def pool(self, e):
                self.begin(e)
                nc.gpsimd.memset(WG[:, :], 0.0).then_inc(m["s5_wg"], 1)
                split_lo(e, unit_no(self.u + 1))
                split_lo(e, unit_no(self.u + 2))
                n = [0]

                def tt(o, a, b, op):
                    nc.gpsimd.tensor_tensor(o, a, b, op).then_inc(m["s5_pool"], 1)
                    n[0] += 1
                    e.wait_ge(m["s5_pool"], n[0])
                for f in range(4):
                    gr = slice(f * GB, f * GB + GB)
                    e.wait_ge(m["s5_half"], f + 1)
                    s = diag[:, 0:GB * 64].rearrange("p (g k) -> p g k", g=GB)
                    c, d, hc, hd = CT[:, :, 0:64], SN[:, :, 0:64], CT[:, :, 64:128], SN[:, :, 64:128]
                    mr, mi = [x[:, 6, gr].unsqueeze(2).to_broadcast([P, GB, 64]) for x in (MR, MI)]
                    tt(hc, c, mr, ALU.mult)
                    tt(s, d, mi, ALU.mult)
                    tt(hc, hc, s, ALU.subtract)
                    tt(hd, c, mi, ALU.mult)
                    tt(s, d, mr, ALU.mult)
                    tt(hd, hd, s, ALU.add)
                    e.engine_nop().then_inc(m["s5_tables"], 1)
                    e.wait_ge(m["s5_mm"], f + 1)
                    if f:
                        e.wait_ge(m["s5_y"], f)
                    pr, pi = [x[:, gr, 1:1 + SC].unsqueeze(3).to_broadcast([P, GB, SC, GRP]) for x in (PR, PI)]
                    s = diag[:, :].rearrange("p (g k h) -> p g k h", g=GB, k=SC)
                    tt(M2[:, :, :, :], pr, C2[:, :, :].unsqueeze(2).to_broadcast([P, GB, SC, GRP]), ALU.mult)
                    tt(s, pi, C1[:, :, :].unsqueeze(2).to_broadcast([P, GB, SC, GRP]), ALU.mult)
                    tt(M2[:, :, :, :], M2[:, :, :, :], s, ALU.subtract)
                    e.engine_nop().then_inc(m["s5_m2"], 1)

            def dve(self, e):
                self.begin(e)
                n = [0]

                def link(ins):
                    ins.then_inc(m["s5_step"], 1)
                    n[0] += 1
                    e.wait_ge(m["s5_step"], n[0])

                def tt(o, a, b, op):
                    link(nc.vector.tensor_tensor(o, a, b, op))

                def ts(o, a, s1, op0, s2=None, op1=ALU.bypass):
                    link(nc.vector.tensor_scalar(o, a, s1, s2, op0, op1))

                S = [sm[:, j, :] for j in range(20)]
                e.wait_ge(m["s5_ld"], 16 * 6)
                ts(S[9], S[19], 1.4426950408889634, ALU.mult)
                ts(S[9], S[9], MAGIC, ALU.add, -MAGIC, ALU.add)
                ts(S[9], S[9], -127.0, ALU.max, 127.0, ALU.min)
                ts(S[0], S[9], -LN2_PARTS[0], ALU.mult)
                tt(S[0], S[0], S[19], ALU.add)
                ts(S[10], S[9], -LN2_PARTS[1], ALU.mult)
                nc.vector.tensor_tensor(S[0], S[0], S[10], ALU.add).then_inc(m["s5_arg"], 1)
                ts(S[9], S[9], 127.0, ALU.add, 8388608.0, ALU.mult)
                link(nc.vector.tensor_copy(ki[:, :], S[9]))

                def expm1(o, th):
                    ts(S[10], th, -1.0, ALU.mult, 1.0, ALU.add)
                    link(nc.vector.reciprocal(S[10], S[10]))
                    tt(o, th, S[10], ALU.mult)
                    ts(o, o, 2.0, ALU.mult)

                e.wait_ge(m["s5_fun"], 1)
                expm1(S[2], S[1])
                ts(S[2], S[2], 1.0, ALU.add)
                tt(S[2], S[2], ki[:, :].bitcast(F32), ALU.mult)
                e.wait_ge(m["s5_natT"], 1)
                ts(S[3], ps[:, 6, 0:NG], -1e-4, ALU.min)
                link(nc.vector.tensor_copy(S[11], ps[:, 6, NG:2 * NG]))
                nc.vector.tensor_tensor(S[4], S[3], S[2], ALU.mult).then_inc(m["s5_arg"], 1)
                tt(S[6], S[11], S[2], ALU.mult)
                ts(S[9], S[6], 1.0 / TWO_PI, ALU.mult)
                ts(S[9], S[9], MAGIC, ALU.add, -MAGIC, ALU.add)
                for c in PI_PARTS:
                    ts(S[10], S[9], -c, ALU.mult)
                    tt(S[6], S[6], S[10], ALU.add)
                ts(S[6], S[6], 3.1415925, ALU.min, -3.1415925, ALU.max)
                nc.vector.tensor_copy(S[12], S[6]).then_inc(m["s5_arg"], 1)
                e.wait_ge(m["s5_fun"], 2)
                expm1(S[5], S[5])
                ts(S[13], S[5], 1.0, ALU.add)
                e.wait_ge(m["s5_fun"], 4)
                tt(S[9], S[8], S[8], ALU.mult)
                ts(S[9], S[9], -2.0, ALU.mult)
                ts(S[8], S[9], 1.0, ALU.add)
                tt(S[10], S[5], S[8], ALU.mult)
                tt(S[9], S[9], S[10], ALU.add)
                tt(S[10], S[13], S[7], ALU.mult)
                tt(S[14], S[3], S[3], ALU.mult)
                tt(S[15], S[11], S[11], ALU.mult)
                tt(S[14], S[14], S[15], ALU.add)
                link(nc.vector.reciprocal(S[14], S[14]))
                tt(S[15], S[9], S[3], ALU.mult)
                tt(S[16], S[10], S[11], ALU.mult)
                tt(S[15], S[15], S[16], ALU.add)
                tt(S[15], S[15], S[14], ALU.mult)
                tt(S[16], S[10], S[3], ALU.mult)
                tt(S[17], S[9], S[11], ALU.mult)
                tt(S[16], S[16], S[17], ALU.subtract)
                tt(S[16], S[16], S[14], ALU.mult)
                link(nc.vector.memset(PR[:, :, 0:1], 1.0))
                link(nc.vector.memset(PI[:, :, 0:1], 0.0))
                link(nc.vector.tensor_scalar(PR[:, :, 1:2], S[9].unsqueeze(2), 1.0, None, ALU.add))
                link(nc.vector.tensor_copy(PI[:, :, 1:2], S[10].unsqueeze(2)))
                scr = tm[:, 0:NG * 4].rearrange("p (g k) -> p g k", g=NG)

                def cmul(o_r, o_i, x_r, x_i, y_r, y_i, s):
                    tt(o_r, x_r, y_r, ALU.mult)
                    tt(s, x_i, y_i, ALU.mult)
                    tt(o_r, o_r, s, ALU.subtract)
                    tt(o_i, x_r, y_i, ALU.mult)
                    tt(s, x_i, y_r, ALU.mult)
                    tt(o_i, o_i, s, ALU.add)

                for k in (1, 2, 4):
                    bc = lambda x: x[:, :, k:k + 1].to_broadcast([P, NG, k])
                    cmul(PR[:, :, k + 1:2 * k + 1], PI[:, :, k + 1:2 * k + 1], PR[:, :, 1:k + 1], PI[:, :, 1:k + 1],
                         bc(PR), bc(PI), scr[:, :, 0:k])
                for k in range(3):
                    tt(S[13], S[13], S[13], ALU.mult)
                link(nc.vector.tensor_copy(MR[:, 0, :], S[8]))
                link(nc.vector.tensor_copy(MI[:, 0, :], S[7]))
                for k in range(3):
                    tt(S[17], MR[:, 0, :], MI[:, 0, :], ALU.mult)
                    tt(MR[:, 0, :], MR[:, 0, :], MR[:, 0, :], ALU.mult)
                    tt(MI[:, 0, :], MI[:, 0, :], MI[:, 0, :], ALU.mult)
                    tt(MR[:, 0, :], MR[:, 0, :], MI[:, 0, :], ALU.subtract)
                    ts(MI[:, 0, :], S[17], 2.0, ALU.mult)
                for j in range(6):
                    cmul(MR[:, j + 1, :], MI[:, j + 1, :], MR[:, j, :], MI[:, j, :], MR[:, j, :], MI[:, j, :], S[17])

                def turn_tables(f):
                    gr = slice(f * GB, f * GB + GB)
                    link(nc.vector.memset(CT[:, :, 0:1], 1.0))
                    link(nc.vector.memset(SN[:, :, 0:1], 0.0))
                    for j in range(6):
                        w = 1 << j
                        s = tm[:, 0:GB * w].rearrange("p (g k) -> p g k", g=GB)
                        bc = lambda x: x[:, j, gr].unsqueeze(2).to_broadcast([P, GB, w])
                        cmul(CT[:, :, w:2 * w], SN[:, :, w:2 * w], CT[:, :, 0:w], SN[:, :, 0:w], bc(MR), bc(MI), s)
                    e.engine_nop().then_inc(m["s5_half"], 1)

                def gated(f):
                    e.wait_ge(m["s5_sg"], f + 1)
                    nc.vector.tensor_tensor(YA[:, :], YA[:, :], zz[:, :, :].rearrange("p g n -> p (g n)"),
                                            ALU.mult).then_inc(m["s5_out"], 1)
                    e.wait_ge(m["s5_out"], f + 1)
                turn_tables(0)
                for f in range(4):
                    gr = slice(f * GB, f * GB + GB)
                    e.wait_ge(m["s5_in"], 128 * (f + 1))
                    q_r = sm[:, 15, gr].unsqueeze(2).to_broadcast([P, GB, GRP])
                    q_i = sm[:, 16, gr].unsqueeze(2).to_broadcast([P, GB, GRP])
                    b1, b2 = bst[:, 0], bst[:, 1]
                    ts(b2, b2, c_sgn, ALU.mult)
                    s1 = tm[:, 0:GB * GRP].rearrange("p (g h) -> p g h", g=GB)
                    tt(BA[:, :, :], b1, q_r, ALU.mult)
                    tt(s1, b2, q_i, ALU.mult)
                    tt(BA[:, :, :], BA[:, :, :], s1, ALU.add)
                    tt(BB[:, :, :], b2, q_r, ALU.mult)
                    tt(s1, b1, q_i, ALU.mult)
                    tt(BB[:, :, :], BB[:, :, :], s1, ALU.subtract)

                    def power_sum(o, lo, cnt, x, y, op, done):
                        pr = PR[:, gr, lo:lo + cnt].unsqueeze(3).to_broadcast([P, GB, cnt, GRP])
                        pi = PI[:, gr, lo:lo + cnt].unsqueeze(3).to_broadcast([P, GB, cnt, GRP])
                        s = tm[:, 0:GB * cnt * GRP].rearrange("p (g k h) -> p g k h", g=GB, k=cnt)
                        tt(o, pr, x.unsqueeze(2).to_broadcast([P, GB, cnt, GRP]), ALU.mult)
                        tt(s, pi, y.unsqueeze(2).to_broadcast([P, GB, cnt, GRP]), ALU.mult)
                        tt(o, o, s, op)
                        e.engine_nop().then_inc(done, 1)

                    if f:
                        e.wait_ge(m["s5_yT"], f)
                    power_sum(WT[:, :, :].rearrange("p g (k h) -> p g k h", h=GRP), 0, SC, BA[:, :, :], BB[:, :, :],
                              ALU.add, m["s5_wt"])
                    e.wait_ge(m["s5_cT"], f + 1)
                    cT = lambda k: ps[:, 6, k * P:(k + 1) * P].rearrange("p (g h) -> p g h", h=GRP)
                    if f:
                        e.wait_ge(m["s5_m2"], f)
                    ts(C1[:, :, :], cT(0), c_nsgn, ALU.mult)
                    ts(C2[:, :, :], cT(1), -1.0, ALU.mult)
                    power_sum(MM[:, :, :, :], 0, SC + 1, C1[:, :, :], C2[:, :, :], ALU.add, m["s5_mm"])
                    if f:
                        gated(f - 1)
                    kp = PP[0:GRP].rearrange("p a g n -> p (a g n)")[:, 0:GB * 240].rearrange("p (g n) -> p g n", g=GB)
                    nc.vector.memset(kp[:, :, 0:7 * GRP], 0.0)
                    e.wait_ge(m["s5_k"], f + 1)
                    link(nc.vector.tensor_copy(kp[:, :, 7 * GRP:240],
                                               ps[0:GRP, 6:8, :].rearrange("p b (g n) -> p (b g) n", n=P)))
                    dg = tm[0:GRP, 0:GB * GRP].rearrange("p (g h) -> p g h", g=GB)
                    tt(dg, ident[0:GRP, 0:GRP].unsqueeze(1).to_broadcast([GRP, GB, GRP]),
                       DD[:, gr].unsqueeze(2).to_broadcast([GRP, GB, GRP]), ALU.mult)
                    nc.vector.tensor_tensor(kp[:, :, 7 * GRP:8 * GRP], kp[:, :, 7 * GRP:8 * GRP], dg,
                                            ALU.add).then_inc(m["s5_kp"], 1)
                    e.wait_ge(m["s5_tables"], f + 1)
                    e.wait_ge(m["s5_v"], f + 1)
                    v = lambda b: ps[:, b:b + 2, :].rearrange("p b (g n) -> p (b g) n", n=P)
                    s = tm[:, 0:L].rearrange("p (g k) -> p g k", g=GB)
                    tt(zz[:, :, :], CT[:, :, :], v(0), ALU.mult)
                    tt(s, SN[:, :, :], v(2), ALU.mult)
                    tt(zz[:, :, :], zz[:, :, :], s, ALU.add)
                    for g in range(GB):
                        link(nc.vector.tensor_tensor_scan(
                            zz[:, g, :], sm[:, 13, f * GB + g:f * GB + g + 1].to_broadcast([P, NC]), zz[:, g, :],
                            0.0, ALU.mult, ALU.add))
                    e.wait_ge(m["s5_tz"], 128 * (f + 1))
                    link(nc.vector.memset(PP[:, :, :, 0:1], 0.0))
                    tt(PP[:, 0, :, 1:], CT[:, :, :], zz[:, :, :], ALU.mult)
                    nc.vector.tensor_tensor(PP[:, 1, :, 1:], SN[:, :, :], zz[:, :, :], ALU.mult).then_inc(m["s5_p"], 1)
                    if f < 3:
                        turn_tables(f + 1)
                gated(3)

            def pe(self, e):
                w = unit_view(self.u, KT)
                e.wait_ge(s_lo.sem, upto_unit(unit_no(self.u), 1))
                for k in range(KT):
                    for x, n in self.norm.ready(k):
                        e.wait_ge(x.sem, n)
                    for s in range(4):
                        for q, (a, b) in enumerate(((0, 0), (0, 1), (1, 0))):
                            last = nc.tensor.matmul(ps[:, s, 0:256], H[a][:, k, s::SC], w(b, k, 0, 256),
                                                    start=(k == 0 and q == 0), stop=(k == KT - 1 and q == 2))
                            if k == 0 and s == 0 and q == 0:
                                last.then_inc(s_begun.sem, 1)
                        if k == KT - 1:
                            last.then_inc(pe_a.sem, 1)
                e.wait_ge(m["s5_ld"], 16 * 6)
                nc.tensor.transpose(ps[:, 6, 0:NG], nat[0:NG, 2, :], ident[0:NG, 0:NG])
                nc.tensor.transpose(ps[:, 6, NG:2 * NG], nat[0:NG, 3, :], ident[0:NG, 0:NG]).then_inc(m["s5_natT"], 1)
                for j in range(2):
                    u = unit_no(self.u + j)
                    w = unit_view(u[0], KT)
                    e.wait_ge(s_lo.sem, upto_unit(u, 1))
                    for s in range(0 if j else 4, SC):
                        n = 8 * j + s
                        e.wait_ge(act_a.sem, self.aa + n - 3)
                        mm3(ps[:, n % 4, 0:256], lambda a, k: H[a][:, k, s::SC], lambda b, k: w(b, k, 0, 256), KT,
                            n == 8).then_inc(pe_a.sem, 1)
                e.wait_ge(act_a.sem, self.aa + 16)
                e.wait_ge(m["s5_arg"], 3)
                for f in range(4):
                    e.wait_ge(m["s5_in"], 128 * (f + 1))
                    if f:
                        e.wait_ge(m["s5_ya"], f)
                    for k in range(2):
                        last = nc.tensor.transpose(ps[:, 6, k * P:(k + 1) * P], nat[:, k, :], ident)
                    last.then_inc(m["s5_cT"], 1)
                    e.wait_ge(m["s5_wt"], f + 1)
                    if f:
                        e.wait_ge(m["s5_sg"], f)
                    for g in range(GB):
                        last = nc.tensor.transpose(ps[:, g // 4, (g % 4) * P:(g % 4 + 1) * P], WT[:, g, :], ident)
                    last.then_inc(m["s5_wT"], 1)
                    if f:
                        e.wait_ge(m["s5_g"], f)
                    for g in range(GB):
                        last = nc.tensor.transpose(
                            ps[:, 4 + g // 4, (g % 4) * P:(g % 4 + 1) * P],
                            U[:, f * GB + g, :, :].rearrange("p s h -> p (s h)"), ident)
                    last.then_inc(m["s5_uT"], 1)
                    e.wait_ge(m["s5_w"], f + 1)
                    e.wait_ge(m["s5_ug"], f + 1)
                    for k, W in enumerate((W1, W2)):
                        for g in range(GB):
                            last = nc.tensor.matmul(ps[:, 2 * k + g // 4, (g % 4) * P:(g % 4 + 1) * P], W[:, g, :],
                                                    ug[:, g, :], start=True, stop=True)
                    last.then_inc(m["s5_v"], 1)
                    e.wait_ge(m["s5_mm"], f + 1)
                    for g in range(GB):
                        last = nc.tensor.matmul(
                            ps[0:GRP, 6 + g // 4, (g % 4) * P:(g % 4 + 1) * P], BA[:, g, :],
                            MM[:, g, 0:SC, :].rearrange("p k h -> p (k h)"), start=True, stop=True)
                    last.then_inc(m["s5_k"], 1)
                    e.wait_ge(m["s5_p"], f + 1)
                    e.wait_ge(m["s5_m2"], f + 1)
                    e.wait_ge(m["s5_tz"], 128 * (f + 1))
                    for g in range(GB):
                        o = ps[:, 4 + g // 4, (g % 4) * P:(g % 4 + 1) * P]
                        nc.tensor.matmul(o, ug[:, g, :], TZ[:, g, :], start=True, stop=False)
                        nc.tensor.matmul(o, PP[:, 0, g, 0:NC], MM[:, g, 1:, :].rearrange("p k h -> p (k h)"),
                                         start=False, stop=False)
                        last = nc.tensor.matmul(o, PP[:, 1, g, 0:NC], M2[:, g, :, :].rearrange("p k h -> p (k h)"),
                                                start=False, stop=True)
                    last.then_inc(m["s5_y"], 1)
                    e.wait_ge(m["s5_g"], f + 1)
                    for t in range(SC):
                        last = nc.tensor.transpose(
                            ps[:, 6 + t // 4, (t % 4) * P:(t % 4 + 1) * P],
                            WT[:, :, :].rearrange("p a b -> p (a b)")[:, t * P:(t + 1) * P], ident)
                    last.then_inc(m["s5_yT"], 1)
                    e.wait_ge(m["s5_ya"], f + 1)
                    e.wait_ge(m["s5_win"], 128 * (f + 1))
                    for half in range(2):
                        last = nc.tensor.matmul(ps[:, half, :], WG[:, :], YA[:, half * HALF:(half + 1) * HALF],
                                                start=True, stop=True)
                    last.then_inc(m["s5_glu"], 1)

        class Conv(Stage):

            def __init__(self):
                super().__init__()
                self.u = take_units(6)
                self.a, self.aa = pe_a.take(24), act_a.take(8)
                self.d = dv.take(1 + 2 * 14)
                d_out.take(16)

            def sp(self, e):
                for j in range(2):
                    for k, o in enumerate((O_X, O_C, O_B)):
                        if 3 * j + k < 2:
                            continue
                        load_unit(e, unit_no(self.u + 3 * j + k), w_cols(A["w_in"][0], 0, o + 256 * j, KT, 256), (KT, 256))

            def act(self, e):
                self.begin(e)
                for j in range(2):
                    split_hi(e, unit_no(self.u + 3 * j + 1))
                    for n in range(4):
                        if j:
                            e.wait_ge(dv.sem, self.d + 1 + 14 * (j - 1) + 7 * (n // 2) + 2)
                        e.wait_ge(pe_a.sem, self.a + 12 * j + n + 1)
                        nc.scalar.activation(cx[:, n // 2, (n % 2) * HALF:(n % 2 + 1) * HALF], ps[:, n, :],
                                             ACT.Copy).then_inc(act_a.sem, 1)
                    split_hi(e, unit_no(self.u + 3 * j + 2))
                    split_hi(e, unit_no(self.u + 3 * j + 3))
                e.wait_ge(dv.sem, self.d + 29)
                e.dma_start(scratch["y_keep"][1], cacc[:, :, :]).then_inc(d_out.sem, 16)

            def pool(self, e):
                for k in range(6):
                    split_lo(e, unit_no(self.u + k + 1))

            def dve(self, e):
                self.begin(e)
                nc.vector.memset(vbuf[:, 0:2], 0.0).then_inc(dv.sem, 1)
                for j in range(2):
                    for q in range(2):
                        f = 2 * j + q
                        d = self.d + 1 + 7 * f
                        for half in range(2):
                            e.wait_ge(act_a.sem, self.aa + 4 * j + 2 * q + half + 1)
                            e.wait_ge(pe_a.sem, self.a + 12 * j + 4 + 2 * q + half + 1)
                            nc.vector.tensor_tensor(vbuf[:, 2 + half * HALF:2 + (half + 1) * HALF],
                                                    cx[:, q, half * HALF:(half + 1) * HALF],
                                                    ps[:, 4 + 2 * q + half, :], ALU.mult).then_inc(dv.sem, 1)
                        e.wait_ge(dv.sem, d + 2)
                        tap = lambda t: vecs[:, V_CW + 4 * t + f:V_CW + 4 * t + f + 1]
                        nc.vector.tensor_scalar(cacc[:, f, :], vbuf[:, 0:L], tap(0), None, ALU.mult).then_inc(dv.sem, 1)
                        for t in (1, 2):
                            e.wait_ge(dv.sem, d + 2 + t)
                            nc.vector.scalar_tensor_tensor(out=cacc[:, f, :], in0=vbuf[:, t:t + L], scalar=tap(t),
                                                           in1=cacc[:, f, :], op0=ALU.mult, op1=ALU.add).then_inc(dv.sem, 1)
                        e.wait_ge(dv.sem, d + 5)
                        for half in range(2):
                            sl = slice(half * HALF, (half + 1) * HALF)
                            e.wait_ge(pe_a.sem, self.a + 12 * j + 8 + 2 * q + half + 1)
                            nc.vector.tensor_tensor(cacc[:, f, sl], cacc[:, f, sl], ps[:, 2 * q + half, :],
                                                    ALU.mult).then_inc(dv.sem, 1)

            def pe(self, e):
                self.begin(e)
                for j in range(2):
                    feature_tiles(e, unit_no(self.u + 3 * j), KT, H, 0,
                                  lambda n: [(dv, self.d + 1 + 14 * (j - 1) + 7 * (n // 2 + 1))] if j else [], pe_a)
                    feature_tiles(e, unit_no(self.u + 3 * j + 1), KT, H, 4, lambda n: [], pe_a)
                    feature_tiles(e, unit_no(self.u + 3 * j + 2), KT, H, 0,
                                  lambda n: [(act_a, self.aa + 4 * j + n + 1)], pe_a)

        class Decay(Stage):

            def __init__(self):
                super().__init__()
                self.u, self.stored = take_units(1), d_out.n
                self.a, self.d, self.c = pe_a.take(2), dv.take(6), ac.take(3)

            def sp(self, e):
                load_unit(e, unit_no(self.u), w_cols(A["w_in"][0], 0, O_F, KT, 256), (KT, 256))

            def act(self, e):
                self.begin(e, stores=False)
                split_hi(e, unit_no(self.u + 1))
                a = PB[0:HEADS, 1, :]
                e.wait_ge(dv.sem, self.d + 1)
                nc.scalar.activation(a, PB[0:HEADS, 0, :], ACT.Abs).then_inc(ac.sem, 1)
                e.wait_ge(ac.sem, self.c + 1)
                nc.scalar.activation(a, a, ACT.Exp, scale=-1.0).then_inc(ac.sem, 1)
                e.wait_ge(ac.sem, self.c + 2)
                nc.scalar.activation(a, a, ACT.Ln, bias=1.0).then_inc(ac.sem, 1)

            def pool(self, e):
                split_lo(e, unit_no(self.u + 1))

            def dve(self, e):
                self.begin(e, stores=False)
                e.wait_ge(pe_a.sem, self.a + 2)
                z = PB[0:HEADS, 0, :]
                nc.vector.tensor_scalar(z, ps[0:HEADS, 4:6, :].rearrange("p b n -> p (b n)"), bf[0:HEADS, 0:1], None,
                                        ALU.add).then_inc(dv.sem, 1)
                e.wait_ge(ac.sem, self.c + 3)
                nc.vector.tensor_scalar(z, z, 0.0, None, ALU.min).then_inc(dv.sem, 1)
                e.wait_ge(dv.sem, self.d + 2)
                nc.vector.tensor_tensor(z, z, PB[0:HEADS, 1, :], ALU.subtract).then_inc(dv.sem, 1)
                e.wait_ge(dv.sem, self.d + 3)
                nc.vector.tensor_tensor_scan(cum[0:HEADS, :], ones[0:HEADS, 0:1].to_broadcast([HEADS, L]), z, 0.0,
                                             ALU.mult, ALU.add).then_inc(dv.sem, 1)
                e.wait_ge(dv.sem, self.d + 4)
                nc.vector.tensor_scalar(cum[32:32 + HEADS, :], cum[0:HEADS, :], -1.0, None, ALU.mult).then_inc(dv.sem, 1)
                e.wait_ge(d_out.sem, self.stored)
                nc.vector.memset(QA[64:66, :, :], 1.0)
                nc.vector.memset(KA[64:66, :, :], 1.0).then_inc(dv.sem, 1)

            def pe(self, e):
                e.wait_ge(dv.sem, self.d - 5)
                u = unit_no(self.u)
                w = unit_view(u[0], KT)
                e.wait_ge(s_lo.sem, upto_unit(u, 1))
                for half in range(2):
                    mm3(ps[:, 4 + half, :], lambda a, k: w(a, k, 0, P),
                        lambda b, k: H[b][:, k, half * HALF:(half + 1) * HALF], KT, half == 0).then_inc(pe_a.sem, 1)

        class Attention(Stage):

            def __init__(self, hg):
                super().__init__()
                self.hg, self.conv_made = hg, dv.n - 6
                self.u = take_units(3)
                self.i = d_in.take(32)
                self.a, self.da = pe_a.take(16 + 32 + 4), dve_a.take(16 + 32 + 4)
                self.b, self.db = pe_b.take(32), dve_b.take(32)
                self.p, self.d, self.c = pe_s.take(32), dv.take(64), ac.take(32)
                if hg:
                    d_out.take(16)

            def sp(self, e):
                for k, o in enumerate((O_Q, O_K, O_V)):
                    load_unit(e, unit_no(self.u + k), w_cols(A["w_in"][0], 0, o + 256 * self.hg, KT, 256), (KT, 256))

            def act(self, e):
                split_hi(e, unit_no(self.u + 1))
                self.begin(e)
                hs = slice(4 * self.hg, 4 * self.hg + 4)
                e.dma_start(QA[64:65, :, :], cum[hs, :]).then_inc(d_in.sem, 16)
                e.dma_start(KA[65:66, :, :], cum[32 + hs.start:32 + hs.stop, :]).then_inc(d_in.sem, 16)
                for k in range(1, 3):
                    split_hi(e, unit_no(self.u + k + 1))
                for n in range(32):
                    kend = P * (n % 8 + 1)
                    e.wait_ge(dve_a.sem, self.da + 16 + n + 1)
                    if n >= 2:
                        e.wait_ge(pe_b.sem, self.b + n - 1)
                    nc.scalar.activation(PB[:, n % 2, 0:kend],
                                         ps[:, 2 * (n % 2):2 * (n % 2) + 2, :].rearrange("p b n -> p (b n)")[:, 0:kend],
                                         ACT.Exp, bias=mx[:, n:n + 1], accum_out=dn[:, n:n + 1]).then_inc(ac.sem, 1)
                if self.hg:
                    e.wait_ge(dve_a.sem, self.da + 52)
                    e.dma_start(scratch["y_keep"][2], Yc[:, :, :]).then_inc(d_out.sem, 16)

            def pool(self, e):
                for k in range(3):
                    split_lo(e, unit_no(self.u + k + 1))

            def dve(self, e):
                self.begin(e)
                for k, X in enumerate((QA, KA)):
                    for n in range(4):
                        j, half = n // 2, n % 2
                        sl = slice(half * HALF, (half + 1) * HALF)
                        e.wait_ge(pe_a.sem, self.a + 4 * k + n + 1)
                        for hh in range(2):
                            last = nc.vector.tensor_scalar(X[0:HD, 2 * j + hh, sl], ps[HD * hh:HD * hh + HD, n, :],
                                                           0.125 if k == 0 else 1.0, None, ALU.mult)
                        last.then_inc(dve_a.sem, 1)
                for t in range(8):
                    e.wait_ge(pe_a.sem, self.a + 8 + t + 1)
                    nc.vector.tensor_copy(VT[:, t, :], ps[:, t % 4, 0:256]).then_inc(dve_a.sem, 1)

                def top(n):
                    kend = P * (n % 8 + 1)
                    e.wait_ge(pe_a.sem, self.a + 16 + n + 1)
                    nc.vector.tensor_reduce(mx[:, n:n + 1],
                                            ps[:, 2 * (n % 2):2 * (n % 2) + 2, :].rearrange("p b n -> p (b n)")[:, 0:kend],
                                            AX, ALU.max, negate=True).then_inc(dve_a.sem, 1)
                top(0)
                top(1)
                for n in range(32):
                    h, i = n // 8, n % 8
                    kend = P * (i + 1)
                    e.wait_ge(pe_b.sem, self.b + n + 1)
                    if n >= 2:
                        e.wait_ge(pe_s.sem, self.p + n - 1)
                    nc.vector.tensor_copy(PT[:, n % 2, 0:kend], ps[:, 4:6, :].rearrange("p b n -> p (b n)")[:, 0:kend]
                                          ).then_inc(dve_b.sem, 1)
                    if n + 2 < 32:
                        top(n + 2)
                    e.wait_ge(ac.sem, self.c + n + 1)
                    nc.vector.reciprocal(rd[:, n:n + 1], dn[:, n:n + 1]).then_inc(dv.sem, 1)
                    e.wait_ge(dv.sem, self.d + 2 * n + 1)
                    e.wait_ge(pe_s.sem, self.p + n + 1)
                    nc.vector.tensor_scalar(OT[:, i, h * HD:(h + 1) * HD], ps[:, 6 + n % 2, 0:HD], rd[:, n:n + 1], None,
                                            ALU.mult).then_inc(dv.sem, 1)
                for n in range(4):
                    j, ig = n // 2, n % 2
                    e.wait_ge(pe_a.sem, self.a + 48 + n + 1)
                    nc.vector.tensor_copy(Yc[:, 2 * self.hg + j, ig * HALF:(ig + 1) * HALF], ps[:, n, :]
                                          ).then_inc(dve_a.sem, 1)

            def pe(self, e):
                if self.hg:
                    self.begin(e, stores=False)
                else:
                    e.wait_ge(dv.sem, self.conv_made)
                for k in range(2):
                    feature_tiles(e, unit_no(self.u + k), KT, H, 0,
                                  lambda n: [(dve_a, self.da + 4 * (k - 1) + n + 1)] if k else [], pe_a)
                u = unit_no(self.u + 2)
                w = unit_view(u[0], KT)
                e.wait_ge(s_lo.sem, upto_unit(u, 1))
                for t in range(8):
                    e.wait_ge(dve_a.sem, self.da + 4 + t + 1)
                    mm3(ps[:, t % 4, 0:256], lambda a, k: H[a][:, k, t * P:(t + 1) * P], lambda b, k: w(b, k, 0, 256), KT,
                        t == 0).then_inc(pe_a.sem, 1)
                e.wait_ge(dve_a.sem, self.da + 16)
                e.wait_ge(d_in.sem, self.i + 32)

                def logits(n):
                    h, i = n // 8, n % 8
                    kend = P * (i + 1)
                    if n >= 2:
                        e.wait_ge(ac.sem, self.c + n - 1)
                    for lo in range(0, kend, HALF):
                        w_ = min(HALF, kend - lo)
                        diag = lo + w_ == kend
                        last = nc.tensor.matmul(ps[:, 2 * (n % 2) + lo // HALF, 0:w_], QA[0:66, h, i * P:(i + 1) * P],
                                                KA[0:66, h, lo:lo + w_], start=True, stop=not diag)
                        if diag:
                            last = nc.tensor.matmul(ps[:, 2 * (n % 2) + lo // HALF, w_ - P:w_], ident, m_causal,
                                                    start=False, stop=True)
                    last.then_inc(pe_a.sem, 1)
                logits(0)
                logits(1)
                for n in range(32):
                    h, i = n // 8, n % 8
                    e.wait_ge(ac.sem, self.c + n + 1)
                    if n:
                        e.wait_ge(dve_b.sem, self.db + n)
                    for k in range(i + 1):
                        last = nc.tensor.transpose(ps[:, 4 + k // 4, (k % 4) * P:(k % 4 + 1) * P],
                                                   PB[:, n % 2, k * P:(k + 1) * P], ident)
                    last.then_inc(pe_b.sem, 1)
                    if n + 2 < 32:
                        logits(n + 2)
                    e.wait_ge(dve_b.sem, self.db + n + 1)
                    if n >= 2:
                        e.wait_ge(dv.sem, self.d + 2 * (n - 1))
                    for k in range(i + 1):
                        last = nc.tensor.matmul(ps[:, 6 + n % 2, 0:HD], PT[:, n % 2, k * P:(k + 1) * P],
                                                VT[:, k, h * HD:(h + 1) * HD], start=k == 0, stop=k == i)
                    last.then_inc(pe_s.sem, 1)
                e.wait_ge(dv.sem, self.d + 64)
                for n in range(4):
                    j, ig = n // 2, n % 2
                    for k in range(4):
                        last = nc.tensor.transpose(ps[:, n, k * P:(k + 1) * P], OT[:, 4 * ig + k, j * P:(j + 1) * P], ident)
                    last.then_inc(pe_a.sem, 1)

        class Rope(Stage):

            def __init__(self):
                super().__init__()
                self.i, self.d, self.c = d_in.take(16), dv.take(10), ac.take(4)

            def act(self, e):
                self.begin(e)
                nc.scalar.activation(mask_r[:, :], cst[:, 0:4 * P], ACT.Copy).then_inc(ac.sem, 1)
                e.dma_start(posi, A["positions_2"].partition_broadcast(P)).then_inc(d_in.sem, 16)
                e.wait_ge(dv.sem, self.d + 8)
                nc.scalar.activation(SINR[:, :], ang, ACT.Sin).then_inc(ac.sem, 1)
                nc.scalar.activation(ang2, ang, ACT.Abs).then_inc(ac.sem, 1)
                e.wait_ge(dv.sem, self.d + 9)
                nc.scalar.activation(COSR[:, :], ang2, ACT.Sin).then_inc(ac.sem, 1)

            def dve(self, e):
                self.begin(e)
                n = [0]

                def step(ins):
                    ins.then_inc(dv.sem, 1)
                    n[0] += 1
                    e.wait_ge(dv.sem, self.d + n[0])
                e.wait_ge(d_in.sem, self.i + 16)
                step(nc.vector.tensor_copy(ang, posi))
                step(nc.vector.tensor_scalar(ang, ang, c_freq, None, ALU.mult))
                step(nc.vector.tensor_scalar(ang2, ang, 1.0 / TWO_PI, None, ALU.mult))
                step(nc.vector.tensor_scalar(ang2, ang2, MAGIC, -MAGIC, ALU.add, ALU.add))
                for c in PI_PARTS[:-1]:
                    step(nc.vector.scalar_tensor_tensor(out=ang, in0=ang2, scalar=-c, in1=ang, op0=ALU.mult, op1=ALU.add))
                step(nc.vector.scalar_tensor_tensor(out=ang, in0=ang2, scalar=-PI_PARTS[-1], in1=ang, op0=ALU.mult,
                                                    op1=ALU.add))
                step(nc.vector.tensor_scalar(ang, ang, 3.1415925, -3.1415925, ALU.min, ALU.max))
                e.wait_ge(ac.sem, self.c + 3)
                step(nc.vector.tensor_scalar(ang2, ang2, -1.0, 1.5707963267948966, ALU.mult, ALU.add))
                step(nc.vector.tensor_scalar(SINR[:, :], SINR[:, :], c_rsgn, None, ALU.mult))

        class Dilated(Stage):

            def __init__(self, g, hg, norm=None):
                super().__init__()
                self.norm, self.stored = norm, d_out_pool.n
                self.g, self.hg, self.dil = g, hg, (1, 4, 8)[g]
                self.prev = [(b > 0, b % 2 == 1, False)[g] for b in range(8)]
                self.u = take_units(3)
                self.a, self.da = pe_a.take(16 + 8), dve_a.take(16 + 8)
                self.b, self.db = pe_b.take(8), dve_b.take(8)
                self.p, self.d, self.c = pe_s.take(8), dv.take(32 + 8), ac.take(8)
                d_out_pool.take(16 * 8)

            def sp(self, e):
                for k in range(3):
                    c = O2_QKV + 1536 * k + 512 * self.g + 256 * self.hg
                    load_unit(e, unit_no(self.u + k), w_cols(A["w_in_2"][0], 0, c, KT, 256), (KT, 256))

            def act(self, e):
                self.begin(e, stores=False)
                for k in range(3):
                    split_hi(e, unit_no(self.u + k + 1))
                for b in range(8):
                    lo = 0 if self.prev[b] else P
                    e.wait_ge(dve_a.sem, self.da + 16 + b + 1)
                    if b == 0 and self.stored:
                        e.wait_ge(d_out_pool.sem, self.stored)
                    if b >= 2:
                        e.wait_ge(pe_b.sem, self.b + b - 1)
                    for h in range(4):
                        last = nc.scalar.activation(
                            PB2[:, b % 2, h, lo:256],
                            ps[:, 2 * (b % 2) + h // 2, (h % 2) * 256 + lo:(h % 2 + 1) * 256],
                            ACT.Exp, bias=mx2[:, 4 * b + h:4 * b + h + 1], accum_out=OS[:, b, h, HD:HD + 1])
                    last.then_inc(ac.sem, 1)

            def pool(self, e):
                for k in range(3):
                    split_lo(e, unit_no(self.u + k + 1))
                dst = scratch["dil_keep"][self.g][:, 4 * self.hg:4 * self.hg + 4, :]
                for b in range(8):
                    e.wait_ge(dv.sem, self.d + 32 + b + 1)
                    s, st = ((b * P, 1), (b // 2 + 4 * P * (b % 2), 4), (b, 8))[self.g]
                    e.dma_start(dst[s:s + st * (P - 1) + 1:st], OS[:, b, :, :]).then_inc(d_out_pool.sem, 16)

            def dve(self, e):
                self.begin(e, stores=False)
                dil = self.dil
                for k, X in enumerate((Q2, K2)):
                    for n in range(4):
                        j, half = n // 2, n % 2
                        sl = slice(half * HALF, (half + 1) * HALF)
                        sc = 0.125 if k == 0 else 1.0
                        d = self.d + 4 * (4 * k + n)
                        e.wait_ge(pe_a.sem, self.a + 4 * k + n + 1)
                        nc.vector.stream_shuffle(rp[:, :], ps[:, n, :], list(range(8, 16)) + list(range(8)) + list(range(16, 32))
                                                 ).then_inc(dv.sem, 1)
                        nc.vector.scalar_tensor_tensor(out=rt[:, :], in0=ps[:, n, :], scalar=sc, in1=COSR[:, sl],
                                                       op0=ALU.mult, op1=ALU.mult).then_inc(dv.sem, 1)
                        e.wait_ge(dv.sem, d + 1)
                        nc.vector.scalar_tensor_tensor(out=rp[:, :], in0=rp[:, :], scalar=sc, in1=SINR[:, sl],
                                                       op0=ALU.mult, op1=ALU.mult).then_inc(dv.sem, 1)
                        e.wait_ge(dv.sem, d + 3)
                        for hh in range(2):
                            o = X[:, 2 * j + hh, :].rearrange("p (r l) -> p l r", r=dil)[:, half * HALF // dil:(half + 1) * HALF // dil, :]
                            pr = slice(HD * hh, HD * hh + HD)
                            last = nc.vector.tensor_tensor(o, rt[pr, :].rearrange("p (l r) -> p l r", r=dil),
                                                           rp[pr, :].rearrange("p (l r) -> p l r", r=dil), ALU.add)
                            if hh == 0:
                                last.then_inc(dv.sem, 1)
                        last.then_inc(dve_a.sem, 1)
                        e.wait_ge(dve_a.sem, self.da + 4 * k + n + 1)
                for t in range(8):
                    e.wait_ge(pe_a.sem, self.a + 8 + t + 1)
                    nc.vector.tensor_copy(V2[:, t, :], ps[:, t % 4, 0:256]).then_inc(dve_a.sem, 1)

                def top(b):
                    lo = 0 if self.prev[b] else P
                    e.wait_ge(pe_a.sem, self.a + 16 + b + 1)
                    nc.vector.tensor_reduce(
                        mx2[:, 4 * b:4 * b + 4],
                        ps[:, 2 * (b % 2):2 * (b % 2) + 2, :].rearrange("p b (h n) -> p (b h) n", h=2)[:, :, lo:256],
                        AX, ALU.max, negate=True).then_inc(dve_a.sem, 1)
                top(0)
                top(1)
                for b in range(8):
                    lo = 0 if self.prev[b] else 1
                    e.wait_ge(pe_b.sem, self.b + b + 1)
                    if b >= 2:
                        e.wait_ge(pe_s.sem, self.p + b - 1)
                    nc.vector.tensor_copy(
                        PT2[:, b % 2, :, lo:2, :],
                        ps[:, 4:6, :].rearrange("p b (h c n) -> p (b h) c n", h=2, c=2)[:, :, lo:2, :]).then_inc(dve_b.sem, 1)
                    if b + 2 < 8:
                        top(b + 2)
                    e.wait_ge(ac.sem, self.c + b + 1)
                    nc.vector.tensor_scalar(OS[:, b, :, HD + 1:HD + 2], mx2[:, 4 * b:4 * b + 4].unsqueeze(2), -1.0, None,
                                            ALU.mult)
                    e.wait_ge(pe_s.sem, self.p + b + 1)
                    nc.vector.tensor_copy(OS[:, b, :, 0:HD], ps[:, 6 + b % 2, 0:256].rearrange("p (h n) -> p h n", h=4)
                                          ).then_inc(dv.sem, 1)

            def pe(self, e):
                if self.norm is None:
                    self.begin(e, stores=False)
                else:
                    first_tiles(e, unit_no(self.u), H, lambda n: [], pe_a,
                                lambda k: [e.wait_ge(x.sem, n) for x, n in self.norm.ready(k)])
                for k in range(0 if self.norm is None else 1, 2):
                    feature_tiles(e, unit_no(self.u + k), KT, H, 0,
                                  lambda n: [(dve_a, self.da + 4 * (k - 1) + n + 1)] if k else [], pe_a)
                u = unit_no(self.u + 2)
                w = unit_view(u[0], KT)
                e.wait_ge(s_lo.sem, upto_unit(u, 1))

                def tokens(a, k, b):
                    x = H[a][:, k, :]
                    if self.g == 0:
                        return x[:, b * P:(b + 1) * P]
                    if self.g == 1:
                        s = b // 2 + 4 * P * (b % 2)
                        return x[:, s:s + 4 * (P - 1) + 1:4]
                    return x[:, b:b + 8 * (P - 1) + 1:8]
                for t in range(8):
                    e.wait_ge(dve_a.sem, self.da + 4 + t + 1)
                    mm3(ps[:, t % 4, 0:256], lambda a, k: tokens(a, k, t), lambda b, k: w(b, k, 0, 256), KT,
                        t == 0).then_inc(pe_a.sem, 1)
                e.wait_ge(dve_a.sem, self.da + 16)

                def logits(b):
                    if b >= 2:
                        e.wait_ge(ac.sem, self.c + b - 1)
                    for h in range(4):
                        lo = 0 if self.prev[b] else P
                        o = ps[:, 2 * (b % 2) + h // 2, (h % 2) * 256 + lo:(h % 2 + 1) * 256]
                        mask = even_r if self.g == 2 else band_r[:, lo:256]
                        nc.tensor.matmul(o, ident_r, mask, start=True, stop=False)
                        last = nc.tensor.matmul(o, Q2[:, h, b * P:(b + 1) * P], K2[:, h, b * P - (P - lo):(b + 1) * P],
                                                start=False, stop=True)
                    last.then_inc(pe_a.sem, 1)
                logits(0)
                logits(1)
                for b in range(8):
                    cs = (0, 1) if self.prev[b] else (1,)
                    e.wait_ge(ac.sem, self.c + b + 1)
                    if b:
                        e.wait_ge(dve_b.sem, self.db + b)
                    for h in range(4):
                        for c in cs:
                            o = (h % 2) * 256 + c * P
                            last = nc.tensor.transpose(ps[:, 4 + h // 2, o:o + P], PB2[:, b % 2, h, c * P:(c + 1) * P], ident)
                    last.then_inc(pe_b.sem, 1)
                    if b + 2 < 8:
                        logits(b + 2)
                    e.wait_ge(dve_b.sem, self.db + b + 1)
                    if b >= 2:
                        e.wait_ge(dv.sem, self.d + 32 + b - 1)
                    for h in range(4):
                        for c in cs:
                            last = nc.tensor.matmul(ps[:, 6 + b % 2, h * HD:(h + 1) * HD], PT2[:, b % 2, h, c, :],
                                                    V2[:, b - 1 + c, h * HD:(h + 1) * HD], start=c == cs[0], stop=c == 1)
                    last.then_inc(pe_s.sem, 1)

        class CombineAndGate(Stage):

            def __init__(self):
                super().__init__()
                self.u = take_units(4)
                order = (["mask"] + ["C0", "C1", "turned", "C2", "C3", "C4", "N0", "C5", "N1", "C6", "N2", "C7", "N3"])
                size = {"m": 1, "t": 1, "C": 15, "N": 12}
                self.at, n = {}, 0
                for x in order:
                    self.at[x] = n
                    n += size[x[0]]
                self.order, self.gate_at = order, n
                self.d = dv.take(n + 16)
                self.c = ac.take(12)
                self.i = (d_in.take(64), d_in2.take(64))
                self.tab = d_tab.take(16 * 11)
                self.a, self.b, self.s = pe_a.take(24), pe_b.take(8), pe_s.take(2 + 8)
                self.aa, self.da = act_a.take(24), dve_a.take(8)
                d_out.take(32)

            def sp(self, e):
                for k, o in enumerate((O2_V, O2_U)):
                    for j in range(2):
                        load_unit(e, unit_no(self.u + 2 * k + j), w_cols(A["w_in_2"][0], 0, o + 256 * j, KT, 256),
                                  (KT, 256))

            def act(self, e):
                self.begin(e)

                def load_tile(t):
                    e.dma_start(dl[:, t % 2], scratch["dil_keep"][:, t * P:(t + 1) * P, :, :].rearrange(
                        "g p h n -> p g h n")).then_inc((d_in, d_in2)[t % 2].sem, 16)
                load_tile(0)
                e.dma_start(wsp[:, :, :], A["w_spatial_2"][0].rearrange("g t s -> t g s")).then_inc(d_tab.sem, 16)
                e.dma_start(lng[:, :], A["sgu_ln_g_2"].partition_broadcast(P)).then_inc(d_tab.sem, 16)
                e.dma_start(lnb[:, :], A["sgu_ln_b_2"].partition_broadcast(P)).then_inc(d_tab.sem, 16)
                for g in range(8):
                    e.dma_start(bsp[64 * (g % 2):64 * (g % 2) + 64, g // 2, :],
                                A["b_spatial_2"][0, g:g + 1, :].partition_broadcast(64)).then_inc(d_tab.sem, 16)

                def weights(t):
                    e.wait_ge(dv.sem, self.d + self.at[f"C{t}"] + 5)
                    if t < 7:
                        load_tile(t + 1)
                    nc.scalar.activation(cw[:, 1, :], cw[:, 1, :], ACT.Exp).then_inc(ac.sem, 1)

                def v_tile(n):
                    j, t = n // 8, n % 8
                    e.wait_ge(pe_a.sem, self.a + n + 1)
                    nc.scalar.activation(gv[:, t, 256 * j:256 * j + 256], ps[:, t % 4, 0:256], ACT.Gelu
                                         ).then_inc(act_a.sem, 1)

                def u_tile(n):
                    j, r = n // 4, n % 4
                    e.wait_ge(pe_a.sem, self.a + 16 + n + 1)
                    nc.scalar.activation(gu[:, 2 * j + r // 2, (r % 2) * HALF:(r % 2 + 1) * HALF], ps[:, r, :],
                                         ACT.Gelu).then_inc(act_a.sem, 1)

                def roots(q):
                    e.wait_ge(dv.sem, self.d + self.at[f"N{q}"] + 5)
                    x = mv[:, 2 * q:2 * q + 2, 2:3]
                    nc.scalar.activation(x, x, ACT.Sqrt).then_inc(ac.sem, 1)
                for q in range(8):
                    if q % 2 == 0:
                        split_hi(e, unit_no(self.u + q // 2 + 1))
                    for n in range(4 * q, 4 * q + 4) if q < 4 else range(2 * q - 8, 2 * q - 6):
                        (v_tile if q < 4 else u_tile)(n)
                    if q > 4:
                        roots(q - 5)
                    weights(q)
                roots(3)
                e.wait_ge(dve_a.sem, self.da + 8)
                e.dma_start(scratch["y_keep"][0], Yd[:, :, :]).then_inc(d_out.sem, 16)
                e.wait_ge(dv.sem, self.d + self.gate_at + 16)
                e.dma_start(scratch["y_keep"][1], gu[:, :, :]).then_inc(d_out.sem, 16)

            def pool(self, e):
                for k in range(4):
                    split_lo(e, unit_no(self.u + k + 1))

            def dve(self, e):
                self.begin(e)
                n = [0]

                def step(ins):
                    ins.then_inc(dv.sem, 1)
                    n[0] += 1
                    e.wait_ge(dv.sem, self.d + n[0])

                def take_turned(t):
                    e.wait_ge(pe_b.sem, self.b + t + 1)
                    nc.vector.tensor_copy(Yd[:, :, t * P:(t + 1) * P],
                                          ps[:, 6 + t % 2, :].rearrange("p (j n) -> p j n", j=4)).then_inc(dve_a.sem, 1)

                def combine(t):
                    e.wait_ge((d_in, d_in2)[t % 2].sem, self.i[t % 2] + 16 * (t // 2 + 1))
                    x = dl[:, t % 2]
                    mg = lambda g: x[:, g, :, HD + 1]
                    by_g = lambda v: v.rearrange("p (g h) -> p g h", g=3)
                    M, W_, S_ = cw[:, 0, 0:8], cw[:, 1, :], cw[:, 2, :]
                    step(nc.vector.tensor_tensor(M, mg(0), mg(1), ALU.max))
                    step(nc.vector.tensor_tensor(M, M, mg(2), ALU.max))
                    for g in range(3):
                        step(nc.vector.tensor_tensor(cw[:, 1, 8 * g:8 * g + 8], mg(g), M, ALU.subtract))
                    if t:
                        take_turned(t - 1)
                    e.wait_ge(ac.sem, self.c + t + 1 + max(0, t - 5 + 1) * (t > 4))
                    step(nc.vector.tensor_tensor(by_g(S_), by_g(W_), x[:, :, :, HD], ALU.mult))
                    step(nc.vector.tensor_tensor(cw[:, 3, 0:8], cw[:, 2, 0:8], cw[:, 2, 8:16], ALU.add))
                    step(nc.vector.tensor_tensor(cw[:, 3, 0:8], cw[:, 3, 0:8], cw[:, 2, 16:24], ALU.add))
                    step(nc.vector.reciprocal(cw[:, 3, 0:8], cw[:, 3, 0:8]))
                    step(nc.vector.tensor_tensor(by_g(W_), by_g(W_), cw[:, 3, 0:8].unsqueeze(1).to_broadcast([P, 3, 8]),
                                                 ALU.mult))
                    o, s = [ct[:, j, :].rearrange("p (h n) -> p h n", h=8) for j in (t % 2, 2)]
                    wg = lambda g: cw[:, 1, 8 * g:8 * g + 8].unsqueeze(2).to_broadcast([P, 8, HD])
                    step(nc.vector.tensor_tensor(o, x[:, 0, :, 0:HD], wg(0), ALU.mult))
                    for g in (1, 2):
                        step(nc.vector.tensor_tensor(s, x[:, g, :, 0:HD], wg(g), ALU.mult))
                        step(nc.vector.tensor_tensor(o, o, s, ALU.add))

                def norm_two(q):
                    for t in (2 * q, 2 * q + 1):
                        e.wait_ge(act_a.sem, self.aa + 8 + t + 1)
                        step(nc.vector.bn_stats(st6[:, :], gv[:, t, :]))
                        step(nc.vector.bn_aggr(mv[:, t, 0:2], st6[:, :]))
                    two = slice(2 * q, 2 * q + 2)
                    step(nc.vector.tensor_scalar(mv[:, two, 2:3], mv[:, two, 1:2], EPS, None, ALU.add))
                    e.wait_ge(ac.sem, self.c + (12 if q == 3 else 2 * q + 6))
                    step(nc.vector.reciprocal(mv[:, two, 3:4], mv[:, two, 2:3]))
                    first = n[0]
                    for k, (t, op) in enumerate((t, op) for op in range(3) for t in (2 * q, 2 * q + 1)):
                        v = gv[:, t, :]
                        if k >= 2:
                            e.wait_ge(dv.sem, self.d + first + k - 1)
                        if op == 0:
                            ins = nc.vector.tensor_scalar(v, v, mv[:, t, 0:1], mv[:, t, 3:4], ALU.subtract, ALU.mult)
                        else:
                            ins = nc.vector.tensor_tensor(v, v, (lng, lnb)[op - 1][:, :], (ALU.mult, ALU.add)[op - 1])
                        ins.then_inc(dv.sem, 1)
                    n[0] += 6
                for x in self.order:
                    assert n[0] == self.at[x], (x, n[0])
                    if x == "mask":
                        e.wait_ge(d_tab.sem, self.tab + 16 * 11)
                        step(nc.vector.tensor_tensor(wsp[:, :, :], wsp[:, :, :], tril.unsqueeze(1).to_broadcast([P, 8, P]),
                                                     ALU.mult))
                    elif x == "turned":
                        e.wait_ge(pe_s.sem, self.s + 2)
                        step(nc.vector.tensor_copy(wspT[:, :, :], ps[:, 4:6, :].rearrange("p b (g n) -> p (b g) n", n=P)))
                    elif x[0] == "C":
                        combine(int(x[1]))
                    else:
                        norm_two(int(x[1]))
                take_turned(7)
                for c in range(8):
                    e.wait_ge(pe_s.sem, self.s + 2 + c + 1)
                    o = gu[:, :, c * P:(c + 1) * P]
                    v = ps[:, c % 4, :].rearrange("p (j n) -> p j n", j=4)
                    tmp = st_tmp[:, c % 2, :, :]
                    nc.vector.tensor_tensor(tmp, v, bsp[:, :, :], ALU.add).then_inc(dv.sem, 1)
                    e.wait_ge(dv.sem, self.d + self.gate_at + 2 * c + 1)
                    nc.vector.tensor_tensor(o, o, tmp, ALU.mult).then_inc(dv.sem, 1)

            def pe(self, e):
                self.begin(e, stores=False)

                def turn(t):
                    e.wait_ge(dv.sem, self.d + self.at[f"C{t}"] + 15)
                    if t >= 2:
                        e.wait_ge(dve_a.sem, self.da + t - 1)
                    for j in range(4):
                        last = nc.tensor.transpose(ps[:, 6 + t % 2, j * P:(j + 1) * P], ct[:, t % 2, j * P:(j + 1) * P],
                                                   ident)
                    last.then_inc(pe_b.sem, 1)
                for j in range(2):
                    u = unit_no(self.u + j)
                    w = unit_view(u[0], KT)
                    e.wait_ge(s_lo.sem, upto_unit(u, 1))
                    for t in range(8):
                        n = 8 * j + t
                        if n >= 4:
                            e.wait_ge(act_a.sem, self.aa + n - 3)
                        mm3(ps[:, t % 4, 0:256], lambda a, k: H[a][:, k, t * P:(t + 1) * P],
                            lambda b, k: w(b, k, 0, 256), KT, t == 0).then_inc(pe_a.sem, 1)
                        if n == 3:
                            e.wait_ge(dv.sem, self.d + self.at["mask"] + 1)
                            for g in range(8):
                                last = nc.tensor.transpose(ps[:, 4 + g // 4, (g % 4) * P:(g % 4 + 1) * P], wsp[:, g, :],
                                                           ident)
                                if g % 4 == 3:
                                    last.then_inc(pe_s.sem, 1)
                        if n % 4 == 3 and n > 3:
                            turn(n // 4 - 1)
                for j in range(2):
                    feature_tiles(e, unit_no(self.u + 2 + j), KT, H, 0,
                                  lambda n: [(act_a, self.aa + 16 + 4 * j + n - 3)], pe_a,
                                  after=lambda n: turn(3 + 2 * j + n // 2) if n % 2 else None)
                e.wait_ge(act_a.sem, self.aa + 24)
                for c in range(8):
                    e.wait_ge(dv.sem, self.d + self.at[f"N{c // 2}"] + 11 + c % 2)
                    if c >= 4:
                        e.wait_ge(dv.sem, self.d + self.gate_at + 2 * (c - 4) + 1)
                    for g in range(8):
                        last = nc.tensor.matmul(ps[64 * (g % 2):64 * (g % 2) + 64, c % 4, (g // 2) * P:(g // 2 + 1) * P],
                                                gv[:, c, g * 64:(g + 1) * 64], wspT[:, g, :], start=True, stop=True)
                    last.then_inc(pe_s.sem, 1)
                    if c == 1:
                        turn(7)

        w_branch = A["w_branch"][0]
        stages = []

        def add(stage, stores=True):
            if isinstance(stage, S5):
                stage.close()
            else:
                stage.close(stores)
            stages.append(stage)
            return stage

        add(LoadX())
        add(Vectors())
        add(Store0(), False)
        norm = add(Norm(V_NORM))
        add(S5(norm))
        add(Conv())
        add(Decay())
        for hg in range(2):
            add(Attention(hg))
        merge = add(Merge(A["w_in"][0], [O_G + D * b for b in range(3)],
                          [w_branch[512 * b:512 * b + 512] for b in range(3)], V_BG))
        mixed = add(Out(A["w_out"][0], merge, add_x=False))
        norm = add(Norm(V_NORM + 2 * KT, post=V_NORM + KT, x=xr, x_in=mixed.x_in, maker=mixed, keep=True), False)
        ff = add(FeedForward([A["w_ff1"][0]], A["w_ff2"][0], DFF, norm, onto_x=False, load_x=True))
        norm = add(Norm(V_NORM + 4 * KT, post=V_NORM + 3 * KT, x=xh, x_in=ff.x_in, maker=ff, bank=0, keep=True))
        add(Rope())
        for g in range(NDIL):
            for hg in range(2):
                add(Dilated(g, hg, norm if g + hg == 0 else None))
        add(CombineAndGate())
        merge = add(Merge(A["w_in_2"][0], [O2_GA, O2_GB], [A["w_proj_attn_2"][0], A["w_proj_sgu_2"][0]], None))
        mixed = add(Out(A["w_out_2"][0], merge, add_x=True))
        norm = add(Norm(V_NORM + 5 * KT, maker=mixed))
        ff = add(FeedForward([A["w_ffn_gate_2"][0], A["w_ffn_up_2"][0]], A["w_ffn_down_2"][0], DFF2, norm, onto_x=True))
        add(Final(ff))
        N_UNITS = units[0]

        block = ctx.enter_context(nc.Block())

        @block.sync
        def _(sp):
            sp.dma_start(cst[:, :], A["constants"]).then_inc(d_const.sem, 16)
            for n, name in enumerate(("g_pre_mix", "g_post_mix", "g_pre_mlp", "g_post_mlp", "norm1_g_2", "norm2_g_2",
                                      "final_g_2")):
                v = A[name].rearrange("(k p) -> k p", p=P) if len(A[name].shape) == 1 else A[name][0].rearrange("(k p) -> k p", p=P)
                sp.dma_start(ht[8 * n:8 * n + 8, 0, 0:P], v).then_inc(d_vec.sem, 16)
            sp.dma_start(ht[V_BG:V_BG + 24, 0, 0:P], A["b_gate"][0].rearrange("(k p) -> k p", p=P)).then_inc(d_vec.sem, 16)
            sp.dma_start(ht[V_CW:V_CW + 12, 0, 0:P], A["conv_w"][0].rearrange("t (k p) -> (t k) p", p=P)).then_inc(d_vec.sem, 16)
            sp.dma_start(bf[0:HEADS, :], A["fox_b_f"][0].rearrange("(h a) -> h a", a=1)).then_inc(d_vec.sem, 16)
            for s in stages:
                s.sp(sp)
            sp.wait_ge(d_out.sem, d_out.n)
            sp.wait_ge(d_out_pool.sem, d_out_pool.n)

        @block.scalar
        def _(act):
            split_hi(act, unit_no(0))
            for s in stages:
                s.act(act)

        @block.gpsimd
        def _(pool):
            split_lo(pool, unit_no(0))
            for s in stages:
                s.pool(pool)

        @block.vector
        def _(dve):
            for s in stages:
                s.dve(dve)

        @block.tensor
        def _(pe):
            for s in stages:
                s.pe(pe)


_INS = ["x", "g_pre_mix", "w_in", "b_gate", "s5_a_re", "s5_a_im", "s5_log_dt", "s5_b_re", "s5_b_im", "s5_c_re",
        "s5_c_im", "s5_d", "s5_w_glu", "conv_w", "fox_b_f", "w_branch", "w_out", "g_post_mix", "g_pre_mlp", "w_ff1",
        "w_ff2", "g_post_mlp", "positions_2", "norm1_g_2", "w_in_2", "sgu_ln_g_2", "sgu_ln_b_2", "w_spatial_2",
        "b_spatial_2", "w_proj_attn_2", "w_proj_sgu_2", "w_out_2", "norm2_g_2", "w_ffn_gate_2", "w_ffn_up_2",
        "w_ffn_down_2", "final_g_2"]


def constants():
    import numpy as np
    c = np.zeros((P, 6 * P + 8), np.float32)
    i, j = np.arange(P)[:, None], np.arange(P)[None, :]
    c[:, 0:P] = i == j
    c[:, P:2 * P] = np.where(j < i, -1e30, 0)
    c[:, 2 * P:3 * P] = np.where(j > i, -1e30, 0)
    c[:, 3 * P:4 * P] = np.where((j > i) | ((i - j) % 2 == 1), -1e30, 0)
    c[:, 4 * P:5 * P] = 1
    c[:, 5 * P:6 * P] = j <= i
    dim = np.arange(P) % HD
    inv = np.float32(500000.0) ** (-np.arange(0, 16, 2, dtype=np.float32) / np.float32(16))
    c[:, 6 * P] = np.where(dim < 16, inv[dim % 8], 0)
    c[:, 6 * P + 1] = np.where(dim < 8, -1, 1)
    c[:, 6 * P + 2] = np.where(np.arange(P) < 64, -1, 1)
    c[:, 6 * P + 3] = -c[:, 6 * P + 2]
    return c


def kernel(**inputs):
    import numpy as _np
    import concourse.bacc as _bacc
    from concourse import mybir as _mybir
    from concourse.bass_utils import run_bass_kernel_spmd as _run

    nc = _bacc.Bacc("TRN2", target_bir_lowering=False, num_devices=1)
    arrays, args = {}, {}
    for name in _INS + ["constants"]:
        a = constants() if name == "constants" else _np.ascontiguousarray(inputs[name])
        arrays[f"in_{name}_dram"] = a
        args[name] = nc.dram_tensor(f"in_{name}_dram", a.shape, _mybir.dt.from_np(a.dtype), kind="ExternalInput").ap()
    out = nc.dram_tensor("out_0_dram", (1, L, D), _mybir.dt.float32, kind="ExternalOutput").ap()
    hybrid_kernel(nc, args, out)
    r = _run(nc, [arrays], core_ids=[0])
    return r.results[0]["out_0_dram"]
```
